# Optimizing a Trainium2 kernel written in Bass

```python
import math
import jax, jax.numpy as jnp
from jax import lax
import numpy as np

D_MODEL = 1024
BATCH = 1
SEQ = 1024
DEPTH = 1
DEC_BATCH = 1
DEC_SEQ = 32
PAST_LEN = 1024

CHUNK = 64
SSM_WIDTH = D_MODEL // 2
SSM_GROUP_CH = 16
SSM_GROUPS = SSM_WIDTH // SSM_GROUP_CH
SSM_STATE = 64
POOL_WIDTH = D_MODEL // 2
POOL_WINDOWS = (2, 4, 8, 16)
POOL_GROUPS = len(POOL_WINDOWS)
POOL_GROUP_CH = POOL_WIDTH // POOL_GROUPS
POOL_OUT_CH = D_MODEL // POOL_GROUPS
POOL_HIST = max(POOL_WINDOWS) - 1
IN_WIDTH = SSM_WIDTH + POOL_WIDTH + 2 * D_MODEL
D_FF = -(-8 * D_MODEL // (3 * 256)) * 256
RMS_EPS = 1e-6
A_RE_MAX = -1e-4

kernel_name = "s5_pool_gated_hybrid_stream_step"

def rmsnorm(x, g):
    xf = x.astype(jnp.float32)
    y = xf * lax.rsqrt(jnp.mean(xf * xf, axis=-1, keepdims=True) + RMS_EPS) * g.astype(jnp.float32)
    return y.astype(x.dtype)

def ssm_branch(u, h0_re, h0_im, a_re, a_im, log_dt, b_re, b_im, c_re, c_im, d_skip, w_glu_a, w_glu_b):
    bsz, t_len, _ = u.shape
    f32 = jnp.float32
    uf = u.astype(f32).reshape(bsz, t_len, SSM_GROUPS, SSM_GROUP_CH)
    lam = lax.complex(jnp.minimum(a_re.astype(f32), A_RE_MAX), a_im.astype(f32))
    dt = jnp.exp(log_dt.astype(f32))[:, None]
    a_bar = jnp.exp(lam * dt)
    b_mat = lax.complex(b_re.astype(f32), b_im.astype(f32))
    b_bar = ((a_bar - 1.0) / lam)[..., None] * b_mat
    c_mat = lax.complex(c_re.astype(f32), c_im.astype(f32))
    bu = jnp.einsum('btgh,gph->btgp', uf, b_bar)
    h0 = lax.complex(h0_re.astype(f32), h0_im.astype(f32))
    bu = bu.at[:, 0].add(a_bar[None] * h0)
    a_seq = jnp.broadcast_to(a_bar, (1, t_len, SSM_GROUPS, SSM_STATE))

    def combine(left, right):
        a_l, b_l = left
        a_r, b_r = right
        return a_l * a_r, a_r * b_l + b_r

    _, hs = lax.associative_scan(combine, (a_seq, bu), axis=1)
    y = jnp.real(jnp.einsum('btgp,ghp->btgh', hs, c_mat)) + d_skip.astype(f32) * uf
    y = jax.nn.gelu(y).reshape(bsz, t_len, SSM_WIDTH).astype(u.dtype)
    out = (y @ w_glu_a) * jax.nn.sigmoid(y @ w_glu_b)
    h_last = hs[:, -1]
    return out, jnp.real(h_last), jnp.imag(h_last)

def pool_branch(u, hist, pos0, pool_w, pool_scale):
    bsz, t_len, _ = u.shape
    full = jnp.concatenate([hist.astype(u.dtype), u], axis=1)
    fullf = full.astype(jnp.float32)
    cs = jnp.concatenate([jnp.zeros((bsz, 1, POOL_WIDTH), jnp.float32),
                          jnp.cumsum(fullf, axis=1)], axis=1)
    uf = u.astype(jnp.float32)
    pos = pos0 + jnp.arange(t_len)
    groups = []
    for gi, w in enumerate(POOL_WINDOWS):
        lo, hi = gi * POOL_GROUP_CH, (gi + 1) * POOL_GROUP_CH
        end = cs[:, POOL_HIST + 1:POOL_HIST + 1 + t_len, lo:hi]
        start = cs[:, POOL_HIST + 1 - w:POOL_HIST + 1 - w + t_len, lo:hi]
        cnt = jnp.minimum(pos + 1, w).astype(jnp.float32)[None, :, None]
        groups.append((end - start) / cnt - uf[..., lo:hi])
    pooled = jnp.stack(groups, axis=2).astype(u.dtype)
    out = jnp.einsum('btgc,gcd->btgd', pooled, pool_w).reshape(bsz, t_len, D_MODEL) * pool_scale
    return out, full[:, -POOL_HIST:]

def trunk(x, h_re, h_im, pool_hist, pos0, g_mix, w_in, ssm_a_re, ssm_a_im, ssm_log_dt,
          ssm_b_re, ssm_b_im, ssm_c_re, ssm_c_im, ssm_d, w_glu_a, w_glu_b, pool_w, pool_scale,
          w_out, g_ffn, w_ffn_gate, w_ffn_up, w_ffn_down, g_final):
    new_re, new_im, new_pool = [], [], []
    h = x
    for l in range(DEPTH):
        n = rmsnorm(h, g_mix[l])
        z = n @ w_in[l]
        u_ssm = z[..., :SSM_WIDTH]
        u_pool = z[..., SSM_WIDTH:SSM_WIDTH + POOL_WIDTH]
        gate_ssm = z[..., SSM_WIDTH + POOL_WIDTH:SSM_WIDTH + POOL_WIDTH + D_MODEL]
        gate_pool = z[..., SSM_WIDTH + POOL_WIDTH + D_MODEL:]
        a_out, s_re, s_im = ssm_branch(u_ssm, h_re[l], h_im[l], ssm_a_re[l], ssm_a_im[l],
                                       ssm_log_dt[l], ssm_b_re[l], ssm_b_im[l], ssm_c_re[l],
                                       ssm_c_im[l], ssm_d[l], w_glu_a[l], w_glu_b[l])
        p_out, p_hist = pool_branch(u_pool, pool_hist[l], pos0, pool_w[l], pool_scale[l])
        merged = jax.nn.sigmoid(gate_ssm) * a_out + jax.nn.sigmoid(gate_pool) * p_out
        h = h + merged @ w_out[l]
        n2 = rmsnorm(h, g_ffn[l])
        h = h + (jax.nn.silu(n2 @ w_ffn_gate[l]) * (n2 @ w_ffn_up[l])) @ w_ffn_down[l]
        new_re.append(s_re.astype(h_re.dtype))
        new_im.append(s_im.astype(h_im.dtype))
        new_pool.append(p_hist.astype(pool_hist.dtype))
    y = rmsnorm(h, g_final)
    return y, jnp.stack(new_re), jnp.stack(new_im), jnp.stack(new_pool)

def setup_inputs(seed: int = 0) -> dict:
    key = jax.random.key(seed)
    ks = jax.random.split(key, 32)
    f32 = jnp.float32

    def nrm(k, shape, scale):
        return jax.random.normal(k, shape, f32) * scale

    n_idx = jnp.arange(SSM_STATE, dtype=f32)
    return {
        "x_prompt": nrm(ks[0], (BATCH, SEQ, D_MODEL), 1.0),
        "x_sample": nrm(ks[1], (DEC_BATCH, DEC_SEQ, D_MODEL), 1.0),
        "state_ssm_re": nrm(ks[2], (DEPTH, DEC_BATCH, SSM_GROUPS, SSM_STATE), 0.1),
        "state_ssm_im": nrm(ks[3], (DEPTH, DEC_BATCH, SSM_GROUPS, SSM_STATE), 0.1),
        "state_pool": nrm(ks[4], (DEPTH, DEC_BATCH, POOL_HIST, POOL_WIDTH), 1.0),
        "g_mix": 1.0 + nrm(ks[5], (DEPTH, D_MODEL), 0.02),
        "w_in": nrm(ks[6], (DEPTH, D_MODEL, IN_WIDTH), D_MODEL ** -0.5),
        "ssm_a_re": -0.5 + nrm(ks[7], (DEPTH, SSM_GROUPS, SSM_STATE), 0.01),
        "ssm_a_im": math.pi * n_idx + nrm(ks[8], (DEPTH, SSM_GROUPS, SSM_STATE), 0.01),
        "ssm_log_dt": jax.random.uniform(ks[9], (DEPTH, SSM_GROUPS), f32,
                                         math.log(1e-3), math.log(1e-1)),
        "ssm_b_re": nrm(ks[10], (DEPTH, SSM_GROUPS, SSM_STATE, SSM_GROUP_CH), (2 * SSM_GROUP_CH) ** -0.5),
        "ssm_b_im": nrm(ks[11], (DEPTH, SSM_GROUPS, SSM_STATE, SSM_GROUP_CH), (2 * SSM_GROUP_CH) ** -0.5),
        "ssm_c_re": nrm(ks[12], (DEPTH, SSM_GROUPS, SSM_GROUP_CH, SSM_STATE), (2 * SSM_STATE) ** -0.5),
        "ssm_c_im": nrm(ks[13], (DEPTH, SSM_GROUPS, SSM_GROUP_CH, SSM_STATE), (2 * SSM_STATE) ** -0.5),
        "ssm_d": nrm(ks[14], (DEPTH, SSM_GROUPS, SSM_GROUP_CH), 1.0),
        "w_glu_a": nrm(ks[15], (DEPTH, SSM_WIDTH, D_MODEL), SSM_WIDTH ** -0.5),
        "w_glu_b": nrm(ks[16], (DEPTH, SSM_WIDTH, D_MODEL), SSM_WIDTH ** -0.5),
        "pool_w": nrm(ks[17], (DEPTH, POOL_GROUPS, POOL_GROUP_CH, POOL_OUT_CH), POOL_GROUP_CH ** -0.5),
        "pool_scale": 1.0 + nrm(ks[18], (DEPTH, D_MODEL), 0.02),
        "w_out": nrm(ks[19], (DEPTH, D_MODEL, D_MODEL), D_MODEL ** -0.5),
        "g_ffn": 1.0 + nrm(ks[20], (DEPTH, D_MODEL), 0.02),
        "w_ffn_gate": nrm(ks[21], (DEPTH, D_MODEL, D_FF), D_MODEL ** -0.5),
        "w_ffn_up": nrm(ks[22], (DEPTH, D_MODEL, D_FF), D_MODEL ** -0.5),
        "w_ffn_down": nrm(ks[23], (DEPTH, D_FF, D_MODEL), D_FF ** -0.5),
        "g_final": 1.0 + nrm(ks[24], (D_MODEL,), 0.02),
    }

def reference(x_prompt, x_sample, state_ssm_re, state_ssm_im, state_pool, g_mix, w_in,
              ssm_a_re, ssm_a_im, ssm_log_dt, ssm_b_re, ssm_b_im, ssm_c_re, ssm_c_im, ssm_d,
              w_glu_a, w_glu_b, pool_w, pool_scale, w_out, g_ffn, w_ffn_gate, w_ffn_up,
              w_ffn_down, g_final):
    weights = (g_mix, w_in, ssm_a_re, ssm_a_im, ssm_log_dt, ssm_b_re, ssm_b_im, ssm_c_re,
               ssm_c_im, ssm_d, w_glu_a, w_glu_b, pool_w, pool_scale, w_out, g_ffn,
               w_ffn_gate, w_ffn_up, w_ffn_down, g_final)
    bp = x_prompt.shape[0]
    zero_ssm = jnp.zeros((DEPTH, bp, SSM_GROUPS, SSM_STATE), state_ssm_re.dtype)
    zero_pool = jnp.zeros((DEPTH, bp, POOL_HIST, POOL_WIDTH), state_pool.dtype)
    y_prompt, p_re, p_im, p_pool = trunk(x_prompt, zero_ssm, zero_ssm, zero_pool, 0, *weights)
    y_sample, s_re, s_im, s_pool = trunk(x_sample, state_ssm_re, state_ssm_im, state_pool,
                                         PAST_LEN, *weights)
    return (y_prompt, y_sample, p_re, p_im, p_pool, s_re, s_im, s_pool)


_drawn_inputs = setup_inputs


def setup_inputs(seed=0):
    import zlib

    import numpy as np

    out = dict(_drawn_inputs(seed))
    spreads = {}
    factors = {'ssm_a_re': 66.538,
     'ssm_c_re': 12.966,
     'ssm_c_im': 12.949,
     'pool_scale': 6.251,
     'g_ffn': 4.315,
     'g_final': 23.168}
    for name, (base, spread) in spreads.items():
        noise = np.random.default_rng([zlib.crc32(name.encode()), seed]).standard_normal(out[name].shape)
        drawn = base * np.exp(spread * noise) if base else spread * noise
        out[name] = __import__('jax').numpy.asarray(drawn.astype(out[name].dtype))
    for name, factor in factors.items():
        out[name] = (out[name] * factor).astype(out[name].dtype)
    return out
```

```python
from contextlib import ExitStack

import numpy as np

import concourse.bass as bass
from concourse import mybir
from concourse.alu_op_type import AluOpType as ALU

F32 = mybir.dt.float32
F32R = mybir.dt.float32r
I32 = mybir.dt.int32
ACT = mybir.ActivationFunctionType
ds = bass.ds

P = 128
D = 1024
SEQ, DEC = 1024, 32
T = SEQ + DEC
KD = D // P
BLK = T // 3
TT = -(-T // P)
W_SSM = W_POOL = D // 2
KS = W_SSM // P
G, H, NS = 32, 16, 64
PAIRS = G // 2
L = 8
NC = T // L
NCP = SEQ // L
NCG = NC + 1
SLOTS = NCG + 1
SEG, STEPS = 8, NCP // 8
WINDOWS = (2, 4, 8, 16)
HIST = 15
FF = 2816
FCH = FF // P // 2
EPS = 1e-6
PRM_LOADS = 15
SLAB = 8 * P
GELU_C = 2.0 * 0.7978845608028654
TWO_PI = (6.28125, 0.0019350051879882812, 3.019916050561733e-07)
LN2 = (0.693359375, -2.12194440e-4)
EXP_POLY = [1.0 / 5040, 1.0 / 720, 1.0 / 120, 1.0 / 24, 1.0 / 6, 0.5, 1.0]
MAGIC = 12582912.0

S_POOL, T_POOL = 4, 4
S_GLU, T_GLU = 20, 24
S_OUT, T_OUT = 36, 48
S_FFN, T_FFN = 44, 56
S_LOOP, T_LOOP = 48, 60
S_LAST, T_LAST = 108, 180


def hybrid_layer(nc, t_in, t_out):
    ctx = ExitStack()
    with ctx:
        def sb(name, shape, dt=F32, stack=ctx):
            return stack.enter_context(nc.sbuf_tensor(name, shape, dt))

        def overlay(*tensors):
            with ExitStack() as stack:
                return [sb(n, s, d, stack) for n, s, d in tensors]

        def sem(name):
            return ctx.enter_context(nc.semaphore(name))

        ident = sb("ident", [P, P])
        ones = sb("ones", [P, P])
        inv_count = sb("inv_count", [P, 4, 16])
        gains = sb("gains", [P, 4, KD])
        stage = sb("stage", [P, 2, SLAB])
        w_hi = sb("w_hi", [P, 2, SLAB], F32R)
        w_lo = sb("w_lo", [P, 2, SLAB], F32R)
        rstd_row = sb("rstd_row", [P, T])
        ss = sb("ss", [P, 4, TT])
        a8pow = sb("a8pow", [P, 2, STEPS, PAIRS])
        neg_a = sb("neg_a", [P, 2, PAIRS])
        pool_hist = sb("pool_hist", [P, 4, HIST])
        new_pool = sb("new_pool", [HIST, 2, W_POOL])
        d_skip = sb("d_skip", [H, G])
        out_state = sb("out_state", [PAIRS, 4, P])
        log_dt = sb("log_dt", [PAIRS, 2])
        zeros = sb("zeros", [P, 16])
        state0 = sb("state0", [P, 2, PAIRS])
        head = sb("head", [P, 16])
        base = ExitStack()
        x_hi = sb("x_hi", [P, KD, T], F32R, base)
        x_lo = sb("x_lo", [P, KD, T], F32R, base)
        U, S, TO, CA, W, UT, pl_hi, pl_lo, gate_t = overlay(
            ("U", [P, G, NCG], F32),
            ("S", [P, 2, PAIRS, SLOTS], F32),
            ("TO", [P, G, P], F32),
            ("CA", [P, 2, PAIRS, (L + 1) * H], F32),
            ("W", [P, 2, PAIRS, P], F32),
            ("UT", [P, KS, L, NCG], F32),
            ("pl_hi", [P, T], F32R), ("pl_lo", [P, T], F32R),
            ("gate_t", [P, 2, T], F32))
        x_t, xg = overlay(("x_t", [P, 2, D], F32), ("xg", [P, 2, D], F32))
        (K_sb,) = overlay(("K_sb", [H, G, P], F32))
        _, x_raw = overlay(("pad0", [P, G * NCG], F32), ("x_raw", [P, 2, D], F32))
        _, WT = overlay(("pad1", [P, G * NCG], F32), ("WT", [P, 2, PAIRS, P], F32))
        q_space = G * NCG + 2 * PAIRS * SLOTS
        _, tmp_a, _, tmp_b = overlay(("pad2", [P, q_space], F32), ("tmp_a", [P, PAIRS * 9 * H], F32),
                                     ("pad3", [P, G * P - PAIRS * 9 * H + 2 * PAIRS * 9 * H], F32),
                                     ("tmp_b", [P, PAIRS * 9 * H], F32))
        ut_at = q_space + G * P + 2 * PAIRS * 9 * H + 2 * PAIRS * P
        _, diag = overlay(("pad4", [P, ut_at], F32), ("diag", [P, TT, P], F32))
        _, UP, sum_a, sum_b = overlay(("pad5", [P, ut_at], F32), ("UP", [P, T + 2 * HIST], F32),
                                      ("sum_a", [P, T + 2 * HIST], F32), ("sum_b", [P, T + 2 * HIST], F32))
        pl_at = ut_at + KS * L * NCG
        _, rows, c_raw, b_raw, prm, pt, BB, CT, PW = overlay(
            ("pad6", [P, pl_at], F32),
            ("rows", [32, 10, P], F32), ("c_raw", [P, 2, 4, 2, NS], F32), ("b_raw", [P, 2, PAIRS, H], F32),
            ("prm", [P, 5, PAIRS], F32), ("pt", [P, 30, PAIRS], F32), ("BB", [P, 2, PAIRS, H], F32),
            ("CT", [P, 2, PAIRS, H], F32), ("PW", [P, 2, L + 1, PAIRS], F32))
        _, skip_k = overlay(("pad16", [P, pl_at], F32), ("skip_k", [H, G * H], F32))
        w_at = q_space + G * P + 2 * PAIRS * 9 * H
        _, sc_a, sc_b = overlay(("pad7", [P, w_at], F32), ("sc_a", [P, PAIRS * 7 * 15], F32),
                                ("sc_b", [P, PAIRS * 7 * 15], F32))
        _, x_sq = overlay(("pad8", [P, ut_at + TT * P], F32), ("x_sq", [P, D], F32))
        y_hi, y_lo = overlay(("y_hi", [P, KS, T], F32R), ("y_lo", [P, KS, T], F32R))
        _, YT = overlay(("pad9", [P, q_space], F32), ("YT", [P, KS, L, NCG], F32))
        _, ge_a, ge_b, ge_c = overlay(("pad10", [P, w_at], F32), ("ge_a", [P, L * NCG], F32),
                                      ("ge_b", [P, L * NCG], F32), ("ge_c", [P, T], F32))
        _, merged = overlay(("pad11", [P, q_space], F32), ("merged", [P, KD, T], F32))
        _, glu_a, glu_b = overlay(("pad12", [P, w_at], F32), ("glu_a", [P, T], F32), ("glu_b", [P, T], F32))
        _, pool_t, sig_s = overlay(("pad13", [P, ut_at], F32), ("pool_t", [P, 2, T], F32),
                                   ("sig_s", [P, 2, T], F32))
        hT, _, hg_hi, hg_lo, sq = overlay(
            ("hT", [P, KD, T], F32), ("pad14", [P, q_space - KD * T], F32),
            ("hg_hi", [P, KD, T], F32R), ("hg_lo", [P, KD, T], F32R), ("sq", [P, 2, T], F32))
        base.close()
        f_hi, f_lo, f_g, f_s, f_u, f_h = overlay(
            ("f_hi", [P, 2, T], F32R), ("f_lo", [P, 2, T], F32R), ("f_g", [P, T], F32), ("f_s", [P, T], F32),
            ("f_u", [P, T], F32), ("f_h", [P, T], F32))
        _, hf = overlay(("pad15", [P, 8 * T], F32), ("hf", [P, KD, T], F32))
        y_out, diag2 = overlay(("y_out", [P, 4, D], F32), ("diag2", [P, TT, P], F32))

        bank_a = ctx.enter_context(nc.psum_tensor("bank_a", [P, 3, 512], F32))
        bank_b = ctx.enter_context(nc.psum_tensor("bank_b", [P, 3, 512], F32))
        aux = ctx.enter_context(nc.psum_tensor("aux", [P, 2, 512], F32))
        A3, B3 = bank_a[:, :, 0:BLK], bank_b[:, :, 0:BLK]

        def b3(ap):
            return ap.rearrange("p (b t) -> p b t", b=3)

        consts_in, prm_in, gains_in = sem("consts_in"), sem("prm_in"), sem("gains_in")
        x_in = [sem("x_in0"), sem("x_in1")]
        stage_in = [sem("stage_in0"), sem("stage_in1")]
        hi_ready, lo_ready = sem("hi_ready"), sem("lo_ready")
        tile_done, evac_done = sem("tile_done"), sem("evac_done")
        ones_ready, act_step, dve_step, pool_step = sem("ones_ready"), sem("act_step"), sem("dve_step"), sem("pool_step")
        x_turned, x_squared, xg_ready, xraw_ready = sem("x_turned"), sem("x_squared"), sem("xg_ready"), sem("xraw_ready")
        x_hi_ready, x_lo_ready, xraw_out = sem("x_hi_ready"), sem("x_lo_ready"), [sem("xraw_out0"), sem("xraw_out1")]
        ms_ready, root_ready, diag_ready, row_ready, row_used = (
            sem("ms_ready"), sem("root_ready"), sem("diag_ready"), sem("row_ready"), sem("row_used"))
        rows_ready, prm_turned, prm_used = sem("rows_ready"), sem("prm_turned"), sem("prm_used")
        angle_ready, sine_ready = sem("angle_ready"), sem("sine_ready")
        ca_ready, wt_ready, k_turn, k_evac, w_turn, w_evac = (
            sem("ca_ready"), sem("wt_ready"), sem("k_turn"), sem("k_evac"), sem("w_turn"), sem("w_evac"))
        to_zero, k_ready, to_in = sem("to_zero"), sem("k_ready"), sem("to_in")
        ut_ready, ut_out, u_in = sem("ut_ready"), sem("ut_out"), sem("u_in")
        pooled_ready, pooled_hi, pooled_lo, np_turned, np_evac = (
            sem("pooled_ready"), sem("pooled_hi"), sem("pooled_lo"), sem("np_turned"), sem("np_evac"))
        gp_ready, gp_sig, mp_ready, mp_out = sem("gp_ready"), sem("gp_sig"), sem("mp_ready"), [sem("mp_out0"), sem("mp_out1")]
        v_turn, v_evac, s_ready, y_turn, y_evac, st_turn, st_evac = (
            sem("v_turn"), sem("v_evac"), sem("s_ready"), sem("y_turn"), sem("y_evac"), sem("st_turn"), sem("st_evac"))
        y_out_dram, yt_in = sem("y_out_dram"), sem("yt_in")
        y_sq, y_arg, y_sig, y_val, y_hi_ready, y_lo_ready = (
            sem("y_sq"), sem("y_arg"), sem("y_sig"), sem("y_val"), sem("y_hi_ready"), sem("y_lo_ready"))
        gs_ready, gs_sig, b_sig, mp_in, merged_ready, m_hi_ready, m_lo_ready = (
            sem("gs_ready"), sem("gs_sig"), sem("b_sig"), [sem("mp_in0"), sem("mp_in1")], sem("merged_ready"),
            sem("m_hi_ready"), sem("m_lo_ready"))
        h_unused, hg_hi_ready, hg_lo_ready, sq_ready, sq_used = (
            sem("h_unused"), sem("hg_hi_ready"), sem("hg_lo_ready"), sem("sq_ready"), sem("sq_used"))
        fg_ready, fs_ready, fh_ready, f_hi_ready, f_lo_ready = (
            sem("fg_ready"), sem("fs_ready"), sem("fh_ready"), sem("f_hi_ready"), sem("f_lo_ready"))
        hf_ready, tok_turned, tok_used, y_stored = (sem("hf_ready"), sem("tok_turned"), [sem("tok_used0"), sem("tok_used1")],
                                                    [sem(f"y_stored{i}") for i in range(4)])
        small_out = sem("small_out")
        xt_in = [sem(f"xt_in{k}") for k in range(KD)]

        w_in = t_in["w_in"][0].rearrange("(k p) n -> p k n", p=P)
        w_a = t_in["w_glu_a"][0].rearrange("(k p) n -> p k n", p=P)
        w_b = t_in["w_glu_b"][0].rearrange("(k p) n -> p k n", p=P)
        w_o = t_in["w_out"][0].rearrange("(k p) n -> p k n", p=P)
        w_g = t_in["w_ffn_gate"][0].rearrange("(k p) n -> p k n", p=P)
        w_u = t_in["w_ffn_up"][0].rearrange("(k p) n -> p k n", p=P)
        w_d = t_in["w_ffn_down"][0].rearrange("(k p) n -> p k n", p=P)
        pool_w = t_in["pool_w"][0]
        xt_dram = nc.dram_tensor("xt_scratch", [D, T], F32).ap()
        u_dram = nc.dram_tensor("u_scratch", [W_SSM, L, NCG], F32).ap()
        y_dram = nc.dram_tensor("y_scratch", [W_SSM, L, NCG], F32).ap()
        mp_dram = nc.dram_tensor("mp_scratch", [D, T], F32).ap()
        x_p, x_s = t_in["x_prompt"][0], t_in["x_sample"][0]

        def tok(tt):
            return min(P, T - tt * P)

        def slab3(slot):
            return stage[:, slot, :].rearrange("p (k n) -> p k n", n=P)

        def spill_x(sp, tt):
            sp.wait_ge(xraw_ready, tt + 1)
            sp.dma_start(xt_dram[:, tt * P:tt * P + tok(tt)].rearrange("(k p) t -> p k t", p=P),
                         x_raw[:, tt % 2, :].rearrange("p (k t) -> p k t", k=KD)[:, :, 0:tok(tt)]).then_inc(xraw_out[tt % 2], 16)

        def spill_mp(sp, g):
            for r in range(2):
                n = 2 * g + r
                sp.wait_ge(evac_done, T_POOL + 5 * g + 4 + r)
                sp.dma_start(mp_dram[n * P:(n + 1) * P, :], gate_t[:, r, :]).then_inc(mp_out[r], 16)

        block = ctx.enter_context(nc.Block())

        @block.sync
        def _(sp):
            def slab(s, slot, pieces):
                if not (isinstance(s, int) and s < 2):
                    sp.wait_ge(lo_ready, s - 1)
                for i, (dst, src) in enumerate(pieces):
                    sp.dma_start(dst, src).then_inc(stage_in[slot], 16)

            sp.dma_start(ident[:], t_in["c_ident"]).then_inc(consts_in, 16)
            sp.dma_start(inv_count[:], t_in["c_inv_count"]).then_inc(consts_in, 16)
            for tt in range(TT):
                if tt >= 2:
                    sp.wait_ge(x_turned, tt - 1)
                    sp.wait_ge(x_squared, tt - 1)
                src = x_p[tt * P:(tt + 1) * P, :] if tt < SEQ // P else x_s
                sp.dma_start(x_t[0:tok(tt), tt % 2, :], src).then_inc(x_in[tt % 2], 16)
                if tt in (1, 2):
                    slab(tt - 1, tt - 1, [(slab3(tt - 1), w_in[:, :, (tt - 1) * P:tt * P])])
                if tt >= 1:
                    spill_x(sp, tt - 1)
            spill_x(sp, TT - 1)
            for s in (2, 3):
                slab(s, s % 2, [(slab3(s % 2), w_in[:, :, s * P:(s + 1) * P])])
            slab(4, 0, [(slab3(0), w_in[:, :, W_SSM:W_SSM + P])])
            sp.wait_ge(evac_done, KS)
            sp.dma_start(u_dram.rearrange("(n p) j c -> p n j c", p=P), UT[:, :, :, :]).then_inc(ut_out, 16)
            slab(5, 1, [(slab3(1), w_in[:, :, 2 * W_SSM + D:2 * W_SSM + D + P])])
            sp.wait_ge(k_ready, 1)
            sp.wait_ge(to_zero, 1)
            for i in range(L):
                j = L - 1 - i
                sp.dma_start(TO[16 * i:16 * i + 16, :, 16 * j:P], K_sb[:, :, 0:P - 16 * j]).then_inc(to_in, 16)
            sp.wait_ge(ut_out, 16)
            sp.wait_ge(to_in, 16 * L)
            for i in range(L):
                sp.dma_start(U[16 * i:16 * i + 16, :, :],
                             u_dram[:, L - 1 - i, :].rearrange("(g h) c -> h g c", h=H)).then_inc(u_in, 16)
            for g in range(4):
                s0 = S_POOL + 4 * g
                if g > 0:
                    slab(s0, 0, [(slab3(0), w_in[:, :, W_SSM + g * P:W_SSM + (g + 1) * P])])
                    c0 = 2 * W_SSM + D + 2 * g * P
                    slab(s0 + 1, 1, [(slab3(1), w_in[:, :, c0:c0 + P])])
                c1 = 2 * W_SSM + D + (2 * g + 1) * P
                slab(s0 + 2, 0, [(slab3(0), w_in[:, :, c1:c1 + P])])
                slab(s0 + 3, 1, [(stage[:, 1, 0:2 * P], pool_w[g])])
                if g > 0:
                    spill_mp(sp, g - 1)
            gs0 = 2 * W_SSM
            for m in range(4):
                s0 = S_GLU + 4 * m
                for r in range(2):
                    n = 2 * m + r
                    slab(s0 + r, r, [(slab3(r), w_in[:, :, gs0 + n * P:gs0 + (n + 1) * P])])
                if m == 0:
                    spill_mp(sp, 3)
                    sp.wait_ge(np_evac, 4)
                    sp.dma_start(t_out["pool_p"][0, 0], new_pool[:, 0, :]).then_inc(small_out, 16)
                    sp.dma_start(t_out["pool_s"][0, 0], new_pool[:, 1, :]).then_inc(small_out, 16)
                    sp.wait_ge(st_evac, 1)
                    for i, name in enumerate(("re_p", "im_p", "re_s", "im_s")):
                        sp.dma_start(t_out[name][0, 0].rearrange("(pr g) p -> pr (g p)", g=2),
                                     out_state[:, i, :]).then_inc(small_out, 16)
                    sp.wait_ge(y_evac, 12)
                    for j in range(L):
                        sp.dma_start(y_dram[:, j, :].rearrange("(g h) c -> h g c", h=H),
                                     U[16 * j:16 * j + 16, :, :]).then_inc(y_out_dram, 16)
                    sp.wait_ge(y_out_dram, 16 * L)
                    for n in range(KS):
                        sp.dma_start(YT[:, n], y_dram[n * P:(n + 1) * P]).then_inc(yt_in, 16)
                    sp.wait_ge(small_out, 16 * 6)
                    for q in mp_out:
                        sp.wait_ge(q, 16 * 4)
                for r in range(2):
                    n = 2 * m + r
                    if n >= 2:
                        sp.wait_ge(merged_ready, n - 1)
                    sp.dma_start(pool_t[:, r, :], mp_dram[n * P:(n + 1) * P, :]).then_inc(mp_in[r], 16)
                    half = slab3(r)
                    slab(s0 + 2 + r, r, [(half[:, 0:4], w_a[:, :, n * P:(n + 1) * P]),
                                         (half[:, 4:8], w_b[:, :, n * P:(n + 1) * P])])
            for n in range(KD):
                slab(S_OUT + n, n % 2, [(slab3(n % 2), w_o[:, :, n * P:(n + 1) * P])])
                if n == 1:
                    sp.wait_ge(tile_done, T_OUT)
                    for q, n_out in zip(xraw_out, (5, 4)):
                        sp.wait_ge(q, 16 * n_out)
                    for k in range(KD):
                        sp.dma_start(hT[:, k, :], xt_dram[k * P:(k + 1) * P, :]).then_inc(xt_in[k], 16)
            for f in range(2):
                slab(S_FFN + 2 * f, 0, [(slab3(0), w_g[:, :, f * P:(f + 1) * P])])
                slab(S_FFN + 2 * f + 1, 1, [(slab3(1), w_u[:, :, f * P:(f + 1) * P])])
            down = [stage[:, r, :].rearrange("p (k n) -> p k n", n=4 * P) for r in range(2)]
            with sp.Fori(1, FCH) as c:
                s0 = 6 * c + (S_LOOP - 6)
                slab(s0, 0, [(slab3(0), w_g[:, :, ds(c * (2 * P), P)])])
                slab(s0 + 1, 1, [(slab3(1), w_u[:, :, ds(c * (2 * P), P)])])
                for r in range(2):
                    slab(s0 + 2 + r, r, [(down[r], w_d[:, ds(c * 2 - 2, 2), r * 4 * P:(r + 1) * 4 * P])])
                slab(s0 + 4, 0, [(slab3(0), w_g[:, :, ds(c * (2 * P) + P, P)])])
                slab(s0 + 5, 1, [(slab3(1), w_u[:, :, ds(c * (2 * P) + P, P)])])
            for r in range(2):
                slab(S_LAST + r, r, [(down[r], w_d[:, 2 * FCH - 2:2 * FCH, r * 4 * P:(r + 1) * 4 * P])])
            for tt in range(TT):
                sp.wait_ge(tok_used[tt % 2], tt // 2 + 1)
                dst = t_out["y_p"][0, tt * P:(tt + 1) * P, :] if tt < SEQ // P else t_out["y_s"][0]
                sp.dma_start(dst, y_out[0:tok(tt), tt % 4, :]).then_inc(y_stored[tt % 4], 16)
            for i in range(4):
                sp.wait_ge(y_stored[i], 16 * len(range(i, TT, 4)))
            sp.wait_ge(small_out, 16 * 6)


        @block.tensor
        def _(pe):
            def tile(t, banks, slot, terms, hi, lo, ready=None):
                if not (isinstance(t, int) and t < 2):
                    pe.wait_ge(evac_done, t - 1)
                for i, (col, k) in enumerate(terms):
                    if ready is not None:
                        pe.wait_ge(ready, k + 1)
                    for step, (w, x) in enumerate(((w_hi, hi), (w_hi, lo), (w_lo, hi))):
                        for b in range(3):
                            mm = pe.matmul(banks[:, b, 0:BLK], w[:, slot, col:col + P],
                                           x[:, k, b * BLK:(b + 1) * BLK],
                                           start=(i == 0 and step == 0), stop=(i == len(terms) - 1 and step == 2))
                mm.then_inc(tile_done, 1)

            ALL = [(k * P, k) for k in range(KD)]

            def rstd_rows(n, scaled):
                pe.wait_ge(diag_ready, n)
                for tt in range(TT):
                    out = aux[:, tt // 4, (tt % 4) * P:(tt % 4 + 1) * P] if tt < 8 else bank_a[:, 2, 384:384 + DEC]
                    mm = pe.matmul(out, ones[0:tok(tt), :], scaled[0:tok(tt), tt, 0:tok(tt)], start=True, stop=True)
                mm.then_inc(row_ready, 1)

            pe.wait_ge(consts_in, 32)
            pe.wait_ge(gains_in, 64)
            pe.transpose(aux[:, 0, 0:32], rows[0:32, 5, :], ident[0:32, 0:32]).then_inc(prm_turned, 1)
            for tt in range(TT):
                pe.wait_ge(x_in[tt % 2], 16 * (tt // 2 + 1))
                if tt >= 2:
                    pe.wait_ge(xraw_ready, tt - 1)
                banks = bank_b if tt % 2 else bank_a
                for k in range(KD):
                    mm = pe.transpose(banks[:, k // 4, (k % 4) * P:(k % 4) * P + tok(tt)],
                                      x_t[0:tok(tt), tt % 2, k * P:(k + 1) * P], ident[0:tok(tt), 0:tok(tt)])
                mm.then_inc(x_turned, 1)
            pe.wait_ge(rows_ready, 1)
            for i in range(5):
                pe.transpose(aux[:, 0, 16 * i:16 * i + 16], rows[0:16, i, :], ident[0:16, 0:16])
            for g in range(4):
                pe.transpose(aux[:, 0, 192 + 16 * g:192 + 16 * g + HIST], rows[0:HIST, 6 + g, :], ident[0:HIST, 0:HIST])
            for comp in range(2):
                for i in range(4):
                    mm = pe.transpose((bank_b[:, 2] if comp else aux[:, 1])[:, i * P:(i + 1) * P],
                                      c_raw[:, comp, i].rearrange("r a p -> r (a p)"), ident[:, :])
            mm.then_inc(prm_turned, 1)
            pe.wait_ge(x_lo_ready, TT)
            pe.wait_ge(xraw_ready, TT)
            for s in range(4):
                pe.wait_ge(lo_ready, s + 1)
                tile(s, bank_b if s % 2 else bank_a, s % 2, ALL, x_hi, x_lo)
                if s == 0:
                    pe.wait_ge(prm_used, 2)
                    rstd_rows(1, diag)
            pe.wait_ge(ca_ready, 1)
            pe.wait_ge(row_used, 1)
            for q in range(8):
                g2, a = q % 2, q // 2
                if q >= 2:
                    pe.wait_ge(k_evac, q - 1)
                for i in range(4):
                    for comp in range(2):
                        mm = pe.matmul(aux[0:H, q % 2, i * P:(i + 1) * P], BB[64 * g2:64 * g2 + 64, comp, 4 * a + i, :],
                                       CA[64 * g2:64 * g2 + 64, comp, 4 * a + i, 0:P], start=(comp == 0), stop=(comp == 1))
                mm.then_inc(k_turn, 1)
            pe.wait_ge(wt_ready, 1)
            pe.wait_ge(k_evac, 8)
            for r in range(8):
                if r >= 2:
                    pe.wait_ge(w_evac, r - 1)
                for i in range(4):
                    mm = pe.transpose(aux[:, r % 2, i * P:(i + 1) * P], WT[:, r // 4, 4 * (r % 4) + i, :], ident[:, :])
                mm.then_inc(w_turn, 1)
            pe.wait_ge(w_evac, 8)

            def pool_group(g):
                s0, t0 = 4 * g + S_POOL, 5 * g + T_POOL
                pe.wait_ge(lo_ready, s0 + 1)
                tile(t0, bank_a, 0, ALL, x_hi, x_lo)
                pe.wait_ge(lo_ready, s0 + 2)
                tile(t0 + 1, bank_b, 1, ALL, x_hi, x_lo)
                pe.wait_ge(lo_ready, s0 + 3)
                tile(t0 + 2, bank_a, 0, ALL, x_hi, x_lo)
                pe.wait_ge(lo_ready, s0 + 4)
                pe.wait_ge(pooled_lo, g + 1)
                hi, lo = pl_hi[:, :].unsqueeze(1), pl_lo[:, :].unsqueeze(1)
                tile(t0 + 3, bank_b, 1, [(0, 0)], hi, lo)
                pe.wait_ge(evac_done, t0 + 4)
                tile(t0 + 4, bank_b, 1, [(P, 0)], hi, lo)
                pe.transpose(aux[0:HIST, 0, 0:P], UP[:, SEQ:SEQ + HIST], ident[:, :])
                pe.transpose(aux[0:HIST, 0, P:2 * P], UP[:, T + HIST:T + 2 * HIST], ident[:, :]).then_inc(np_turned, 1)

            pool_group(0)
            pe.wait_ge(u_in, 16 * L)
            pe.wait_ge(np_evac, 1)
            for pr in range(PAIRS):
                if pr >= 2:
                    pe.wait_ge(v_evac, pr - 1)
                for comp in range(2):
                    for g2 in range(2):
                        mm = pe.matmul(aux[64 * g2:64 * g2 + 64, pr % 2, comp * NCG:(comp + 1) * NCG],
                                       W[:, comp, pr, 64 * g2:64 * g2 + 64], U[:, 2 * pr + g2, :], start=True, stop=True)
                mm.then_inc(v_turn, 1)
            pe.wait_ge(v_evac, PAIRS)
            with pe.Fori(1, 4) as g:
                pe.wait_ge(np_evac, g)
                pool_group(g)
            pe.wait_ge(s_ready, 1)
            pe.wait_ge(to_in, 16 * L)
            pe.wait_ge(np_evac, 4)
            for r in range(12):
                g2, prs = r % 2, range(3 * (r // 2), min(3 * (r // 2) + 3, PAIRS))
                if r >= 2:
                    pe.wait_ge(y_evac, r - 1)
                for i, pr in enumerate(prs):
                    out = aux[:, g2, i * NCG:(i + 1) * NCG]
                    pe.matmul(out, TO[:, 2 * pr + g2, :], U[:, 2 * pr + g2, :], start=True, stop=False)
                    for comp in range(2):
                        mm = pe.matmul(out, CA[64 * g2:64 * g2 + 64, comp, pr, H:9 * H],
                                       S[64 * g2:64 * g2 + 64, comp, pr, 0:NCG], start=False, stop=(comp == 1))
                mm.then_inc(y_turn, 1)
            pe.wait_ge(y_evac, 12)
            for i, (comp, slot) in enumerate(((0, NCP), (1, NCP), (0, NCG), (1, NCG))):
                mm = pe.transpose(aux[0:PAIRS, 0, i * P:(i + 1) * P], S[:, comp, :, slot], ident[:, :])
            mm.then_inc(st_turn, 1)
            with pe.Fori(0, 4) as m:
                s0, t0 = 4 * m + S_GLU, 6 * m + T_GLU
                for r, banks in enumerate((bank_a, bank_b)):
                    pe.wait_ge(lo_ready, s0 + 1 + r)
                    tile(t0 + r, banks, r, ALL, x_hi, x_lo)
                pe.wait_ge(y_lo_ready, KS)
                for r in range(2):
                    pe.wait_ge(lo_ready, s0 + 3 + r)
                    tile(t0 + 2 + 2 * r, bank_a, r, [(k * P, k) for k in range(KS)], y_hi, y_lo)
                    tile(t0 + 3 + 2 * r, bank_b, r, [((KS + k) * P, k) for k in range(KS)], y_hi, y_lo)

            def start_sums():
                pe.matmul(aux[:, 0, 0:TT], ones[:, :], zeros[:, 0:TT], start=True, stop=False, skip_group_check=True)

            def add_squares(n, slot):
                pe.wait_ge(sq_ready, n + 1)
                for tt in range(TT):
                    mm = pe.matmul(aux[0:tok(tt), 0, tt:tt + 1], sq[:, slot, tt * P:tt * P + tok(tt)], ones[:, 0:1],
                                   start=False, stop=False, skip_group_check=True)
                mm.then_inc(sq_used, 1)

            pe.wait_ge(st_evac, 1)
            start_sums()
            pe.wait_ge(lo_ready, S_OUT + 1)
            tile(T_OUT, bank_a, 0, ALL, x_hi, x_lo, ready=m_lo_ready)
            with pe.Fori(0, 3) as i:
                for r, banks in ((1, bank_b), (0, bank_a)):
                    n = 2 * i + 2 - r
                    pe.wait_ge(lo_ready, n + (S_OUT + 1))
                    tile(n + T_OUT, banks, r, ALL, x_hi, x_lo)
                    add_squares(n - 1, 1 - r)
            pe.wait_ge(lo_ready, S_OUT + 8)
            tile(T_OUT + 7, bank_b, 1, ALL, x_hi, x_lo)
            add_squares(6, 0)
            pe.wait_ge(lo_ready, S_FFN + 1)
            tile(T_FFN, bank_a, 0, ALL, hg_hi, hg_lo, ready=hg_lo_ready)
            add_squares(7, 1)
            pe.wait_ge(lo_ready, S_FFN + 2)
            tile(T_FFN + 1, bank_b, 1, ALL, hg_hi, hg_lo)
            rstd_rows(2, diag2)
            for r, banks in enumerate((bank_a, bank_b)):
                pe.wait_ge(lo_ready, S_FFN + 3 + r)
                tile(T_FFN + 2 + r, banks, r, ALL, hg_hi, hg_lo)

            def down(t0, s0, n, done=None):
                if n % 4 == 0:
                    pe.wait_ge(lo_ready, s0 + 1 + n // 4)
                col = (n % 4) * P
                tile(t0 + n, bank_b if n % 2 else bank_a, n // 4, [(col, 0), (4 * P + col, 1)], f_hi, f_lo)

            with pe.Fori(1, FCH) as c:
                s0, t0 = 6 * c + (S_LOOP - 6), 12 * c + (T_LOOP - 12)
                for r, banks in enumerate((bank_a, bank_b)):
                    pe.wait_ge(lo_ready, s0 + 1 + r)
                    tile(t0 + r, banks, r, ALL, hg_hi, hg_lo)
                pe.wait_ge(f_lo_ready, 2 * c)
                for n in range(KD):
                    down(t0 + 2, s0 + 2, n)
                for r, banks in enumerate((bank_a, bank_b)):
                    pe.wait_ge(lo_ready, s0 + 5 + r)
                    tile(t0 + 10 + r, banks, r, ALL, hg_hi, hg_lo)
            pe.wait_ge(f_lo_ready, 2 * FCH)
            start_sums()
            for n in range(KD):
                down(T_LAST, S_LAST, n)
                if n:
                    add_squares(KD + n - 1, (n - 1) % 2)
            add_squares(2 * KD - 1, 1)
            pe.wait_ge(hf_ready, KD)
            pe.wait_ge(evac_done, T_LAST + KD)
            for tt in range(TT):
                if tt >= 2:
                    pe.wait_ge(tok_used[tt % 2], tt // 2)
                banks = bank_b if tt % 2 else bank_a
                for k in range(KD):
                    mm = pe.transpose(banks[0:tok(tt), k // 4, (k % 4) * P:(k % 4 + 1) * P],
                                      hf[:, k, tt * P:tt * P + tok(tt)], ident[:, :])
                mm.then_inc(tok_turned, 1)

        @block.scalar
        def _(act):
            def split(s, slot, landed, done, cols=SLAB):
                act.wait_ge(stage_in[slot], landed)
                if done is not None:
                    act.wait_ge(tile_done, done)
                act.activation(w_hi[:, slot, 0:cols], stage[:, slot, 0:cols], ACT.Copy).then_inc(hi_ready, 1)

            def landed(s):
                return 16 * (s // 2 + 1) + (64 if s >= S_OUT else 0)

            for dst, src in ((rows[0:8, 5, :], t_in["g_mix"][0]), (rows[8:16, 5, :], t_in["g_ffn"][0]),
                             (rows[16:24, 5, :], t_in["g_final"]), (rows[24:32, 5, :], t_in["pool_scale"][0])):
                act.dma_start(dst, src.rearrange("(k p) -> k p", p=P)).then_inc(gains_in, 16)
            loads = [
                (rows[0:16, 0, :], t_in["ssm_a_re"][0].rearrange("(pr g) p -> pr (g p)", g=2)),
                (rows[0:16, 1, :], t_in["ssm_a_im"][0].rearrange("(pr g) p -> pr (g p)", g=2)),
                (rows[0:16, 2, :], t_in["state_ssm_re"][0, 0].rearrange("(pr g) p -> pr (g p)", g=2)),
                (rows[0:16, 3, :], t_in["state_ssm_im"][0, 0].rearrange("(pr g) p -> pr (g p)", g=2)),
                (log_dt[:, :], t_in["ssm_log_dt"][0].rearrange("(pr g) -> pr g", g=2)),
                (rows[0:HIST, 6:10, :], t_in["state_pool"][0, 0].rearrange("i (g c) -> i g c", g=4)),
            ]
            for comp, name in enumerate(("ssm_c_re", "ssm_c_im")):
                src = t_in[name][0].rearrange("(t g) h p -> (g h) t p", t=4)
                for copy in range(2):
                    loads.append((c_raw[:, comp, :, copy, :], src))
            for comp, name in enumerate(("ssm_b_re", "ssm_b_im")):
                src = t_in[name][0].rearrange("(pr g) p h -> g p pr h", g=2)
                for g2 in range(2):
                    loads.append((b_raw[64 * g2:64 * g2 + 64, comp], src[g2]))
            with nc.allow_non_contiguous_dma(reason="512 skip weights, one per (channel, group)"):
                loads.append((d_skip[:, :], t_in["ssm_d"][0].rearrange("g h -> h g")))
                assert len(loads) == PRM_LOADS
                for dst, src in loads:
                    act.dma_start(dst, src).then_inc(prm_in, 16)
            act.wait_ge(ones_ready, 1)
            for tt in range(TT + 1):
                if tt < TT:
                    act.wait_ge(x_in[tt % 2], 16 * (tt // 2 + 1))
                    if tt:
                        act.wait_ge(x_squared, tt)
                    act.activation(x_sq[0:tok(tt), :], x_t[0:tok(tt), tt % 2, :], ACT.Square,
                                   accum_out=ss[0:tok(tt), 0, tt:tt + 1]).then_inc(x_squared, 1)
                if tt:
                    u = tt - 1
                    act.wait_ge(xg_ready, tt)
                    act.activation(x_hi[:, :, u * P:u * P + tok(u)],
                                   xg[:, u % 2, :].rearrange("p (k t) -> p k t", k=KD)[:, :, 0:tok(u)],
                                   ACT.Copy).then_inc(x_hi_ready, 1)
                if tt in (5, 7):
                    s = (tt - 5) // 2
                    split(s, s, landed(s), None)

            def root(n):
                act.wait_ge(ms_ready, n)
                act.activation(ss[:, 1, :], ss[:, 0, :], ACT.Sqrt).then_inc(root_ready, 1)

            root(1)
            act.wait_ge(angle_ready, 1)
            act.activation(pt[:, 8:10, :], pt[:, 6:8, :], ACT.Sin).then_inc(sine_ready, 1)
            for s in range(2, 6):
                split(s, s % 2, landed(s), s - 1)
            act.wait_ge(x_lo_ready, TT)
            for q in range(8):
                g2, a = q % 2, q // 2
                act.wait_ge(k_turn, q + 1)
                act.activation(K_sb[:, 8 * a + g2:8 * a + 8:2, :], aux[0:H, q % 2, :].rearrange("h (i c) -> h i c", i=4),
                               ACT.Copy).then_inc(k_evac, 1)
            for r in range(8):
                act.wait_ge(w_turn, r + 1)
                act.activation(W[:, r // 4, 4 * (r % 4):4 * (r % 4) + 4, :],
                               aux[:, r % 2, :].rearrange("p (i c) -> p i c", i=4), ACT.Copy).then_inc(w_evac, 1)
            for g in range(4):
                s0, t0 = 4 * g + S_POOL, 5 * g + T_POOL
                split(s0 + 2, 0, landed(s0 + 2), t0 + 1)
                act.wait_ge(pooled_ready, g + 1)
                act.activation(pl_hi[:, :], (sum_b if g % 2 == 0 else sum_a)[:, 0:T], ACT.Copy).then_inc(pooled_hi, 1)
                for r in range(2):
                    split(s0 + 3 + r, 1 - r, landed(s0 + 3 + r), t0 + 2 + r, cols=(2 * P, SLAB)[r])
                    act.wait_ge(evac_done, t0 + 2 + r)
                    act.activation(gate_t[:, r, :], gate_t[:, r, :], ACT.Sigmoid).then_inc(gp_sig, 1)
                split(s0 + 5, 1, landed(s0 + 5), t0 + 5)
                act.wait_ge(np_turned, g + 1)
                act.activation(new_pool[:, :, g * P:(g + 1) * P], aux[0:HIST, 0, 0:2 * P].rearrange("i (a c) -> i a c", a=2),
                               ACT.Copy).then_inc(np_evac, 1)
                if g == 0:
                    act.wait_ge(wt_ready, 1)
                    for pr in range(PAIRS):
                        act.wait_ge(v_turn, pr + 1)
                        act.activation(S[:, :, pr, 1:NCG + 1], aux[:, pr % 2, 0:2 * NCG].rearrange("p (a c) -> p a c", a=2),
                                       ACT.Copy).then_inc(v_evac, 1)
            for r in range(12):
                g2, n = r % 2, min(3, PAIRS - 3 * (r // 2))
                act.wait_ge(y_turn, r + 1)
                act.activation(U[:, 6 * (r // 2) + g2:6 * (r // 2) + 2 * n:2, :],
                               aux[:, g2, 0:n * NCG].rearrange("p (i c) -> p i c", i=n), ACT.Copy).then_inc(y_evac, 1)
            act.wait_ge(st_turn, 1)
            act.activation(out_state[:, :, :], aux[0:PAIRS, 0, :].rearrange("q (i c) -> q i c", i=4), ACT.Copy).then_inc(st_evac, 1)

            def gelu(n):
                if n:
                    act.wait_ge(y_val, n)
                act.activation(ge_a[:, :], YT[:, n].rearrange("p j c -> p (j c)"), ACT.Square).then_inc(y_sq, 1)
                act.wait_ge(y_arg, n + 1)
                act.activation(ge_b[:, :], ge_a[:, :], ACT.Sigmoid, scale=GELU_C).then_inc(y_sig, 1)
                act.wait_ge(y_val, n + 1)
                act.activation(y_hi[:, n, :], ge_c[:, :], ACT.Copy).then_inc(y_hi_ready, 1)

            def glu_gates(m, r):
                s0, t0 = 4 * m + S_GLU, 6 * m + T_GLU
                split(s0 + 2 + r, r, 48 * m + 208, t0 + 1 + r)
                act.wait_ge(evac_done, t0 + 1 + r)
                act.activation(sig_s[:, r, :], sig_s[:, r, :], ACT.Sigmoid).then_inc(gs_sig, 1)

            def glu_b_side(m, r):
                s0, t0 = 4 * m + S_GLU, 6 * m + T_GLU
                split(s0 + 4 + r, r, 48 * m + 224, t0 + 4 + 2 * r)
                act.activation(b3(glu_b[:, :]), B3, ACT.Sigmoid).then_inc(b_sig, 1)

            def merged_hi(n):
                act.wait_ge(merged_ready, n + 1)
                act.activation(x_hi[:, n, :], merged[:, n, :], ACT.Copy).then_inc(m_hi_ready, 1)

            act.wait_ge(yt_in, 16 * KS)
            for r in range(2):
                gelu(2 * r)
                gelu(2 * r + 1)
                glu_gates(0, r)
            for r in range(2):
                glu_b_side(0, r)
            with act.Fori(1, 3) as m:
                for r in range(2):
                    glu_gates(m, r)
                for r in range(2):
                    glu_b_side(m, r)
            for r in range(2):
                glu_gates(3, r)
            for n in range(6):
                merged_hi(n)
            for r in range(2):
                glu_b_side(3, r)
            merged_hi(6)
            merged_hi(7)

            def squares(n, slot, src):
                if n >= 2:
                    act.wait_ge(sq_used, n - 1)
                act.activation(sq[:, slot, :], src, ACT.Square).then_inc(sq_ready, 1)

            for n in range(KD):
                split(S_OUT + n + 2, n % 2, landed(S_OUT + n + 2), T_OUT + n + 1)
                act.wait_ge(evac_done, T_OUT + n + 1)
                act.activation(hg_hi[:, n, :], hT[:, n, :], ACT.Copy, scale=gains[:, 1, n:n + 1]).then_inc(hg_hi_ready, 1)
                squares(n, n % 2, hT[:, n, :])

            def sig_f(count, t_gate):
                act.wait_ge(evac_done, t_gate + 1)
                act.activation(f_s[:, :], f_g[:, :], ACT.Sigmoid).then_inc(fs_ready, 1)

            def hi_f(r, count):
                act.wait_ge(fh_ready, count)
                act.activation(f_hi[:, r, :], f_h[:, :], ACT.Copy).then_inc(f_hi_ready, 1)

            split(S_FFN + 2, 0, landed(S_FFN + 2), T_FFN + 1)
            root(2)
            split(S_FFN + 3, 1, landed(S_FFN + 3), T_FFN + 2)
            sig_f(1, T_FFN)
            split(S_FFN + 4, 0, landed(S_FFN + 4), T_FFN + 3)
            hi_f(0, 1)
            sig_f(2, T_FFN + 2)
            split(S_FFN + 5, 1, landed(S_FFN + 5), T_FFN + 4)
            hi_f(1, 2)
            with act.Fori(1, FCH) as c:
                s0, t0 = 6 * c + (S_LOOP - 6), 12 * c + (T_LOOP - 12)
                l0 = 48 * c + (landed(S_LOOP) - 48)
                split(s0 + 2, 0, l0 + 16, t0 + 1)
                sig_f(0, t0)
                split(s0 + 3, 1, l0 + 16, t0 + 2)
                split(s0 + 4, 0, l0 + 32, t0 + 6)
                split(s0 + 5, 1, l0 + 32, t0 + 10)
                hi_f(0, 2 * c + 1)
                split(s0 + 6, 0, l0 + 48, t0 + 11)
                sig_f(0, t0 + 10)
                split(s0 + 7, 1, l0 + 48, t0 + 12)
                hi_f(1, 2 * c + 2)
            for n in range(KD):
                act.wait_ge(evac_done, T_LAST + n + 1)
                squares(KD + n, n % 2, hT[:, n, :])
                act.activation(hf[:, n, :], hT[:, n, :], ACT.Copy, scale=gains[:, 2, n:n + 1]).then_inc(hf_ready, 1)
            root(3)
            act.wait_ge(diag_ready, 3)
            for tt in range(1, TT, 2):
                act.wait_ge(tok_turned, tt + 1)
                if tt >= 4:
                    act.wait_ge(y_stored[tt % 4], 16 * (tt // 4))
                act.activation(y_out[0:tok(tt), tt % 4, :], bank_b[0:tok(tt), 0:2, :].rearrange("p b c -> p (b c)"), ACT.Copy,
                               scale=ss[0:tok(tt), 2, tt:tt + 1]).then_inc(tok_used[1], 1)

        @block.gpsimd
        def _(pool):
            def lo(s, slot, cols=SLAB):
                pool.wait_ge(hi_ready, s + 1)
                pool.tensor_tensor(w_lo[:, slot, 0:cols], stage[:, slot, 0:cols], w_hi[:, slot, 0:cols],
                                   ALU.subtract).then_inc(lo_ready, 1)

            for tt in range(TT):
                pool.wait_ge(x_hi_ready, tt + 1)
                cut = slice(tt * P, tt * P + tok(tt))
                pool.tensor_tensor(x_lo[:, :, cut], xg[:, tt % 2, :].rearrange("p (k t) -> p k t", k=KD)[:, :, 0:tok(tt)],
                                   x_hi[:, :, cut], ALU.subtract).then_inc(x_lo_ready, 1)
                if tt in (4, 6):
                    lo((tt - 4) // 2, (tt - 4) // 2)
            for s in range(2, 5):
                lo(s, s % 2)
            pool.wait_ge(wt_ready, 1)
            pool.memset(TO[:, :, :], 0.0).then_inc(to_zero, 1)
            for s in range(5, S_GLU):
                lo(s, s % 2, 2 * P if s % 4 == 3 else SLAB)
            with pool.Fori(0, (S_LAST + 2 - S_GLU) // 2) as i:
                for r in range(2):
                    lo(2 * i + (S_GLU + r), r)

        @block.vector
        def _(dve):
            steps = [0]

            def then(ins):
                steps[0] += 1
                ins.then_inc(dve_step, 1)
                dve.wait_ge(dve_step, steps[0])

            def tt_(out, a, b, op):
                return dve.tensor_tensor(out, a, b, op)

            MUL, ADD, SUB = ALU.mult, ALU.add, ALU.subtract
            dve.memset(zeros[:, :], 0.0)
            dve.memset(ss[:, :, :], 1.0)
            dve.memset(ones[:, :], 1.0).then_inc(ones_ready, 1)
            dve.wait_ge(prm_turned, 1)
            dve.tensor_copy(gains[:, :, :], aux[:, 0, 0:32].rearrange("p (v k) -> p v k", v=4)).then_inc(prm_used, 1)
            dve.wait_ge(prm_used, 1)
            for tt in range(TT):
                dve.wait_ge(x_turned, tt + 1)
                if tt >= 2:
                    dve.wait_ge(x_lo_ready, tt - 1)
                    dve.wait_ge(xraw_out[tt % 2], 16 * (tt // 2))
                turned = (bank_b if tt % 2 else bank_a)[:, 0:2, :].rearrange("p b (k t) -> p (b k) t", t=P)[:, :, 0:tok(tt)]

                def cut(buf):
                    return buf[:, tt % 2, :].rearrange("p (k t) -> p k t", k=KD)[:, :, 0:tok(tt)]
                tt_(cut(xg), turned, gains[:, 0, :].unsqueeze(2).to_broadcast([P, KD, tok(tt)]), MUL).then_inc(xg_ready, 1)
                dve.tensor_copy(cut(x_raw), turned).then_inc(xraw_ready, 1)

            def inverse_root(n, mean_in, scaled):
                dve.tensor_scalar(ss[:, 0, :], mean_in, 1.0 / D, EPS, MUL, ADD).then_inc(ms_ready, 1)
                dve.wait_ge(root_ready, n)
                then(dve.reciprocal(ss[:, 2, :], ss[:, 1, :]))
                then(tt_(ss[:, 3, :], ss[:, 2, :], ss[:, 2, :], MUL))
                then(tt_(ss[:, 3, :], ss[:, 3, :], ss[:, 0, :], MUL))
                then(dve.tensor_scalar(ss[:, 3, :], ss[:, 3, :], -0.5, 1.5, MUL, ADD))
                if scaled is None:
                    tt_(ss[:, 2, :], ss[:, 2, :], ss[:, 3, :], MUL).then_inc(diag_ready, 1)
                    return
                then(tt_(ss[:, 2, :], ss[:, 2, :], ss[:, 3, :], MUL))
                tt_(scaled[:, :, :], ident[:, :].unsqueeze(1).to_broadcast([P, TT, P]),
                    ss[:, 2, :].unsqueeze(2).to_broadcast([P, TT, P]), MUL).then_inc(diag_ready, 1)

            def take_rows(n):
                dve.wait_ge(row_ready, n)
                dve.tensor_copy(rstd_row[:, 0:SEQ], aux[:, :, :].rearrange("p b c -> p (b c)"))
                dve.tensor_copy(rstd_row[:, SEQ:T], bank_a[:, 2, 384:384 + DEC]).then_inc(row_used, 1)
                dve.wait_ge(row_used, n)

            dve.wait_ge(prm_in, 16 * PRM_LOADS)
            dve.tensor_copy(rows[0:16, 4, :].rearrange("q (g p) -> q g p", g=2),
                            log_dt[:, :].unsqueeze(2).to_broadcast([16, 2, NS])).then_inc(rows_ready, 1)
            dve.wait_ge(x_squared, TT)
            inverse_root(1, ss[:, 0, :], diag)
            dve.wait_ge(prm_turned, 2)
            dve.tensor_copy(prm[:, :, :], aux[:, 0, 0:80].rearrange("p (i q) -> p i q", i=5))
            dve.tensor_copy(state0[:, :, :], aux[:, 0, 32:64].rearrange("p (a q) -> p a q", a=2))
            dve.tensor_copy(pool_hist[:, :, :], aux[:, 0, 192:256].rearrange("p (g i) -> p g i", g=4)[:, :, 0:HIST])
            for comp, turned in enumerate((aux[:, 1], bank_b[:, 2])):
                by_group = turned.rearrange("p (q g h) -> p g q h", g=2, h=H)
                for g2 in range(2):
                    half = slice(64 * g2, 64 * g2 + 64)
                    ins = dve.tensor_copy(CT[half, comp], by_group[half, g2])
            ins.then_inc(prm_used, 1)
            dve.wait_ge(prm_used, 2)

            q = [pt[:, i, :] for i in range(30)]

            def exp_of(out, x, k, r, p):
                then(dve.tensor_scalar(x, x, -87.0, 88.0, ALU.max, ALU.min))
                then(dve.tensor_scalar(k, x, 1.4426950408889634, None, MUL))
                then(dve.tensor_scalar(k, k, MAGIC, None, ADD))
                then(dve.tensor_scalar(k, k, MAGIC, None, SUB))
                then(dve.scalar_tensor_tensor(r, k, -LN2[0], x, MUL, ADD))
                then(dve.scalar_tensor_tensor(r, k, -LN2[1], r, MUL, ADD))
                then(dve.tensor_scalar(p, r, EXP_POLY[0], None, MUL))
                for coef in EXP_POLY[1:]:
                    then(dve.scalar_tensor_tensor(p, p, coef, r, ADD, MUL))
                then(dve.tensor_scalar(r.bitcast(I32), k, 127.0, 8388608.0, ADD, MUL))
                then(dve.scalar_tensor_tensor(out, p, 1.0, r, ADD, MUL))

            def cmul(re, im, ar, ai, br, bi, t1, t2):
                tt_(t1, ar, br, MUL)
                then(tt_(t2, ai, bi, MUL))
                then(tt_(re, t1, t2, SUB))
                tt_(t1, ar, bi, MUL)
                then(tt_(t2, ai, br, MUL))
                then(tt_(im, t1, t2, ADD))

            lam, om, dt, e = q[0], prm[:, 1, :], q[1], q[2]
            then(dve.tensor_copy(q[3], prm[:, 4, :]))
            exp_of(dt, q[3], q[4], q[5], q[10])
            then(dve.tensor_scalar(lam, prm[:, 0, :], -1e-4, None, ALU.min))
            then(tt_(q[3], lam, dt, MUL))
            exp_of(e, q[3], q[4], q[5], q[10])
            then(tt_(q[3], om, dt, MUL))
            then(dve.tensor_scalar(q[4], q[3], 0.15915494309189535, None, MUL))
            then(dve.tensor_scalar(q[4], q[4], MAGIC, None, ADD))
            then(dve.tensor_scalar(q[4], q[4], MAGIC, None, SUB))
            for part in TWO_PI:
                then(dve.scalar_tensor_tensor(q[3], q[4], -part, q[3], MUL, ADD))
            then(dve.tensor_scalar(q[6], q[3], 3.1415925, -3.1415925, ALU.min, ALU.max))
            then(dve.tensor_scalar(q[7], q[6], -1.0, None, MUL))
            then(tt_(q[7], q[6], q[7], ALU.max))
            dve.tensor_scalar(q[7], q[7], -1.0, 1.5707963267948966, MUL, ADD).then_inc(angle_ready, 1)
            take_rows(1)
            dve.wait_ge(sine_ready, 1)
            then(dve.memset(PW[:, 1, 0, :], 0.0))
            then(dve.memset(PW[:, 0, 0, :], 1.0))
            ar, ai = PW[:, 0, 1, :], PW[:, 1, 1, :]
            then(tt_(ar, e, q[9], MUL))
            then(tt_(ai, e, q[8], MUL))
            then(tt_(q[10], lam, lam, MUL))
            then(tt_(q[11], om, om, MUL))
            then(tt_(q[10], q[10], q[11], ADD))
            then(dve.reciprocal(q[11], q[10]))
            then(dve.tensor_scalar(q[12], ar, -1.0, None, ADD))
            then(tt_(q[13], q[12], lam, MUL))
            then(tt_(q[14], ai, om, MUL))
            then(tt_(q[13], q[13], q[14], ADD))
            then(tt_(q[13], q[13], q[11], MUL))
            then(tt_(q[14], ai, lam, MUL))
            then(tt_(q[15], q[12], om, MUL))
            then(tt_(q[14], q[14], q[15], SUB))
            then(tt_(q[14], q[14], q[11], MUL))

            def bc_h(ap):
                return ap.unsqueeze(2).to_broadcast([P, PAIRS, H])
            wide = [P, PAIRS * H]
            dve.wait_ge(xraw_out[0], 16 * 5)
            dve.wait_ge(xraw_out[1], 16 * 4)
            t1, t2 = [t[:, 0:PAIRS * H].rearrange("p (q h) -> p q h", h=H) for t in (tmp_a, tmp_b)]
            cmul(BB[:, 0], BB[:, 1], bc_h(q[13]), bc_h(q[14]), b_raw[:, 0], b_raw[:, 1], t1, t2)

            def powers(tab, n, t1, t2):
                k = 1
                while k < n:
                    last = [tab[:, c, k - 1, :].unsqueeze(1).to_broadcast([P, k, PAIRS]) for c in range(2)]
                    cmul(tab[:, 0, k:2 * k, :], tab[:, 1, k:2 * k, :], tab[:, 0, 0:k, :], tab[:, 1, 0:k, :],
                         last[0], last[1], t1[:, 0:k, :], t2[:, 0:k, :])
                    k *= 2
            tp1, tp2 = [t[:, 0:8 * PAIRS].rearrange("p (k q) -> p k q", q=PAIRS) for t in (tmp_a, tmp_b)]
            powers(PW[:, :, 1:L + 1, :], L, tp1, tp2)
            then(dve.tensor_copy(a8pow[:, :, 0, :], PW[:, :, L, :]))
            powers(a8pow, STEPS, tp1, tp2)
            then(dve.tensor_scalar(neg_a[:, 0, :], a8pow[:, 1, 0, :], -1.0, None, MUL))
            then(dve.tensor_scalar(neg_a[:, 1, :], a8pow[:, 1, STEPS - 1, :], -1.0, None, MUL))

            def take_u(n):
                dve.wait_ge(tile_done, n + 1)
                banks = bank_b if n % 2 else bank_a
                for b0, nb, c0, nch, to in ((0, 2, 0, 44, 0), (2, 1, 88, 40, 88), (2, 1, 128, 4, NCP + 1)):
                    o = UT[:, n, :, to:to + nb * nch].rearrange("p j (b c) -> p b c j", b=nb)
                    off = 0 if c0 != 128 else 40 * L
                    i0 = banks[:, b0:b0 + nb, off:off + nch * L].rearrange("p b (c j) -> p b c j", j=L)
                    i1 = rstd_row[:, c0 * L:(c0 + nb * nch) * L].rearrange("p (b c j) -> p b c j", b=nb, j=L)
                    ins = tt_(o, i0, i1, MUL)
                ins.then_inc(evac_done, 1)

            dve.wait_ge(row_used, 1)
            take_u(0)
            big = [P, PAIRS, L + 1, H]

            def big_of(t):
                return t[:, 0:PAIRS * 9 * H].rearrange("p (q k h) -> p q k h", q=PAIRS, h=H)
            pw = [PW[:, c].rearrange("p k q -> p q k").unsqueeze(3).to_broadcast(big) for c in range(2)]
            ct = [CT[:, c].unsqueeze(2).to_broadcast(big) for c in range(2)]
            ca = [CA[:, c].rearrange("p q (k h) -> p q k h", h=H) for c in range(2)]
            tt_(big_of(tmp_a), ct[0], pw[0], MUL)
            then(tt_(big_of(tmp_b), ct[1], pw[1], MUL))
            then(tt_(ca[0], big_of(tmp_a), big_of(tmp_b), SUB))
            tt_(big_of(tmp_a), ct[0], pw[1], MUL)
            then(tt_(big_of(tmp_b), ct[1], pw[0], MUL))
            dve.scalar_tensor_tensor(CA[:, 1].rearrange("p q c -> p (q c)"), tmp_a[:, :], -1.0, tmp_b[:, :], MUL,
                                     SUB).then_inc(ca_ready, 1)
            take_u(1)
            mid = [P, PAIRS, L, H]

            def mid_of(t):
                return t[:, 0:PAIRS * L * H].rearrange("p (q k h) -> p q k h", q=PAIRS, h=H)
            pw = [PW[:, c, 0:L, :].rearrange("p k q -> p q k").unsqueeze(3).to_broadcast(mid) for c in range(2)]
            bb = [BB[:, c].unsqueeze(2).to_broadcast(mid) for c in range(2)]
            wt = [WT[:, c].rearrange("p q (k h) -> p q k h", h=H) for c in range(2)]
            dve.wait_ge(ca_ready, 1)
            tt_(mid_of(tmp_a), bb[0], pw[0], MUL)
            then(tt_(mid_of(tmp_b), bb[1], pw[1], MUL))
            then(tt_(wt[0], mid_of(tmp_a), mid_of(tmp_b), SUB))
            take_u(2)
            tt_(mid_of(tmp_a), bb[0], pw[1], MUL)
            then(tt_(mid_of(tmp_b), bb[1], pw[0], MUL))
            tt_(wt[1], mid_of(tmp_a), mid_of(tmp_b), ADD).then_inc(wt_ready, 1)
            then(dve.memset(UT[:, :, :, NCP:NCP + 1], 0.0))
            take_u(3)
            dve.wait_ge(k_evac, 8)
            lag0 = K_sb[:, :, 0:H]
            skip = skip_k[:, :].rearrange("h (g c) -> h g c", g=G)
            then(tt_(skip, ident[0:H, 0:H].unsqueeze(1).to_broadcast([H, G, H]),
                     d_skip[:, :].unsqueeze(2).to_broadcast([H, G, H]), MUL))
            tt_(lag0, lag0, skip, ADD).then_inc(k_ready, 1)

            re, im = S[:, 0], S[:, 1]

            def advance(cur, prev, shape, a_re, a_im, a_neg):
                n = int(np.prod(shape[1:]))
                u1 = [sc_a[:, c * n:(c + 1) * n] for c in range(2)]
                u2 = [sc_b[:, c * n:(c + 1) * n] for c in range(2)]

                def f(ap):
                    return ap if len(shape) == 2 else ap.rearrange("p (q s) -> p q s", q=PAIRS)

                def bc(ap):
                    return ap if len(shape) == 2 else ap.unsqueeze(2).to_broadcast(shape)
                tt_(f(u1[0]), prev[0], bc(a_re), MUL)
                tt_(f(u1[1]), prev[1], bc(a_re), MUL)
                tt_(f(u2[0]), prev[1], bc(a_neg), MUL)
                then(tt_(f(u2[1]), prev[0], bc(a_im), MUL))
                then(tt_(sc_a[:, 0:2 * n], sc_a[:, 0:2 * n], sc_b[:, 0:2 * n], ADD))
                tt_(cur[0], cur[0], f(u1[0]), ADD)
                then(tt_(cur[1], cur[1], f(u1[1]), ADD))

            seg = [x[:, :, 1:NCP + 1].rearrange("p q (s i) -> p q s i", i=STEPS) for x in (re, im)]

            def scan_steps(i0, i1):
                for i in range(i0, i1):
                    advance([x[:, :, :, i] for x in seg], [x[:, :, :, i - 1] for x in seg], [P, PAIRS, SEG],
                            a8pow[:, 0, 0, :], a8pow[:, 1, 0, :], neg_a[:, 0, :])

            def scan_ends():
                for s in range(1, SEG):
                    advance([x[:, :, s, STEPS - 1] for x in seg], [x[:, :, s - 1, STEPS - 1] for x in seg], [P, PAIRS],
                            a8pow[:, 0, STEPS - 1, :], a8pow[:, 1, STEPS - 1, :], neg_a[:, 1, :])

            def scan_sample():
                for k in range(NCP + 2, SLOTS):
                    advance([x[:, :, k] for x in (re, im)], [x[:, :, k - 1] for x in (re, im)], [P, PAIRS],
                            a8pow[:, 0, 0, :], a8pow[:, 1, 0, :], neg_a[:, 0, :])

            def scan_fill(c, done=None):
                for q0 in range(0, PAIRS, 8):
                    shape = [P, 8, SEG - 1, STEPS - 1]
                    n = 8 * (SEG - 1) * (STEPS - 1)
                    end = [x[:, q0:q0 + 8, 0:SEG - 1, STEPS - 1].unsqueeze(3).to_broadcast(shape) for x in seg]
                    apw = [a8pow[:, k, 0:STEPS - 1, q0:q0 + 8].rearrange("p i q -> p q i").unsqueeze(2).to_broadcast(shape)
                           for k in range(2)]
                    u1 = sc_a[:, 0:n].rearrange("p (q s i) -> p q s i", q=8, s=SEG - 1)
                    u2 = sc_b[:, 0:n].rearrange("p (q s i) -> p q s i", q=8, s=SEG - 1)
                    dst = seg[c][:, q0:q0 + 8, 1:SEG, 0:STEPS - 1]
                    tt_(u1, end[0], apw[c], MUL)
                    then(tt_(u2, end[1], apw[1 - c], MUL))
                    then(tt_(sc_a[:, 0:n], sc_a[:, 0:n], sc_b[:, 0:n], SUB if c == 0 else ADD))
                    if q0 and done is not None:
                        tt_(dst, dst, u1, ADD).then_inc(done, 1)
                    else:
                        then(tt_(dst, dst, u1, ADD))

            def scan_start():
                dve.wait_ge(v_evac, PAIRS)
                then(dve.memset(S[:, :, :, 0:1], 0.0))
                then(dve.tensor_copy(S[:, :, :, NCP + 1], state0[:, :, :]))

            then(dve.memset(UP[:, 0:HIST], 0.0))
            for g in range(4):
                t0 = 5 * g + T_POOL
                if g:
                    dve.wait_ge(np_turned, g)
                else:
                    dve.wait_ge(ut_out, 16)
                then(dve.tensor_copy(UP[:, HIST + SEQ:2 * HIST + SEQ], pool_hist[:, g, :]))
                dve.wait_ge(tile_done, t0 + 1)
                tt_(UP[:, HIST:HIST + 2 * BLK].rearrange("p (b t) -> p b t", b=2), A3[:, 0:2],
                    rstd_row[:, 0:2 * BLK].rearrange("p (b t) -> p b t", b=2), MUL)
                tt_(UP[:, HIST + 2 * BLK:HIST + SEQ], bank_a[:, 2, 0:BLK - DEC], rstd_row[:, 2 * BLK:SEQ], MUL)
                tt_(UP[:, 2 * HIST + SEQ:], bank_a[:, 2, BLK - DEC:BLK], rstd_row[:, SEQ:], MUL).then_inc(evac_done, 1)
                dve.wait_ge(evac_done, t0 + 1)
                src, dst = UP, sum_a
                for k in range(g + 1):
                    sh = 1 << k
                    lo_i = 2 * sh - 1
                    then(tt_(dst[:, lo_i:], src[:, lo_i:], src[:, lo_i - sh:T + 2 * HIST - sh], ADD))
                    src, dst = dst, (sum_b if dst is sum_a else sum_a)
                w = WINDOWS[g]
                dve.scalar_tensor_tensor(dst[:, 0:SEQ], src[:, HIST:HIST + SEQ], 1.0 / w, UP[:, HIST:HIST + SEQ], MUL, SUB)
                dve.scalar_tensor_tensor(dst[:, SEQ:T], src[:, 2 * HIST + SEQ:], 1.0 / w, UP[:, 2 * HIST + SEQ:], MUL, SUB)
                then(tt_(head[:, :], src[:, HIST:HIST + 16], inv_count[:, g, :], MUL))
                tt_(dst[:, 0:16], head[:, :], UP[:, HIST:HIST + 16], SUB).then_inc(pooled_ready, 1)
                dve.wait_ge(pooled_hi, g + 1)
                tt_(pl_lo[:, :], dst[:, 0:T], pl_hi[:, :], SUB).then_inc(pooled_lo, 1)
                if g == 3:
                    scan_ends()
                for r, banks in enumerate((B3, A3)):
                    dve.wait_ge(tile_done, t0 + 2 + r)
                    if g:
                        dve.wait_ge(mp_out[r], 16 * g)
                    tt_(b3(gate_t[:, r, :]), banks, b3(rstd_row[:, :]), MUL).then_inc(evac_done, 1)
                    if r == 0 and g:
                        if g == 1:
                            scan_start()
                        if g < 3:
                            scan_steps(*((1, 5), (9, 13))[g - 1])
                        else:
                            scan_sample()
                            scan_fill(0)
                for r in range(2):
                    dve.wait_ge(gp_sig, 2 * g + r + 1)
                    dve.wait_ge(tile_done, t0 + 4 + r)
                    dve.scalar_tensor_tensor(b3(gate_t[:, r, :]), B3, gains[:, 3, 2 * g + r:2 * g + r + 1],
                                             b3(gate_t[:, r, :]), MUL, MUL).then_inc(evac_done, 1)
                if g in (1, 2):
                    scan_steps(*((5, 9), (13, STEPS))[g - 1])
            scan_fill(1, done=s_ready)

            def gelu(n):
                y = YT[:, n].rearrange("p j c -> p (j c)")
                dve.wait_ge(y_sq, n + 1)
                then(dve.tensor_scalar(ge_a[:, :], ge_a[:, :], 0.044715, 1.0, MUL, ADD))
                tt_(ge_a[:, :], ge_a[:, :], y, MUL).then_inc(y_arg, 1)
                dve.wait_ge(y_sig, n + 1)
                if n:
                    dve.wait_ge(y_hi_ready, n)
                s = ge_b[:, :].rearrange("p (j c) -> p j c", c=NCG)
                tt_(ge_c[:, 0:SEQ].rearrange("p (c j) -> p j c", j=L), YT[:, n, :, 0:NCP], s[:, :, 0:NCP], MUL)
                tt_(ge_c[:, SEQ:T].rearrange("p (c j) -> p j c", j=L), YT[:, n, :, NCP + 1:], s[:, :, NCP + 1:],
                    MUL).then_inc(y_val, 1)
                dve.wait_ge(y_hi_ready, n + 1)
                tt_(y_lo[:, n, :], ge_c[:, :], y_hi[:, n, :], SUB).then_inc(y_lo_ready, 1)

            def glu_gates(m, r):
                t0 = 6 * m + T_GLU
                dve.wait_ge(tile_done, t0 + 1 + r)
                tt_(b3(sig_s[:, r, :]), B3 if r else A3, b3(rstd_row[:, :]), MUL).then_inc(evac_done, 1)

            def merge(m, r):
                t0 = 6 * m + T_GLU
                dve.wait_ge(gs_sig, 2 * m + r + 1)
                dve.wait_ge(tile_done, t0 + 3 + 2 * r)
                if not (isinstance(m, int) and m == r == 0):
                    dve.wait_ge(merged_ready, 2 * m + r)
                tt_(b3(glu_a[:, :]), A3, b3(sig_s[:, r, :]), MUL).then_inc(evac_done, 1)
                dve.wait_ge(evac_done, t0 + 3 + 2 * r)
                dve.wait_ge(b_sig, 2 * m + r + 1)
                tt_(glu_a[:, :], glu_a[:, :], glu_b[:, :], MUL).then_inc(evac_done, 1)
                dve.wait_ge(evac_done, t0 + 4 + 2 * r)
                dve.wait_ge(mp_in[r], 16 * m + 16)
                out = merged[:, 2 * m + r, :] if isinstance(m, int) else merged[:, ds(2 * m + r, 1), :].rearrange("p a t -> p (a t)")
                tt_(out, glu_a[:, :], pool_t[:, r, :], ADD).then_inc(merged_ready, 1)

            def merged_lo(n):
                dve.wait_ge(m_hi_ready, n + 1)
                tt_(x_lo[:, n, :], merged[:, n, :], x_hi[:, n, :], SUB).then_inc(m_lo_ready, 1)

            for r in range(2):
                gelu(2 * r)
                gelu(2 * r + 1)
                glu_gates(0, r)
            for r in range(2):
                merge(0, r)
            with dve.Fori(1, 3) as m:
                for r in range(2):
                    glu_gates(m, r)
                for r in range(2):
                    merge(m, r)
            for r in range(2):
                glu_gates(3, r)
            for n in range(6):
                merged_lo(n)
            for r in range(2):
                merge(3, r)
            merged_lo(6)
            merged_lo(7)

            for n in range(KD):
                dve.wait_ge(tile_done, T_OUT + n + 1)
                dve.wait_ge(xt_in[n], 16)
                tt_(b3(hT[:, n, :]), B3 if n % 2 else A3, b3(hT[:, n, :]), ADD).then_inc(evac_done, 1)
                dve.wait_ge(hg_hi_ready, n + 1)
                dve.scalar_tensor_tensor(hg_lo[:, n, :], hT[:, n, :], gains[:, 1, n:n + 1], hg_hi[:, n, :], MUL,
                                         SUB).then_inc(hg_lo_ready, 1)
            dve.wait_ge(sq_used, KD)
            inverse_root(2, aux[:, 0, 0:TT], diag2)
            take_rows(2)

            def hidden(r, t_gate, t_up, n, step):
                dve.wait_ge(tile_done, t_gate + 1)
                tt_(b3(f_g[:, :]), A3, b3(rstd_row[:, :]), MUL).then_inc(evac_done, 1)
                dve.wait_ge(evac_done, t_gate + 1)
                dve.wait_ge(fs_ready, n + 1)
                tt_(f_g[:, :], f_g[:, :], f_s[:, :], MUL).then_inc(dve_step, 1)
                dve.wait_ge(tile_done, t_up + 1)
                tt_(b3(f_u[:, :]), B3, b3(rstd_row[:, :]), MUL).then_inc(evac_done, 1)
                dve.wait_ge(dve_step, step)
                dve.wait_ge(evac_done, t_up + 1)
                tt_(f_h[:, :], f_g[:, :], f_u[:, :], MUL).then_inc(fh_ready, 1)

            def hidden_lo(r, n):
                dve.wait_ge(f_hi_ready, n + 1)
                tt_(f_lo[:, r, :], f_h[:, :], f_hi[:, r, :], SUB).then_inc(f_lo_ready, 1)

            def add_down(t0, n):
                dve.wait_ge(tile_done, t0 + n + 1)
                tt_(b3(hT[:, n, :]), B3 if n % 2 else A3, b3(hT[:, n, :]), ADD).then_inc(evac_done, 1)

            base_step = steps[0]
            for r in range(2):
                hidden(r, T_FFN + 2 * r, T_FFN + 2 * r + 1, r, base_step + r + 1)
                hidden_lo(r, r)
            with dve.Fori(1, FCH) as c:
                t0 = 12 * c + (T_LOOP - 12)
                hidden(0, t0, t0 + 1, 2 * c, 2 * c + (base_step + 1))
                for n in range(KD):
                    add_down(t0 + 2, n)
                hidden_lo(0, 2 * c)
                hidden(1, t0 + 10, t0 + 11, 2 * c + 1, 2 * c + (base_step + 2))
                hidden_lo(1, 2 * c + 1)
            steps[0] = base_step + 2 * FCH
            for n in range(KD):
                add_down(T_LAST, n)
            dve.wait_ge(sq_used, 2 * KD)
            inverse_root(3, aux[:, 0, 0:TT], None)
            dve.wait_ge(diag_ready, 3)
            for tt in range(0, TT, 2):
                dve.wait_ge(tok_turned, tt + 1)
                if tt >= 4:
                    dve.wait_ge(y_stored[tt % 4], 16 * (tt // 4))
                dve.tensor_scalar(y_out[0:tok(tt), tt % 4, :], bank_a[0:tok(tt), 0:2, :].rearrange("p b c -> p (b c)"),
                                  ss[0:tok(tt), 2, tt:tt + 1], None, MUL).then_inc(tok_used[0], 1)


INPUTS = ["x_prompt", "x_sample", "state_ssm_re", "state_ssm_im", "state_pool", "g_mix", "w_in", "ssm_a_re", "ssm_a_im",
          "ssm_log_dt", "ssm_b_re", "ssm_b_im", "ssm_c_re", "ssm_c_im", "ssm_d", "w_glu_a", "w_glu_b", "pool_w",
          "pool_scale", "w_out", "g_ffn", "w_ffn_gate", "w_ffn_up", "w_ffn_down", "g_final"]
OUTPUTS = {"y_p": (1, SEQ, D), "y_s": (1, DEC, D), "re_p": (1, 1, G, NS), "im_p": (1, 1, G, NS),
           "pool_p": (1, 1, HIST, W_POOL), "re_s": (1, 1, G, NS), "im_s": (1, 1, G, NS), "pool_s": (1, 1, HIST, W_POOL)}


def kernel(**inputs):
    import concourse.bacc as bacc
    from concourse.bass_utils import run_bass_kernel_spmd

    arrays = {name: np.ascontiguousarray(inputs[name]) for name in INPUTS}
    arrays["c_ident"] = np.eye(P, dtype=np.float32)
    counts = [[1.0 / min(t + 1, w) for t in range(16)] for w in WINDOWS]
    arrays["c_inv_count"] = np.broadcast_to(np.array(counts, np.float32), (P, 4, 16)).copy()
    nc = bacc.Bacc("TRN2", target_bir_lowering=False, num_devices=1, dynamic_dma_scratch_size=1024)
    t_in = {n: nc.dram_tensor(f"in_{n}", a.shape, F32, kind="ExternalInput").ap() for n, a in arrays.items()}
    t_out = {n: nc.dram_tensor(f"out_{n}", s, F32, kind="ExternalOutput").ap() for n, s in OUTPUTS.items()}
    hybrid_layer(nc, t_in, t_out)
    r = run_bass_kernel_spmd(nc, [{f"in_{n}": a for n, a in arrays.items()}], core_ids=[0])
    return tuple(r.results[0][f"out_{n}"] for n in OUTPUTS)
```

```python
from contextlib import ExitStack

import numpy as np

import concourse.bass as bass
from concourse import mybir
from concourse.alu_op_type import AluOpType as ALU

F32 = mybir.dt.float32
F32R = mybir.dt.float32r
I32 = mybir.dt.int32
ACT = mybir.ActivationFunctionType
ds = bass.ds

P = 128
D = 1024
SEQ, DEC = 1024, 32
T = SEQ + DEC
KD = D // P
BLK = T // 3
TT = -(-T // P)
W_SSM = W_POOL = D // 2
KS = W_SSM // P
G, H, NS = 32, 16, 64
PAIRS = G // 2
L = 8
NC = T // L
NCP = SEQ // L
NCG = NC + 1
SLOTS = NCG + 1
SEG, STEPS = 8, NCP // 8
WINDOWS = (2, 4, 8, 16)
HIST = 15
FF = 2816
FCH = FF // P // 2
EPS = 1e-6
X_SLOTS, XG_SLOTS = 4, 4
PRM_LOADS = 15
SLAB = 8 * P
GELU_C = 2.0 * 0.7978845608028654
TWO_PI = (6.28125, 0.0019350051879882812, 3.019916050561733e-07)
LN2 = (0.693359375, -2.12194440e-4)
EXP_POLY = [1.0 / 5040, 1.0 / 720, 1.0 / 120, 1.0 / 24, 1.0 / 6, 0.5, 1.0]
MAGIC = 12582912.0

S_POOL, T_POOL = 4, 4
S_GATE, T_GATE = 20, 24
S_GLU, T_GLU = 28, 32
S_OUT, T_OUT = 36, 48
S_FFN, T_FFN = 44, 56
S_LOOP, T_LOOP = 48, 60
S_LAST, T_LAST = 108, 180


def hybrid_layer(nc, t_in, t_out):
    ctx = ExitStack()
    with ctx:
        def sb(name, shape, dt=F32, stack=ctx):
            return stack.enter_context(nc.sbuf_tensor(name, shape, dt))

        def overlay(*tensors):
            with ExitStack() as stack:
                return [sb(n, s, d, stack) for n, s, d in tensors]

        def sem(name):
            return ctx.enter_context(nc.semaphore(name))

        ident = sb("ident", [P, P])
        ones = sb("ones", [P, P])
        inv_count = sb("inv_count", [P, 4, 16])
        gains = sb("gains", [P, 4, KD])
        stage = sb("stage", [P, 2, SLAB])
        w_hi = sb("w_hi", [P, 2, SLAB], F32R)
        w_lo = sb("w_lo", [P, 2, SLAB], F32R)
        rstd_row = sb("rstd_row", [P, T])
        ss = sb("ss", [P, 4, TT])
        a8pow = sb("a8pow", [P, 2, STEPS, PAIRS])
        neg_a = sb("neg_a", [P, 2, PAIRS])
        pool_hist = sb("pool_hist", [P, 4, HIST])
        new_pool = sb("new_pool", [HIST, 2, W_POOL])
        d_skip = sb("d_skip", [H, G])
        out_state = sb("out_state", [PAIRS, 4, P])
        log_dt = sb("log_dt", [PAIRS, 2])
        zeros = sb("zeros", [P, 16])
        state0 = sb("state0", [P, 2, PAIRS])
        head = sb("head", [P, 16])
        base = ExitStack()
        x_hi = sb("x_hi", [P, KD, T], F32R, base)
        x_lo = sb("x_lo", [P, KD, T], F32R, base)
        U, S, TO, CA, W, UT, pl_hi, pl_lo, gate_t = overlay(
            ("U", [P, G, NCG], F32),
            ("S", [P, 2, PAIRS, SLOTS], F32),
            ("TO", [P, G, P], F32),
            ("CA", [P, 2, PAIRS, (L + 1) * H], F32),
            ("W", [P, 2, PAIRS, P], F32),
            ("UT", [P, KS, L, NCG], F32),
            ("pl_hi", [P, T], F32R), ("pl_lo", [P, T], F32R),
            ("gate_t", [P, 2, T], F32))
        (xg,) = overlay(("xg", [P, XG_SLOTS, D], F32))
        (K_sb,) = overlay(("K_sb", [H, G, P], F32))
        _, x_raw = overlay(("pad0", [P, G * NCG], F32), ("x_raw", [P, 2, D], F32))
        _, WT = overlay(("pad1", [P, G * NCG], F32), ("WT", [P, 2, PAIRS, P], F32))
        q_space = G * NCG + 2 * PAIRS * SLOTS
        _, x_t = overlay(("pad17", [P, q_space], F32), ("x_t", [P, X_SLOTS, D], F32))
        _, tmp_a, _, tmp_b = overlay(("pad2", [P, q_space], F32), ("tmp_a", [P, PAIRS * 9 * H], F32),
                                     ("pad3", [P, G * P - PAIRS * 9 * H + 2 * PAIRS * 9 * H], F32),
                                     ("tmp_b", [P, PAIRS * 9 * H], F32))
        ut_at = q_space + G * P + 2 * PAIRS * 9 * H + 2 * PAIRS * P
        _, diag = overlay(("pad4", [P, ut_at], F32), ("diag", [P, TT, P], F32))
        _, UP, sum_a, sum_b = overlay(("pad5", [P, ut_at], F32), ("UP", [P, T + 2 * HIST], F32),
                                      ("sum_a", [P, T + 2 * HIST], F32), ("sum_b", [P, T + 2 * HIST], F32))
        pl_at = ut_at + KS * L * NCG
        _, rows, c_raw, b_raw, prm, pt, BB, CT, PW = overlay(
            ("pad6", [P, pl_at], F32),
            ("rows", [32, 10, P], F32), ("c_raw", [P, 2, 4, 2, NS], F32), ("b_raw", [P, 2, PAIRS, H], F32),
            ("prm", [P, 5, PAIRS], F32), ("pt", [P, 30, PAIRS], F32), ("BB", [P, 2, PAIRS, H], F32),
            ("CT", [P, 2, PAIRS, H], F32), ("PW", [P, 2, L + 1, PAIRS], F32))
        _, skip_k = overlay(("pad16", [P, pl_at], F32), ("skip_k", [H, G * H], F32))
        w_at = q_space + G * P + 2 * PAIRS * 9 * H
        _, sc_a, sc_b = overlay(("pad7", [P, w_at], F32), ("sc_a", [P, PAIRS * 7 * 15], F32),
                                ("sc_b", [P, PAIRS * 7 * 15], F32))
        _, x_sq = overlay(("pad8", [P, ut_at + TT * P], F32), ("x_sq", [P, D], F32))
        y_hi, y_lo = overlay(("y_hi", [P, KS, T], F32R), ("y_lo", [P, KS, T], F32R))
        _, YT = overlay(("pad9", [P, ut_at + 4 * T], F32), ("YT", [P, KS, L, NCG], F32))
        _, ge_a, ge_b, ge_c = overlay(("pad10", [P, w_at], F32), ("ge_a", [P, L * NCG], F32),
                                      ("ge_b", [P, L * NCG], F32), ("ge_c", [P, T], F32))
        _, merged = overlay(("pad11", [P, q_space], F32), ("merged", [P, KD, T], F32))
        _, glu_a, glu_b = overlay(("pad12", [P, w_at], F32), ("glu_a", [P, T], F32), ("glu_b", [P, T], F32))
        _, pool_t, sig_s = overlay(("pad13", [P, ut_at], F32), ("pool_t", [P, 2, T], F32),
                                   ("sig_s", [P, 2, T], F32))
        hT, _, hg_hi, hg_lo, sq, sq_sum = overlay(
            ("hT", [P, KD, T], F32), ("pad14", [P, q_space - KD * T], F32),
            ("hg_hi", [P, KD, T], F32R), ("hg_lo", [P, KD, T], F32R), ("sq", [P, 2, T], F32), ("sq_sum", [P, T], F32))
        base.close()
        f_hi, f_lo, f_g, f_s, f_u, f_h = overlay(
            ("f_hi", [P, 2, T], F32R), ("f_lo", [P, 2, T], F32R), ("f_g", [P, T], F32), ("f_s", [P, T], F32),
            ("f_u", [P, T], F32), ("f_h", [P, T], F32))
        _, hf = overlay(("pad15", [P, 8 * T], F32), ("hf", [P, KD, T], F32))
        y_out, diag2 = overlay(("y_out", [P, 4, D], F32), ("diag2", [P, TT, P], F32))

        bank_a = ctx.enter_context(nc.psum_tensor("bank_a", [P, 3, 512], F32))
        bank_b = ctx.enter_context(nc.psum_tensor("bank_b", [P, 3, 512], F32))
        aux = ctx.enter_context(nc.psum_tensor("aux", [P, 2, 512], F32))
        A3, B3 = bank_a[:, :, 0:BLK], bank_b[:, :, 0:BLK]

        def gate_at(n):
            return sig_s[:, n, :] if n < 2 else merged[:, n, :]

        def at_tile(buf, n):
            return buf[:, n, :] if isinstance(n, int) else buf[:, ds(n, 1), :].rearrange("p a t -> p (a t)")

        def b3(ap):
            return ap.rearrange("p (b t) -> p b t", b=3)

        consts_in, prm_in, gains_in = sem("consts_in"), sem("prm_in"), sem("gains_in")
        x_in = [sem(f"x_in{i}") for i in range(X_SLOTS)]
        stage_in = [sem("stage_in0"), sem("stage_in1")]
        hi_ready, lo_ready = sem("hi_ready"), sem("lo_ready")
        tile_done, evac_done = sem("tile_done"), sem("evac_done")
        ones_ready, dve_step = sem("ones_ready"), sem("dve_step")
        x_turned, x_squared, xg_ready, xraw_ready = sem("x_turned"), sem("x_squared"), sem("xg_ready"), sem("xraw_ready")
        x_hi_ready, x_lo_ready, xraw_out = sem("x_hi_ready"), sem("x_lo_ready"), [sem("xraw_out0"), sem("xraw_out1")]
        ms_ready, root_ready, diag_ready, row_ready, row_used = (
            sem("ms_ready"), sem("root_ready"), sem("diag_ready"), sem("row_ready"), sem("row_used"))
        rows_ready, prm_turned, prm_used = sem("rows_ready"), sem("prm_turned"), sem("prm_used")
        angle_ready, sine_ready = sem("angle_ready"), sem("sine_ready")
        ca_ready, wt_ready, k_turn, k_evac, w_turn, w_evac = (
            sem("ca_ready"), sem("wt_ready"), sem("k_turn"), sem("k_evac"), sem("w_turn"), sem("w_evac"))
        to_zero, k_ready, to_in = sem("to_zero"), sem("k_ready"), sem("to_in")
        ut_out, u_in = sem("ut_out"), sem("u_in")
        pooled_ready, pooled_hi, pooled_lo, np_turned, np_evac = (
            sem("pooled_ready"), sem("pooled_hi"), sem("pooled_lo"), sem("np_turned"), sem("np_evac"))
        gp_sig, mp_out = sem("gp_sig"), [sem("mp_out0"), sem("mp_out1")]
        v_turn, v_evac, s_ready, y_turn, y_evac, st_turn, st_evac = (
            sem("v_turn"), sem("v_evac"), sem("s_ready"), sem("y_turn"), sem("y_evac"), sem("st_turn"), sem("st_evac"))
        y_out_dram, yt_in = sem("y_out_dram"), [sem(f"yt_in{n}") for n in range(KS)]
        y_sq, y_arg, y_sig, y_val, y_hi_ready, y_lo_ready = (
            sem("y_sq"), sem("y_arg"), sem("y_sig"), sem("y_val"), sem("y_hi_ready"), sem("y_lo_ready"))
        gs_sig, b_sig, mp_in, merged_ready, m_hi_ready, m_lo_ready = (
            sem("gs_sig"), sem("b_sig"), [sem("mp_in0"), sem("mp_in1")], sem("merged_ready"),
            sem("m_hi_ready"), sem("m_lo_ready"))
        ss_turned, hg_hi_ready, hg_lo_ready, sq_ready, sq_used = (
            sem("ss_turned"), sem("hg_hi_ready"), sem("hg_lo_ready"), sem("sq_ready"), sem("sq_used"))
        fg_ready, fs_ready, fh_ready, f_hi_ready, f_lo_ready = (
            sem("fg_ready"), sem("fs_ready"), sem("fh_ready"), sem("f_hi_ready"), sem("f_lo_ready"))
        hf_ready, tok_turned, tok_used, y_stored = (sem("hf_ready"), sem("tok_turned"), [sem("tok_used0"), sem("tok_used1")],
                                                    [sem(f"y_stored{i}") for i in range(4)])
        small_out = sem("small_out")
        xt_in = [sem(f"xt_in{k}") for k in range(KD)]

        w_in = t_in["w_in"][0].rearrange("(k p) n -> p k n", p=P)
        w_a = t_in["w_glu_a"][0].rearrange("(k p) n -> p k n", p=P)
        w_b = t_in["w_glu_b"][0].rearrange("(k p) n -> p k n", p=P)
        w_o = t_in["w_out"][0].rearrange("(k p) n -> p k n", p=P)
        w_g = t_in["w_ffn_gate"][0].rearrange("(k p) n -> p k n", p=P)
        w_u = t_in["w_ffn_up"][0].rearrange("(k p) n -> p k n", p=P)
        w_d = t_in["w_ffn_down"][0].rearrange("(k p) n -> p k n", p=P)
        pool_w = t_in["pool_w"][0]
        xt_dram = nc.dram_tensor("xt_scratch", [D, T], F32).ap()
        u_dram = nc.dram_tensor("u_scratch", [W_SSM, L, NCG], F32).ap()
        y_dram = nc.dram_tensor("y_scratch", [W_SSM, L, NCG], F32).ap()
        mp_dram = nc.dram_tensor("mp_scratch", [D, T], F32).ap()
        x_p, x_s = t_in["x_prompt"][0], t_in["x_sample"][0]

        def tok(tt):
            return min(P, T - tt * P)

        def slab3(slot):
            return stage[:, slot, :].rearrange("p (k n) -> p k n", n=P)

        prm_loads = [
            (rows[0:16, 0, :], t_in["ssm_a_re"][0].rearrange("(pr g) p -> pr (g p)", g=2)),
            (rows[0:16, 1, :], t_in["ssm_a_im"][0].rearrange("(pr g) p -> pr (g p)", g=2)),
            (rows[0:16, 2, :], t_in["state_ssm_re"][0, 0].rearrange("(pr g) p -> pr (g p)", g=2)),
            (rows[0:16, 3, :], t_in["state_ssm_im"][0, 0].rearrange("(pr g) p -> pr (g p)", g=2)),
            (log_dt[:, :], t_in["ssm_log_dt"][0].rearrange("(pr g) -> pr g", g=2)),
            (rows[0:HIST, 6:10, :], t_in["state_pool"][0, 0].rearrange("i (g c) -> i g c", g=4)),
            (d_skip[:, :], t_in["ssm_d"][0].rearrange("g h -> h g")),
        ]
        for comp, name in enumerate(("ssm_c_re", "ssm_c_im")):
            src = t_in[name][0].rearrange("(t g) h p -> (g h) t p", t=4)
            for copy in range(2):
                prm_loads.append((c_raw[:, comp, :, copy, :], src))
        for comp, name in enumerate(("ssm_b_re", "ssm_b_im")):
            src = t_in[name][0].rearrange("(pr g) p h -> g p pr h", g=2)
            for g2 in range(2):
                prm_loads.append((b_raw[64 * g2:64 * g2 + 64, comp], src[g2]))
        assert len(prm_loads) == PRM_LOADS

        def spill_x(sp, tt):
            sp.wait_ge(xraw_ready, tt + 1)
            sp.dma_start(xt_dram[:, tt * P:tt * P + tok(tt)].rearrange("(k p) t -> p k t", p=P),
                         x_raw[:, tt % 2, :].rearrange("p (k t) -> p k t", k=KD)[:, :, 0:tok(tt)]).then_inc(xraw_out[tt % 2], 16)

        def spill_mp(sp, g):
            for r in range(2):
                n = 2 * g + r
                sp.wait_ge(evac_done, T_POOL + 5 * g + 4 + r)
                sp.dma_start(mp_dram[n * P:(n + 1) * P, :], gate_t[:, r, :]).then_inc(mp_out[r], 16)

        block = ctx.enter_context(nc.Block())

        @block.sync
        def _(sp):
            def slab(s, slot, pieces):
                if not (isinstance(s, int) and s < 2):
                    sp.wait_ge(lo_ready, s - 1)
                for i, (dst, src) in enumerate(pieces):
                    sp.dma_start(dst, src).then_inc(stage_in[slot], 16)

            sp.dma_start(ident[:], t_in["c_ident"]).then_inc(consts_in, 16)
            sp.dma_start(inv_count[:], t_in["c_inv_count"]).then_inc(consts_in, 16)

            def load_x(tt):
                if tt >= X_SLOTS:
                    sp.wait_ge(x_turned, tt - X_SLOTS + 1)
                    sp.wait_ge(x_squared, tt - X_SLOTS + 1)
                src = x_p[tt * P:(tt + 1) * P, :] if tt < SEQ // P else x_s
                sp.dma_start(x_t[0:tok(tt), tt % X_SLOTS, :], src).then_inc(x_in[tt % X_SLOTS], 16)

            for tt in range(X_SLOTS):
                load_x(tt)
            for s in range(2):
                slab(s, s, [(slab3(s), w_in[:, :, s * P:(s + 1) * P])])
            with nc.allow_non_contiguous_dma(reason="512 skip weights, one per (channel, group)"):
                for dst, src in prm_loads:
                    sp.dma_start(dst, src).then_inc(prm_in, 16)
            for tt in range(TT):
                if tt + X_SLOTS < TT:
                    load_x(tt + X_SLOTS)
                spill_x(sp, tt)
            for s in (2, 3):
                slab(s, s % 2, [(slab3(s % 2), w_in[:, :, s * P:(s + 1) * P])])
            slab(4, 0, [(slab3(0), w_in[:, :, W_SSM:W_SSM + P])])
            slab(5, 1, [(slab3(1), w_in[:, :, 2 * W_SSM + D:2 * W_SSM + D + P])])
            sp.wait_ge(evac_done, KS)
            sp.dma_start(u_dram.rearrange("(n p) j c -> p n j c", p=P), UT[:, :, :, :]).then_inc(ut_out, 16)
            sp.wait_ge(k_ready, 1)
            sp.wait_ge(to_zero, 1)
            for i in range(L):
                j = L - 1 - i
                sp.dma_start(TO[16 * i:16 * i + 16, :, 16 * j:P], K_sb[:, :, 0:P - 16 * j]).then_inc(to_in, 16)
            sp.wait_ge(ut_out, 16)
            sp.wait_ge(to_in, 16 * L)
            for i in range(L):
                sp.dma_start(U[16 * i:16 * i + 16, :, :],
                             u_dram[:, L - 1 - i, :].rearrange("(g h) c -> h g c", h=H)).then_inc(u_in, 16)
            for g in range(4):
                s0 = S_POOL + 4 * g
                if g > 0:
                    slab(s0, 0, [(slab3(0), w_in[:, :, W_SSM + g * P:W_SSM + (g + 1) * P])])
                    c0 = 2 * W_SSM + D + 2 * g * P
                    slab(s0 + 1, 1, [(slab3(1), w_in[:, :, c0:c0 + P])])
                c1 = 2 * W_SSM + D + (2 * g + 1) * P
                slab(s0 + 2, 0, [(slab3(0), w_in[:, :, c1:c1 + P])])
                slab(s0 + 3, 1, [(stage[:, 1, 0:2 * P], pool_w[g])])
                if g > 0:
                    spill_mp(sp, g - 1)
            def gate_slab(n):
                c0 = 2 * W_SSM + n * P
                slab(S_GATE + n, n % 2, [(slab3(n % 2), w_in[:, :, c0:c0 + P])])

            for n in range(2):
                gate_slab(n)
            spill_mp(sp, 3)
            for n in range(2, 6):
                gate_slab(n)
            sp.wait_ge(np_evac, 4)
            sp.dma_start(t_out["pool_p"][0, 0], new_pool[:, 0, :]).then_inc(small_out, 16)
            sp.dma_start(t_out["pool_s"][0, 0], new_pool[:, 1, :]).then_inc(small_out, 16)
            sp.wait_ge(y_evac, 12)
            for j in range(L):
                sp.dma_start(y_dram[:, j, :].rearrange("(g h) c -> h g c", h=H),
                             U[16 * j:16 * j + 16, :, :]).then_inc(y_out_dram, 16)
            for q in mp_out:
                sp.wait_ge(q, 16 * 4)
            sp.wait_ge(y_out_dram, 16 * L)
            for n in range(KS):
                sp.dma_start(YT[:, n], y_dram[n * P:(n + 1) * P]).then_inc(yt_in[n], 16)
            sp.wait_ge(st_evac, 1)
            for i, name in enumerate(("re_p", "im_p", "re_s", "im_s")):
                sp.dma_start(t_out[name][0, 0].rearrange("(pr g) p -> pr (g p)", g=2),
                             out_state[:, i, :]).then_inc(small_out, 16)
            for n in range(6, KD):
                gate_slab(n)
            for n in range(KD):
                r = n % 2
                half = slab3(r)
                slab(S_GLU + n, r, [(half[:, 0:4], w_a[:, :, n * P:(n + 1) * P]),
                                    (half[:, 4:8], w_b[:, :, n * P:(n + 1) * P])])
                if n >= 2:
                    sp.wait_ge(merged_ready, n - 1)
                sp.dma_start(pool_t[:, r, :], mp_dram[n * P:(n + 1) * P, :]).then_inc(mp_in[r], 16)
            for n in range(KD):
                slab(S_OUT + n, n % 2, [(slab3(n % 2), w_o[:, :, n * P:(n + 1) * P])])
                if n == 1:
                    sp.wait_ge(tile_done, T_OUT)
                    for q, n_out in zip(xraw_out, (5, 4)):
                        sp.wait_ge(q, 16 * n_out)
                    for k in range(KD):
                        sp.dma_start(hT[:, k, :], xt_dram[k * P:(k + 1) * P, :]).then_inc(xt_in[k], 16)
            for f in range(2):
                slab(S_FFN + 2 * f, 0, [(slab3(0), w_g[:, :, f * P:(f + 1) * P])])
                slab(S_FFN + 2 * f + 1, 1, [(slab3(1), w_u[:, :, f * P:(f + 1) * P])])
            down = [stage[:, r, :].rearrange("p (k n) -> p k n", n=4 * P) for r in range(2)]
            with sp.Fori(1, FCH) as c:
                s0 = 6 * c + (S_LOOP - 6)
                slab(s0, 0, [(slab3(0), w_g[:, :, ds(c * (2 * P), P)])])
                slab(s0 + 1, 1, [(slab3(1), w_u[:, :, ds(c * (2 * P), P)])])
                for r in range(2):
                    slab(s0 + 2 + r, r, [(down[r], w_d[:, ds(c * 2 - 2, 2), r * 4 * P:(r + 1) * 4 * P])])
                slab(s0 + 4, 0, [(slab3(0), w_g[:, :, ds(c * (2 * P) + P, P)])])
                slab(s0 + 5, 1, [(slab3(1), w_u[:, :, ds(c * (2 * P) + P, P)])])
            for r in range(2):
                slab(S_LAST + r, r, [(down[r], w_d[:, 2 * FCH - 2:2 * FCH, r * 4 * P:(r + 1) * 4 * P])])
            for tt in range(TT):
                sp.wait_ge(tok_used[tt % 2], tt // 2 + 1)
                dst = t_out["y_p"][0, tt * P:(tt + 1) * P, :] if tt < SEQ // P else t_out["y_s"][0]
                sp.dma_start(dst, y_out[0:tok(tt), tt % 4, :]).then_inc(y_stored[tt % 4], 16)
            for i in range(4):
                sp.wait_ge(y_stored[i], 16 * len(range(i, TT, 4)))
            sp.wait_ge(small_out, 16 * 6)


        @block.tensor
        def _(pe):
            def tile(t, banks, slot, terms, hi, lo, ready=None):
                if not (isinstance(t, int) and t < 2):
                    pe.wait_ge(evac_done, t - 1)
                for i, (col, k) in enumerate(terms):
                    if ready is not None:
                        pe.wait_ge(ready, k + 1)
                    for step, (w, x) in enumerate(((w_hi, hi), (w_hi, lo), (w_lo, hi))):
                        for b in range(3):
                            mm = pe.matmul(banks[:, b, 0:BLK], w[:, slot, col:col + P],
                                           x[:, k, b * BLK:(b + 1) * BLK],
                                           start=(i == 0 and step == 0), stop=(i == len(terms) - 1 and step == 2))
                mm.then_inc(tile_done, 1)

            ALL = [(k * P, k) for k in range(KD)]

            def rstd_rows(n, scaled):
                pe.wait_ge(diag_ready, n)
                for tt in range(TT):
                    out = aux[:, tt // 4, (tt % 4) * P:(tt % 4 + 1) * P] if tt < 8 else bank_a[:, 2, 384:384 + DEC]
                    mm = pe.matmul(out, ones[0:tok(tt), :], scaled[0:tok(tt), tt, 0:tok(tt)], start=True, stop=True)
                mm.then_inc(row_ready, 1)

            pe.wait_ge(consts_in, 32)
            pe.wait_ge(gains_in, 64)
            pe.transpose(aux[:, 0, 0:32], rows[0:32, 5, :], ident[0:32, 0:32]).then_inc(prm_turned, 1)
            for tt in range(TT):
                pe.wait_ge(x_in[tt % X_SLOTS], 16 * (tt // X_SLOTS + 1))
                if tt >= 2:
                    pe.wait_ge(xraw_ready, tt - 1)
                banks = bank_b if tt % 2 else bank_a
                for k in range(KD):
                    mm = pe.transpose(banks[:, k // 4, (k % 4) * P:(k % 4) * P + tok(tt)],
                                      x_t[0:tok(tt), tt % X_SLOTS, k * P:(k + 1) * P], ident[0:tok(tt), 0:tok(tt)])
                mm.then_inc(x_turned, 1)
            pe.wait_ge(rows_ready, 1)
            for i in range(5):
                pe.transpose(aux[:, 0, 16 * i:16 * i + 16], rows[0:16, i, :], ident[0:16, 0:16])
            for g in range(4):
                pe.transpose(aux[:, 0, 192 + 16 * g:192 + 16 * g + HIST], rows[0:HIST, 6 + g, :], ident[0:HIST, 0:HIST])
            for comp in range(2):
                for i in range(4):
                    mm = pe.transpose((bank_b[:, 2] if comp else aux[:, 1])[:, i * P:(i + 1) * P],
                                      c_raw[:, comp, i].rearrange("r a p -> r (a p)"), ident[:, :])
            mm.then_inc(prm_turned, 1)
            pe.wait_ge(x_lo_ready, TT)
            pe.wait_ge(xraw_ready, TT)
            for s in range(4):
                pe.wait_ge(lo_ready, s + 1)
                tile(s, bank_b if s % 2 else bank_a, s % 2, ALL, x_hi, x_lo)
                if s == 0:
                    pe.wait_ge(prm_used, 2)
                    rstd_rows(1, diag)
            pe.wait_ge(ca_ready, 1)
            pe.wait_ge(row_used, 1)
            for q in range(8):
                g2, a = q % 2, q // 2
                if q >= 2:
                    pe.wait_ge(k_evac, q - 1)
                for i in range(4):
                    for comp in range(2):
                        mm = pe.matmul(aux[0:H, q % 2, i * P:(i + 1) * P], BB[64 * g2:64 * g2 + 64, comp, 4 * a + i, :],
                                       CA[64 * g2:64 * g2 + 64, comp, 4 * a + i, 0:P], start=(comp == 0), stop=(comp == 1))
                mm.then_inc(k_turn, 1)
            pe.wait_ge(wt_ready, 1)
            pe.wait_ge(k_evac, 8)
            for r in range(8):
                if r >= 2:
                    pe.wait_ge(w_evac, r - 1)
                for i in range(4):
                    mm = pe.transpose(aux[:, r % 2, i * P:(i + 1) * P], WT[:, r // 4, 4 * (r % 4) + i, :], ident[:, :])
                mm.then_inc(w_turn, 1)
            pe.wait_ge(w_evac, 8)

            def pool_group(g):
                s0, t0 = 4 * g + S_POOL, 5 * g + T_POOL
                pe.wait_ge(lo_ready, s0 + 1)
                tile(t0, bank_a, 0, ALL, x_hi, x_lo)
                pe.wait_ge(lo_ready, s0 + 2)
                tile(t0 + 1, bank_b, 1, ALL, x_hi, x_lo)
                pe.wait_ge(lo_ready, s0 + 3)
                tile(t0 + 2, bank_a, 0, ALL, x_hi, x_lo)
                pe.wait_ge(lo_ready, s0 + 4)
                pe.wait_ge(pooled_lo, g + 1)
                hi, lo = pl_hi[:, :].unsqueeze(1), pl_lo[:, :].unsqueeze(1)
                tile(t0 + 3, bank_b, 1, [(0, 0)], hi, lo)
                pe.wait_ge(evac_done, t0 + 4)
                tile(t0 + 4, bank_b, 1, [(P, 0)], hi, lo)
                pe.transpose(aux[0:HIST, 0, 0:P], UP[:, SEQ:SEQ + HIST], ident[:, :])
                pe.transpose(aux[0:HIST, 0, P:2 * P], UP[:, T + HIST:T + 2 * HIST], ident[:, :]).then_inc(np_turned, 1)

            pool_group(0)
            pe.wait_ge(u_in, 16 * L)
            pe.wait_ge(np_evac, 1)
            for pr in range(PAIRS):
                if pr >= 2:
                    pe.wait_ge(v_evac, pr - 1)
                for comp in range(2):
                    for g2 in range(2):
                        mm = pe.matmul(aux[64 * g2:64 * g2 + 64, pr % 2, comp * NCG:(comp + 1) * NCG],
                                       W[:, comp, pr, 64 * g2:64 * g2 + 64], U[:, 2 * pr + g2, :], start=True, stop=True)
                mm.then_inc(v_turn, 1)
            pe.wait_ge(v_evac, PAIRS)
            with pe.Fori(1, 4) as g:
                pe.wait_ge(np_evac, g)
                pool_group(g)
            for r, banks in enumerate((bank_a, bank_b)):
                pe.wait_ge(lo_ready, S_GATE + 1 + r)
                tile(T_GATE + r, banks, r, ALL, x_hi, x_lo)
            pe.wait_ge(s_ready, 1)
            pe.wait_ge(to_in, 16 * L)
            pe.wait_ge(np_evac, 4)
            for r in range(12):
                g2, prs = r % 2, range(3 * (r // 2), min(3 * (r // 2) + 3, PAIRS))
                if r >= 2:
                    pe.wait_ge(y_evac, r - 1)
                for i, pr in enumerate(prs):
                    out = aux[:, g2, i * NCG:(i + 1) * NCG]
                    pe.matmul(out, TO[:, 2 * pr + g2, :], U[:, 2 * pr + g2, :], start=True, stop=False)
                    for comp in range(2):
                        mm = pe.matmul(out, CA[64 * g2:64 * g2 + 64, comp, pr, H:9 * H],
                                       S[64 * g2:64 * g2 + 64, comp, pr, 0:NCG], start=False, stop=(comp == 1))
                mm.then_inc(y_turn, 1)
            pe.wait_ge(y_evac, 12)
            for i, (comp, slot) in enumerate(((0, NCP), (1, NCP), (0, NCG), (1, NCG))):
                mm = pe.transpose(aux[0:PAIRS, 0, i * P:(i + 1) * P], S[:, comp, :, slot], ident[:, :])
            mm.then_inc(st_turn, 1)
            with pe.Fori(1, 4) as m:
                for r, banks in enumerate((bank_a, bank_b)):
                    pe.wait_ge(lo_ready, 2 * m + (S_GATE + 1 + r))
                    tile(2 * m + (T_GATE + r), banks, r, ALL, x_hi, x_lo)
            pe.wait_ge(y_lo_ready, KS)
            with pe.Fori(0, 4) as m:
                for r in range(2):
                    pe.wait_ge(lo_ready, 2 * m + (S_GLU + 1 + r))
                    tile(4 * m + (T_GLU + 2 * r), bank_a, r, [(k * P, k) for k in range(KS)], y_hi, y_lo)
                    tile(4 * m + (T_GLU + 2 * r + 1), bank_b, r, [((KS + k) * P, k) for k in range(KS)], y_hi, y_lo)

            def sum_squares(n):
                pe.wait_ge(sq_used, (KD - 1) * n)
                pe.matmul(aux[:, 0, 0:TT], ones[:, :], zeros[:, 0:TT], start=True, stop=False, skip_group_check=True)
                for tt in range(TT):
                    mm = pe.matmul(aux[0:tok(tt), 0, tt:tt + 1], sq_sum[:, tt * P:tt * P + tok(tt)], ones[:, 0:1],
                                   start=False, stop=False, skip_group_check=True)
                mm.then_inc(ss_turned, 1)

            pe.wait_ge(st_evac, 1)
            pe.wait_ge(lo_ready, S_OUT + 1)
            tile(T_OUT, bank_a, 0, ALL, x_hi, x_lo, ready=m_lo_ready)
            with pe.Fori(0, 3) as i:
                for r, banks in ((1, bank_b), (0, bank_a)):
                    n = 2 * i + 2 - r
                    pe.wait_ge(lo_ready, n + (S_OUT + 1))
                    tile(n + T_OUT, banks, r, ALL, x_hi, x_lo)
            pe.wait_ge(lo_ready, S_OUT + 8)
            tile(T_OUT + 7, bank_b, 1, ALL, x_hi, x_lo)
            pe.wait_ge(lo_ready, S_FFN + 1)
            tile(T_FFN, bank_a, 0, ALL, hg_hi, hg_lo, ready=hg_lo_ready)
            sum_squares(1)
            pe.wait_ge(lo_ready, S_FFN + 2)
            tile(T_FFN + 1, bank_b, 1, ALL, hg_hi, hg_lo)
            rstd_rows(2, diag2)
            for r, banks in enumerate((bank_a, bank_b)):
                pe.wait_ge(lo_ready, S_FFN + 3 + r)
                tile(T_FFN + 2 + r, banks, r, ALL, hg_hi, hg_lo)

            def down(t0, s0, n):
                if n % 4 == 0:
                    pe.wait_ge(lo_ready, s0 + 1 + n // 4)
                col = (n % 4) * P
                tile(t0 + n, bank_b if n % 2 else bank_a, n // 4, [(col, 0), (4 * P + col, 1)], f_hi, f_lo)

            with pe.Fori(1, FCH) as c:
                s0, t0 = 6 * c + (S_LOOP - 6), 12 * c + (T_LOOP - 12)
                for r, banks in enumerate((bank_a, bank_b)):
                    pe.wait_ge(lo_ready, s0 + 1 + r)
                    tile(t0 + r, banks, r, ALL, hg_hi, hg_lo)
                pe.wait_ge(f_lo_ready, 2 * c)
                for n in range(KD):
                    down(t0 + 2, s0 + 2, n)
                for r, banks in enumerate((bank_a, bank_b)):
                    pe.wait_ge(lo_ready, s0 + 5 + r)
                    tile(t0 + 10 + r, banks, r, ALL, hg_hi, hg_lo)
            pe.wait_ge(f_lo_ready, 2 * FCH)
            for n in range(KD):
                down(T_LAST, S_LAST, n)
            sum_squares(2)
            pe.wait_ge(hf_ready, KD)
            pe.wait_ge(evac_done, T_LAST + KD)
            for tt in range(TT):
                if tt >= 2:
                    pe.wait_ge(tok_used[tt % 2], tt // 2)
                banks = bank_b if tt % 2 else bank_a
                for k in range(KD):
                    mm = pe.transpose(banks[0:tok(tt), k // 4, (k % 4) * P:(k % 4 + 1) * P],
                                      hf[:, k, tt * P:tt * P + tok(tt)], ident[:, :])
                mm.then_inc(tok_turned, 1)

        @block.scalar
        def _(act):
            def split(s, slot, landed, done, cols=SLAB):
                act.wait_ge(stage_in[slot], landed)
                if done is not None:
                    act.wait_ge(tile_done, done)
                act.activation(w_hi[:, slot, 0:cols], stage[:, slot, 0:cols], ACT.Copy).then_inc(hi_ready, 1)

            def landed(s):
                return 16 * (s // 2 + 1) + (64 if s >= S_OUT else 16 * ((s - S_GLU) // 2 + 1) if s >= S_GLU else 0)

            for dst, src in ((rows[0:8, 5, :], t_in["g_mix"][0]), (rows[8:16, 5, :], t_in["g_ffn"][0]),
                             (rows[16:24, 5, :], t_in["g_final"]), (rows[24:32, 5, :], t_in["pool_scale"][0])):
                act.dma_start(dst, src.rearrange("(k p) -> k p", p=P)).then_inc(gains_in, 16)
            act.wait_ge(ones_ready, 1)
            for tt in range(TT + 1):
                if tt < TT:
                    act.wait_ge(x_in[tt % X_SLOTS], 16 * (tt // X_SLOTS + 1))
                    if tt:
                        act.wait_ge(x_squared, tt)
                    act.activation(x_sq[0:tok(tt), :], x_t[0:tok(tt), tt % X_SLOTS, :], ACT.Square,
                                   accum_out=ss[0:tok(tt), 0, tt:tt + 1]).then_inc(x_squared, 1)
                if tt:
                    u = tt - 1
                    act.wait_ge(xg_ready, tt)
                    act.activation(x_hi[:, :, u * P:u * P + tok(u)],
                                   xg[:, u % XG_SLOTS, :].rearrange("p (k t) -> p k t", k=KD)[:, :, 0:tok(u)],
                                   ACT.Copy).then_inc(x_hi_ready, 1)
                if tt in (5, 7):
                    s = (tt - 5) // 2
                    split(s, s, landed(s), None)

            def root(n):
                act.wait_ge(ms_ready, n)
                act.activation(ss[:, 1, :], ss[:, 0, :], ACT.Sqrt).then_inc(root_ready, 1)

            root(1)
            act.wait_ge(angle_ready, 1)
            act.activation(pt[:, 8:10, :], pt[:, 6:8, :], ACT.Sin).then_inc(sine_ready, 1)
            for s in range(2, 6):
                split(s, s % 2, landed(s), s - 1)
            act.wait_ge(x_lo_ready, TT)
            for q in range(8):
                g2, a = q % 2, q // 2
                act.wait_ge(k_turn, q + 1)
                act.activation(K_sb[:, 8 * a + g2:8 * a + 8:2, :], aux[0:H, q % 2, :].rearrange("h (i c) -> h i c", i=4),
                               ACT.Copy).then_inc(k_evac, 1)
            for r in range(8):
                act.wait_ge(w_turn, r + 1)
                act.activation(W[:, r // 4, 4 * (r % 4):4 * (r % 4) + 4, :],
                               aux[:, r % 2, :].rearrange("p (i c) -> p i c", i=4), ACT.Copy).then_inc(w_evac, 1)
            for g in range(4):
                s0, t0 = 4 * g + S_POOL, 5 * g + T_POOL
                split(s0 + 2, 0, landed(s0 + 2), t0 + 1)
                act.wait_ge(pooled_ready, g + 1)
                act.activation(pl_hi[:, :], (sum_b if g % 2 == 0 else sum_a)[:, 0:T], ACT.Copy).then_inc(pooled_hi, 1)
                for r in range(2):
                    split(s0 + 3 + r, 1 - r, landed(s0 + 3 + r), t0 + 2 + r, cols=(2 * P, SLAB)[r])
                    act.wait_ge(evac_done, t0 + 2 + r)
                    act.activation(gate_t[:, r, :], gate_t[:, r, :], ACT.Sigmoid).then_inc(gp_sig, 1)
                split(s0 + 5, 1, landed(s0 + 5), t0 + 5)
                act.wait_ge(np_turned, g + 1)
                act.activation(new_pool[:, :, g * P:(g + 1) * P], aux[0:HIST, 0, 0:2 * P].rearrange("i (a c) -> i a c", a=2),
                               ACT.Copy).then_inc(np_evac, 1)
                if g == 0:
                    act.wait_ge(wt_ready, 1)
                    for pr in range(PAIRS):
                        act.wait_ge(v_turn, pr + 1)
                        act.activation(S[:, :, pr, 1:NCG + 1], aux[:, pr % 2, 0:2 * NCG].rearrange("p (a c) -> p a c", a=2),
                                       ACT.Copy).then_inc(v_evac, 1)

            def gate(n):
                split(S_GATE + n + 2, n % 2, landed(S_GATE + n + 2), T_GATE + n + 1)
                act.wait_ge(evac_done, T_GATE + n + 1)
                g_at = gate_at(n)
                act.activation(g_at, g_at, ACT.Sigmoid).then_inc(gs_sig, 1)

            gate(0)
            gate(1)
            for r in range(12):
                g2, n = r % 2, min(3, PAIRS - 3 * (r // 2))
                act.wait_ge(y_turn, r + 1)
                act.activation(U[:, 6 * (r // 2) + g2:6 * (r // 2) + 2 * n:2, :],
                               aux[:, g2, 0:n * NCG].rearrange("p (i c) -> p i c", i=n), ACT.Copy).then_inc(y_evac, 1)
            act.wait_ge(st_turn, 1)
            act.activation(out_state[:, :, :], aux[0:PAIRS, 0, :].rearrange("q (i c) -> q i c", i=4), ACT.Copy).then_inc(st_evac, 1)

            def gelu(n):
                act.wait_ge(yt_in[n], 16)
                if n:
                    act.wait_ge(y_val, n)
                act.activation(ge_a[:, :], YT[:, n].rearrange("p j c -> p (j c)"), ACT.Square).then_inc(y_sq, 1)
                act.wait_ge(y_arg, n + 1)
                act.activation(ge_b[:, :], ge_a[:, :], ACT.Sigmoid, scale=GELU_C).then_inc(y_sig, 1)
                act.wait_ge(y_val, n + 1)
                act.activation(y_hi[:, n, :], ge_c[:, :], ACT.Copy).then_inc(y_hi_ready, 1)

            def glu(n, r, count):
                act.wait_ge(tile_done, n * 2 + (T_GLU + 2))
                act.activation(b3(glu_b[:, :]), B3, ACT.Sigmoid).then_inc(b_sig, 1)
                split(n + (S_GLU + 2), r, count, None)
                act.wait_ge(merged_ready, n + 1)
                act.activation(at_tile(x_hi, n), at_tile(merged, n), ACT.Copy).then_inc(m_hi_ready, 1)

            gate(2)
            gate(3)
            for n in range(KS):
                gelu(n)
                gate(n + 4)
            with act.Fori(0, 3) as m:
                for r in range(2):
                    glu(2 * m + r, r, 32 * m + (landed(S_GLU) + 32))
            for n in (6, 7):
                glu(n, n % 2, landed(S_OUT + n - 6))

            def squares(n, i0, src):
                if n >= 3:
                    act.wait_ge(sq_used, i0 + n - 2)
                act.activation(sq[:, n % 2, :] if n else sq_sum[:, :], src, ACT.Square).then_inc(sq_ready, 1)

            for n in range(KD):
                split(S_OUT + n + 2, n % 2, landed(S_OUT + n + 2), T_OUT + n + 1)
                act.wait_ge(evac_done, T_OUT + n + 1)
                act.activation(hg_hi[:, n, :], hT[:, n, :], ACT.Copy, scale=gains[:, 1, n:n + 1]).then_inc(hg_hi_ready, 1)
                squares(n, 0, hT[:, n, :])

            def sig_f(t_gate):
                act.wait_ge(evac_done, t_gate + 1)
                act.activation(f_s[:, :], f_g[:, :], ACT.Sigmoid).then_inc(fs_ready, 1)

            def hi_f(r, count):
                act.wait_ge(fh_ready, count)
                act.activation(f_hi[:, r, :], f_h[:, :], ACT.Copy).then_inc(f_hi_ready, 1)

            split(S_FFN + 2, 0, landed(S_FFN + 2), T_FFN + 1)
            root(2)
            split(S_FFN + 3, 1, landed(S_FFN + 3), T_FFN + 2)
            sig_f(T_FFN)
            split(S_FFN + 4, 0, landed(S_FFN + 4), T_FFN + 3)
            hi_f(0, 1)
            sig_f(T_FFN + 2)
            split(S_FFN + 5, 1, landed(S_FFN + 5), T_FFN + 4)
            hi_f(1, 2)
            with act.Fori(1, FCH) as c:
                s0, t0 = 6 * c + (S_LOOP - 6), 12 * c + (T_LOOP - 12)
                l0 = 48 * c + (landed(S_LOOP) - 48)
                split(s0 + 2, 0, l0 + 16, t0 + 1)
                sig_f(t0)
                split(s0 + 3, 1, l0 + 16, t0 + 2)
                split(s0 + 4, 0, l0 + 32, t0 + 6)
                split(s0 + 5, 1, l0 + 32, t0 + 10)
                hi_f(0, 2 * c + 1)
                split(s0 + 6, 0, l0 + 48, t0 + 11)
                sig_f(t0 + 10)
                split(s0 + 7, 1, l0 + 48, t0 + 12)
                hi_f(1, 2 * c + 2)
            for n in range(KD):
                act.wait_ge(evac_done, T_LAST + n + 1)
                squares(n, KD - 1, hT[:, n, :])
                act.activation(hf[:, n, :], hT[:, n, :], ACT.Copy, scale=gains[:, 2, n:n + 1]).then_inc(hf_ready, 1)
            root(3)
            act.wait_ge(diag_ready, 3)
            for tt in range(1, TT, 2):
                act.wait_ge(tok_turned, tt + 1)
                if tt >= 4:
                    act.wait_ge(y_stored[tt % 4], 16 * (tt // 4))
                act.activation(y_out[0:tok(tt), tt % 4, :], bank_b[0:tok(tt), 0:2, :].rearrange("p b c -> p (b c)"), ACT.Copy,
                               scale=ss[0:tok(tt), 2, tt:tt + 1]).then_inc(tok_used[1], 1)

        @block.gpsimd
        def _(pool):
            def lo(s, slot, cols=SLAB):
                pool.wait_ge(hi_ready, s + 1)
                pool.tensor_tensor(w_lo[:, slot, 0:cols], stage[:, slot, 0:cols], w_hi[:, slot, 0:cols],
                                   ALU.subtract).then_inc(lo_ready, 1)

            for tt in range(TT):
                pool.wait_ge(x_hi_ready, tt + 1)
                cut = slice(tt * P, tt * P + tok(tt))
                pool.tensor_tensor(x_lo[:, :, cut], xg[:, tt % XG_SLOTS, :].rearrange("p (k t) -> p k t", k=KD)[:, :, 0:tok(tt)],
                                   x_hi[:, :, cut], ALU.subtract).then_inc(x_lo_ready, 1)
                if tt in (4, 6):
                    lo((tt - 4) // 2, (tt - 4) // 2)
            for s in range(2, 5):
                lo(s, s % 2)
            pool.wait_ge(wt_ready, 1)
            pool.memset(TO[:, :, :], 0.0).then_inc(to_zero, 1)
            for s in range(5, S_GATE):
                lo(s, s % 2, 2 * P if s % 4 == 3 else SLAB)
            with pool.Fori(0, (S_OUT + 2 - S_GATE) // 2) as i:
                for r in range(2):
                    lo(2 * i + (S_GATE + r), r)
            for n in range(KD):
                lo(S_OUT + n + 2, n % 2)
                if n:
                    pool.wait_ge(sq_ready, n + 1)
                    if n >= 2:
                        pool.wait_ge(sq_used, n - 1)
                    pool.tensor_tensor(sq_sum[:, :], sq_sum[:, :], sq[:, n % 2, :], ALU.add).then_inc(sq_used, 1)
            with pool.Fori(0, (S_LAST - S_FFN) // 2) as i:
                for r in range(2):
                    lo(2 * i + (S_FFN + 2 + r), r)

        @block.vector
        def _(dve):
            steps = [0]

            def then(ins):
                steps[0] += 1
                ins.then_inc(dve_step, 1)
                dve.wait_ge(dve_step, steps[0])

            def tt_(out, a, b, op):
                return dve.tensor_tensor(out, a, b, op)

            MUL, ADD, SUB = ALU.mult, ALU.add, ALU.subtract
            dve.memset(zeros[:, :], 0.0)
            dve.memset(ss[:, :, :], 1.0)
            dve.memset(ones[:, :], 1.0).then_inc(ones_ready, 1)
            dve.wait_ge(prm_turned, 1)
            dve.tensor_copy(gains[:, :, :], aux[:, 0, 0:32].rearrange("p (v k) -> p v k", v=4)).then_inc(prm_used, 1)
            dve.wait_ge(prm_used, 1)
            for tt in range(TT):
                dve.wait_ge(x_turned, tt + 1)
                if tt >= XG_SLOTS:
                    dve.wait_ge(x_lo_ready, tt - XG_SLOTS + 1)
                if tt >= 2:
                    dve.wait_ge(xraw_out[tt % 2], 16 * (tt // 2))
                turned = (bank_b if tt % 2 else bank_a)[:, 0:2, :].rearrange("p b (k t) -> p (b k) t", t=P)[:, :, 0:tok(tt)]

                def cut(buf, slots):
                    return buf[:, tt % slots, :].rearrange("p (k t) -> p k t", k=KD)[:, :, 0:tok(tt)]
                tt_(cut(xg, XG_SLOTS), turned, gains[:, 0, :].unsqueeze(2).to_broadcast([P, KD, tok(tt)]), MUL).then_inc(xg_ready, 1)
                dve.tensor_copy(cut(x_raw, 2), turned).then_inc(xraw_ready, 1)

            def inverse_root(n, mean_in, scaled):
                dve.tensor_scalar(ss[:, 0, :], mean_in, 1.0 / D, EPS, MUL, ADD).then_inc(ms_ready, 1)
                dve.wait_ge(root_ready, n)
                then(dve.reciprocal(ss[:, 2, :], ss[:, 1, :]))
                then(tt_(ss[:, 3, :], ss[:, 2, :], ss[:, 2, :], MUL))
                then(tt_(ss[:, 3, :], ss[:, 3, :], ss[:, 0, :], MUL))
                then(dve.tensor_scalar(ss[:, 3, :], ss[:, 3, :], -0.5, 1.5, MUL, ADD))
                if scaled is None:
                    tt_(ss[:, 2, :], ss[:, 2, :], ss[:, 3, :], MUL).then_inc(diag_ready, 1)
                    return
                then(tt_(ss[:, 2, :], ss[:, 2, :], ss[:, 3, :], MUL))
                tt_(scaled[:, :, :], ident[:, :].unsqueeze(1).to_broadcast([P, TT, P]),
                    ss[:, 2, :].unsqueeze(2).to_broadcast([P, TT, P]), MUL).then_inc(diag_ready, 1)

            def take_rows(n):
                dve.wait_ge(row_ready, n)
                dve.tensor_copy(rstd_row[:, 0:SEQ], aux[:, :, :].rearrange("p b c -> p (b c)"))
                dve.tensor_copy(rstd_row[:, SEQ:T], bank_a[:, 2, 384:384 + DEC]).then_inc(row_used, 1)
                dve.wait_ge(row_used, n)

            dve.wait_ge(prm_in, 16 * PRM_LOADS)
            dve.tensor_copy(rows[0:16, 4, :].rearrange("q (g p) -> q g p", g=2),
                            log_dt[:, :].unsqueeze(2).to_broadcast([16, 2, NS])).then_inc(rows_ready, 1)
            dve.wait_ge(x_squared, TT)
            inverse_root(1, ss[:, 0, :], diag)
            dve.wait_ge(prm_turned, 2)
            dve.tensor_copy(prm[:, :, :], aux[:, 0, 0:80].rearrange("p (i q) -> p i q", i=5))
            dve.tensor_copy(state0[:, :, :], aux[:, 0, 32:64].rearrange("p (a q) -> p a q", a=2))
            dve.tensor_copy(pool_hist[:, :, :], aux[:, 0, 192:256].rearrange("p (g i) -> p g i", g=4)[:, :, 0:HIST])
            for comp, turned in enumerate((aux[:, 1], bank_b[:, 2])):
                by_group = turned.rearrange("p (q g h) -> p g q h", g=2, h=H)
                for g2 in range(2):
                    half = slice(64 * g2, 64 * g2 + 64)
                    ins = dve.tensor_copy(CT[half, comp], by_group[half, g2])
            ins.then_inc(prm_used, 1)
            dve.wait_ge(prm_used, 2)

            q = [pt[:, i, :] for i in range(30)]

            def exp_of(out, x, k, r, p):
                then(dve.tensor_scalar(x, x, -87.0, 88.0, ALU.max, ALU.min))
                then(dve.tensor_scalar(k, x, 1.4426950408889634, None, MUL))
                then(dve.tensor_scalar(k, k, MAGIC, None, ADD))
                then(dve.tensor_scalar(k, k, MAGIC, None, SUB))
                then(dve.scalar_tensor_tensor(r, k, -LN2[0], x, MUL, ADD))
                then(dve.scalar_tensor_tensor(r, k, -LN2[1], r, MUL, ADD))
                then(dve.tensor_scalar(p, r, EXP_POLY[0], None, MUL))
                for coef in EXP_POLY[1:]:
                    then(dve.scalar_tensor_tensor(p, p, coef, r, ADD, MUL))
                then(dve.tensor_scalar(r.bitcast(I32), k, 127.0, 8388608.0, ADD, MUL))
                then(dve.scalar_tensor_tensor(out, p, 1.0, r, ADD, MUL))

            def cmul(re, im, ar, ai, br, bi, t1, t2):
                tt_(t1, ar, br, MUL)
                then(tt_(t2, ai, bi, MUL))
                then(tt_(re, t1, t2, SUB))
                tt_(t1, ar, bi, MUL)
                then(tt_(t2, ai, br, MUL))
                then(tt_(im, t1, t2, ADD))

            lam, om, dt, e = q[0], prm[:, 1, :], q[1], q[2]
            then(dve.tensor_copy(q[3], prm[:, 4, :]))
            exp_of(dt, q[3], q[4], q[5], q[10])
            then(dve.tensor_scalar(lam, prm[:, 0, :], -1e-4, None, ALU.min))
            then(tt_(q[3], lam, dt, MUL))
            exp_of(e, q[3], q[4], q[5], q[10])
            then(tt_(q[3], om, dt, MUL))
            then(dve.tensor_scalar(q[4], q[3], 0.15915494309189535, None, MUL))
            then(dve.tensor_scalar(q[4], q[4], MAGIC, None, ADD))
            then(dve.tensor_scalar(q[4], q[4], MAGIC, None, SUB))
            for part in TWO_PI:
                then(dve.scalar_tensor_tensor(q[3], q[4], -part, q[3], MUL, ADD))
            then(dve.tensor_scalar(q[6], q[3], 3.1415925, -3.1415925, ALU.min, ALU.max))
            then(dve.tensor_scalar(q[7], q[6], -1.0, None, MUL))
            then(tt_(q[7], q[6], q[7], ALU.max))
            dve.tensor_scalar(q[7], q[7], -1.0, 1.5707963267948966, MUL, ADD).then_inc(angle_ready, 1)
            take_rows(1)
            dve.wait_ge(sine_ready, 1)
            then(dve.memset(PW[:, 1, 0, :], 0.0))
            then(dve.memset(PW[:, 0, 0, :], 1.0))
            ar, ai = PW[:, 0, 1, :], PW[:, 1, 1, :]
            then(tt_(ar, e, q[9], MUL))
            then(tt_(ai, e, q[8], MUL))
            then(tt_(q[10], lam, lam, MUL))
            then(tt_(q[11], om, om, MUL))
            then(tt_(q[10], q[10], q[11], ADD))
            then(dve.reciprocal(q[11], q[10]))
            then(dve.tensor_scalar(q[12], ar, -1.0, None, ADD))
            then(tt_(q[13], q[12], lam, MUL))
            then(tt_(q[14], ai, om, MUL))
            then(tt_(q[13], q[13], q[14], ADD))
            then(tt_(q[13], q[13], q[11], MUL))
            then(tt_(q[14], ai, lam, MUL))
            then(tt_(q[15], q[12], om, MUL))
            then(tt_(q[14], q[14], q[15], SUB))
            then(tt_(q[14], q[14], q[11], MUL))

            def bc_h(ap):
                return ap.unsqueeze(2).to_broadcast([P, PAIRS, H])
            dve.wait_ge(xraw_out[0], 16 * 5)
            dve.wait_ge(xraw_out[1], 16 * 4)
            t1, t2 = [t[:, 0:PAIRS * H].rearrange("p (q h) -> p q h", h=H) for t in (tmp_a, tmp_b)]
            cmul(BB[:, 0], BB[:, 1], bc_h(q[13]), bc_h(q[14]), b_raw[:, 0], b_raw[:, 1], t1, t2)

            def powers(tab, n, t1, t2):
                k = 1
                while k < n:
                    last = [tab[:, c, k - 1, :].unsqueeze(1).to_broadcast([P, k, PAIRS]) for c in range(2)]
                    cmul(tab[:, 0, k:2 * k, :], tab[:, 1, k:2 * k, :], tab[:, 0, 0:k, :], tab[:, 1, 0:k, :],
                         last[0], last[1], t1[:, 0:k, :], t2[:, 0:k, :])
                    k *= 2
            tp1, tp2 = [t[:, 0:8 * PAIRS].rearrange("p (k q) -> p k q", q=PAIRS) for t in (tmp_a, tmp_b)]
            powers(PW[:, :, 1:L + 1, :], L, tp1, tp2)
            then(dve.tensor_copy(a8pow[:, :, 0, :], PW[:, :, L, :]))
            powers(a8pow, STEPS, tp1, tp2)
            then(dve.tensor_scalar(neg_a[:, 0, :], a8pow[:, 1, 0, :], -1.0, None, MUL))
            then(dve.tensor_scalar(neg_a[:, 1, :], a8pow[:, 1, STEPS - 1, :], -1.0, None, MUL))

            def take_u(n):
                dve.wait_ge(tile_done, n + 1)
                banks = bank_b if n % 2 else bank_a
                for b0, nb, c0, nch, to in ((0, 2, 0, 44, 0), (2, 1, 88, 40, 88), (2, 1, 128, 4, NCP + 1)):
                    o = UT[:, n, :, to:to + nb * nch].rearrange("p j (b c) -> p b c j", b=nb)
                    off = 0 if c0 != 128 else 40 * L
                    i0 = banks[:, b0:b0 + nb, off:off + nch * L].rearrange("p b (c j) -> p b c j", j=L)
                    i1 = rstd_row[:, c0 * L:(c0 + nb * nch) * L].rearrange("p (b c j) -> p b c j", b=nb, j=L)
                    ins = tt_(o, i0, i1, MUL)
                ins.then_inc(evac_done, 1)

            dve.wait_ge(row_used, 1)
            take_u(0)
            big = [P, PAIRS, L + 1, H]

            def big_of(t):
                return t[:, 0:PAIRS * 9 * H].rearrange("p (q k h) -> p q k h", q=PAIRS, h=H)
            pw = [PW[:, c].rearrange("p k q -> p q k").unsqueeze(3).to_broadcast(big) for c in range(2)]
            ct = [CT[:, c].unsqueeze(2).to_broadcast(big) for c in range(2)]
            ca = [CA[:, c].rearrange("p q (k h) -> p q k h", h=H) for c in range(2)]
            tt_(big_of(tmp_a), ct[0], pw[0], MUL)
            then(tt_(big_of(tmp_b), ct[1], pw[1], MUL))
            then(tt_(ca[0], big_of(tmp_a), big_of(tmp_b), SUB))
            tt_(big_of(tmp_a), ct[0], pw[1], MUL)
            then(tt_(big_of(tmp_b), ct[1], pw[0], MUL))
            dve.scalar_tensor_tensor(CA[:, 1].rearrange("p q c -> p (q c)"), tmp_a[:, :], -1.0, tmp_b[:, :], MUL,
                                     SUB).then_inc(ca_ready, 1)
            take_u(1)
            mid = [P, PAIRS, L, H]

            def mid_of(t):
                return t[:, 0:PAIRS * L * H].rearrange("p (q k h) -> p q k h", q=PAIRS, h=H)
            pw = [PW[:, c, 0:L, :].rearrange("p k q -> p q k").unsqueeze(3).to_broadcast(mid) for c in range(2)]
            bb = [BB[:, c].unsqueeze(2).to_broadcast(mid) for c in range(2)]
            wt = [WT[:, c].rearrange("p q (k h) -> p q k h", h=H) for c in range(2)]
            dve.wait_ge(ca_ready, 1)
            tt_(mid_of(tmp_a), bb[0], pw[0], MUL)
            then(tt_(mid_of(tmp_b), bb[1], pw[1], MUL))
            then(tt_(wt[0], mid_of(tmp_a), mid_of(tmp_b), SUB))
            take_u(2)
            tt_(mid_of(tmp_a), bb[0], pw[1], MUL)
            then(tt_(mid_of(tmp_b), bb[1], pw[0], MUL))
            tt_(wt[1], mid_of(tmp_a), mid_of(tmp_b), ADD).then_inc(wt_ready, 1)
            then(dve.memset(UT[:, :, :, NCP:NCP + 1], 0.0))
            take_u(3)
            dve.wait_ge(k_evac, 8)
            lag0 = K_sb[:, :, 0:H]
            skip = skip_k[:, :].rearrange("h (g c) -> h g c", g=G)
            then(tt_(skip, ident[0:H, 0:H].unsqueeze(1).to_broadcast([H, G, H]),
                     d_skip[:, :].unsqueeze(2).to_broadcast([H, G, H]), MUL))
            tt_(lag0, lag0, skip, ADD).then_inc(k_ready, 1)

            re, im = S[:, 0], S[:, 1]

            def advance(cur, prev, shape, a_re, a_im, a_neg):
                n = int(np.prod(shape[1:]))
                u1 = [sc_a[:, c * n:(c + 1) * n] for c in range(2)]
                u2 = [sc_b[:, c * n:(c + 1) * n] for c in range(2)]

                def f(ap):
                    return ap if len(shape) == 2 else ap.rearrange("p (q s) -> p q s", q=PAIRS)

                def bc(ap):
                    return ap if len(shape) == 2 else ap.unsqueeze(2).to_broadcast(shape)
                tt_(f(u1[0]), prev[0], bc(a_re), MUL)
                tt_(f(u1[1]), prev[1], bc(a_re), MUL)
                tt_(f(u2[0]), prev[1], bc(a_neg), MUL)
                then(tt_(f(u2[1]), prev[0], bc(a_im), MUL))
                then(tt_(sc_a[:, 0:2 * n], sc_a[:, 0:2 * n], sc_b[:, 0:2 * n], ADD))
                tt_(cur[0], cur[0], f(u1[0]), ADD)
                then(tt_(cur[1], cur[1], f(u1[1]), ADD))

            seg = [x[:, :, 1:NCP + 1].rearrange("p q (s i) -> p q s i", i=STEPS) for x in (re, im)]

            def scan_steps(i0, i1):
                for i in range(i0, i1):
                    advance([x[:, :, :, i] for x in seg], [x[:, :, :, i - 1] for x in seg], [P, PAIRS, SEG],
                            a8pow[:, 0, 0, :], a8pow[:, 1, 0, :], neg_a[:, 0, :])

            def scan_ends():
                for s in range(1, SEG):
                    advance([x[:, :, s, STEPS - 1] for x in seg], [x[:, :, s - 1, STEPS - 1] for x in seg], [P, PAIRS],
                            a8pow[:, 0, STEPS - 1, :], a8pow[:, 1, STEPS - 1, :], neg_a[:, 1, :])

            def scan_sample():
                for k in range(NCP + 2, SLOTS):
                    advance([x[:, :, k] for x in (re, im)], [x[:, :, k - 1] for x in (re, im)], [P, PAIRS],
                            a8pow[:, 0, 0, :], a8pow[:, 1, 0, :], neg_a[:, 0, :])

            def scan_fill(c, done=None):
                for q0 in range(0, PAIRS, 8):
                    shape = [P, 8, SEG - 1, STEPS - 1]
                    n = 8 * (SEG - 1) * (STEPS - 1)
                    end = [x[:, q0:q0 + 8, 0:SEG - 1, STEPS - 1].unsqueeze(3).to_broadcast(shape) for x in seg]
                    apw = [a8pow[:, k, 0:STEPS - 1, q0:q0 + 8].rearrange("p i q -> p q i").unsqueeze(2).to_broadcast(shape)
                           for k in range(2)]
                    u1 = sc_a[:, 0:n].rearrange("p (q s i) -> p q s i", q=8, s=SEG - 1)
                    u2 = sc_b[:, 0:n].rearrange("p (q s i) -> p q s i", q=8, s=SEG - 1)
                    dst = seg[c][:, q0:q0 + 8, 1:SEG, 0:STEPS - 1]
                    tt_(u1, end[0], apw[c], MUL)
                    then(tt_(u2, end[1], apw[1 - c], MUL))
                    then(tt_(sc_a[:, 0:n], sc_a[:, 0:n], sc_b[:, 0:n], SUB if c == 0 else ADD))
                    if q0 and done is not None:
                        tt_(dst, dst, u1, ADD).then_inc(done, 1)
                    else:
                        then(tt_(dst, dst, u1, ADD))

            def scan_start():
                dve.wait_ge(v_evac, PAIRS)
                then(dve.memset(S[:, :, :, 0:1], 0.0))
                then(dve.tensor_copy(S[:, :, :, NCP + 1], state0[:, :, :]))

            dve.wait_ge(ut_out, 16)
            then(dve.memset(UP[:, 0:HIST], 0.0))
            for g in range(4):
                t0 = 5 * g + T_POOL
                if g:
                    dve.wait_ge(np_turned, g)
                then(dve.tensor_copy(UP[:, HIST + SEQ:2 * HIST + SEQ], pool_hist[:, g, :]))
                dve.wait_ge(tile_done, t0 + 1)
                tt_(UP[:, HIST:HIST + 2 * BLK].rearrange("p (b t) -> p b t", b=2), A3[:, 0:2],
                    rstd_row[:, 0:2 * BLK].rearrange("p (b t) -> p b t", b=2), MUL)
                tt_(UP[:, HIST + 2 * BLK:HIST + SEQ], bank_a[:, 2, 0:BLK - DEC], rstd_row[:, 2 * BLK:SEQ], MUL)
                tt_(UP[:, 2 * HIST + SEQ:], bank_a[:, 2, BLK - DEC:BLK], rstd_row[:, SEQ:], MUL).then_inc(evac_done, 1)
                dve.wait_ge(evac_done, t0 + 1)
                src, dst = UP, sum_a
                for k in range(g + 1):
                    sh = 1 << k
                    lo_i = 2 * sh - 1
                    then(tt_(dst[:, lo_i:], src[:, lo_i:], src[:, lo_i - sh:T + 2 * HIST - sh], ADD))
                    src, dst = dst, (sum_b if dst is sum_a else sum_a)
                w = WINDOWS[g]
                dve.scalar_tensor_tensor(dst[:, 0:SEQ], src[:, HIST:HIST + SEQ], 1.0 / w, UP[:, HIST:HIST + SEQ], MUL, SUB)
                dve.scalar_tensor_tensor(dst[:, SEQ:T], src[:, 2 * HIST + SEQ:], 1.0 / w, UP[:, 2 * HIST + SEQ:], MUL, SUB)
                then(tt_(head[:, :], src[:, HIST:HIST + 16], inv_count[:, g, :], MUL))
                tt_(dst[:, 0:16], head[:, :], UP[:, HIST:HIST + 16], SUB).then_inc(pooled_ready, 1)
                dve.wait_ge(pooled_hi, g + 1)
                tt_(pl_lo[:, :], dst[:, 0:T], pl_hi[:, :], SUB).then_inc(pooled_lo, 1)
                if g == 3:
                    scan_ends()
                for r, banks in enumerate((B3, A3)):
                    dve.wait_ge(tile_done, t0 + 2 + r)
                    if g:
                        dve.wait_ge(mp_out[r], 16 * g)
                    tt_(b3(gate_t[:, r, :]), banks, b3(rstd_row[:, :]), MUL).then_inc(evac_done, 1)
                    if r == 0 and g:
                        if g == 1:
                            scan_start()
                        if g < 3:
                            scan_steps(*((1, 5), (9, 13))[g - 1])
                        else:
                            scan_sample()
                for r in range(2):
                    dve.wait_ge(gp_sig, 2 * g + r + 1)
                    dve.wait_ge(tile_done, t0 + 4 + r)
                    dve.scalar_tensor_tensor(b3(gate_t[:, r, :]), B3, gains[:, 3, 2 * g + r:2 * g + r + 1],
                                             b3(gate_t[:, r, :]), MUL, MUL).then_inc(evac_done, 1)
                if g in (1, 2):
                    scan_steps(*((5, 9), (13, STEPS))[g - 1])
            scan_fill(0)
            scan_fill(1, done=s_ready)

            def gelu(n):
                y = YT[:, n].rearrange("p j c -> p (j c)")
                dve.wait_ge(y_sq, n + 1)
                then(dve.tensor_scalar(ge_a[:, :], ge_a[:, :], 0.044715, 1.0, MUL, ADD))
                tt_(ge_a[:, :], ge_a[:, :], y, MUL).then_inc(y_arg, 1)
                dve.wait_ge(y_sig, n + 1)
                if n:
                    dve.wait_ge(y_hi_ready, n)
                s = ge_b[:, :].rearrange("p (j c) -> p j c", c=NCG)
                tt_(ge_c[:, 0:SEQ].rearrange("p (c j) -> p j c", j=L), YT[:, n, :, 0:NCP], s[:, :, 0:NCP], MUL)
                tt_(ge_c[:, SEQ:T].rearrange("p (c j) -> p j c", j=L), YT[:, n, :, NCP + 1:], s[:, :, NCP + 1:],
                    MUL).then_inc(y_val, 1)
                dve.wait_ge(y_hi_ready, n + 1)
                tt_(y_lo[:, n, :], ge_c[:, :], y_hi[:, n, :], SUB).then_inc(y_lo_ready, 1)

            def gate(n):
                dve.wait_ge(tile_done, T_GATE + n + 1)
                tt_(b3(gate_at(n)), B3 if n % 2 else A3, b3(rstd_row[:, :]), MUL).then_inc(evac_done, 1)

            def merge(n, m, r):
                dve.wait_ge(tile_done, n * 2 + (T_GLU + 1))
                if not (isinstance(n, int) and n == 0):
                    dve.wait_ge(merged_ready, n)
                tt_(b3(glu_a[:, :]), A3, b3(gate_at(n) if isinstance(n, int) else at_tile(merged, n)),
                    MUL).then_inc(evac_done, 1)
                dve.wait_ge(evac_done, n * 2 + (T_GLU + 1))
                dve.wait_ge(b_sig, n + 1)
                tt_(glu_a[:, :], glu_a[:, :], glu_b[:, :], MUL).then_inc(evac_done, 1)
                dve.wait_ge(evac_done, n * 2 + (T_GLU + 2))
                dve.wait_ge(mp_in[r], m * 16 + 16)
                tt_(at_tile(merged, n), glu_a[:, :], pool_t[:, r, :], ADD).then_inc(merged_ready, 1)
                dve.wait_ge(m_hi_ready, n + 1)
                tt_(at_tile(x_lo, n), at_tile(merged, n), at_tile(x_hi, n), SUB).then_inc(m_lo_ready, 1)

            for n in range(4):
                gate(n)
            for n in range(KS):
                gelu(n)
                gate(n + 4)
            dve.wait_ge(gs_sig, KD)
            for r in range(2):
                merge(r, 0, r)
            with dve.Fori(1, 4) as m:
                for r in range(2):
                    merge(2 * m + r, m, r)

            for n in range(KD):
                dve.wait_ge(tile_done, T_OUT + n + 1)
                dve.wait_ge(xt_in[n], 16)
                tt_(b3(hT[:, n, :]), B3 if n % 2 else A3, b3(hT[:, n, :]), ADD).then_inc(evac_done, 1)
                dve.wait_ge(hg_hi_ready, n + 1)
                dve.scalar_tensor_tensor(hg_lo[:, n, :], hT[:, n, :], gains[:, 1, n:n + 1], hg_hi[:, n, :], MUL,
                                         SUB).then_inc(hg_lo_ready, 1)
            dve.wait_ge(ss_turned, 1)
            inverse_root(2, aux[:, 0, 0:TT], diag2)
            take_rows(2)

            def hidden(r, t_gate, t_up, n, step):
                dve.wait_ge(tile_done, t_gate + 1)
                tt_(b3(f_g[:, :]), A3, b3(rstd_row[:, :]), MUL).then_inc(evac_done, 1)
                dve.wait_ge(evac_done, t_gate + 1)
                dve.wait_ge(fs_ready, n + 1)
                tt_(f_g[:, :], f_g[:, :], f_s[:, :], MUL).then_inc(dve_step, 1)
                dve.wait_ge(tile_done, t_up + 1)
                tt_(b3(f_u[:, :]), B3, b3(rstd_row[:, :]), MUL).then_inc(evac_done, 1)
                dve.wait_ge(dve_step, step)
                dve.wait_ge(evac_done, t_up + 1)
                tt_(f_h[:, :], f_g[:, :], f_u[:, :], MUL).then_inc(fh_ready, 1)

            def hidden_lo(r, n):
                dve.wait_ge(f_hi_ready, n + 1)
                tt_(f_lo[:, r, :], f_h[:, :], f_hi[:, r, :], SUB).then_inc(f_lo_ready, 1)

            def add_down(t0, n):
                dve.wait_ge(tile_done, t0 + n + 1)
                tt_(b3(hT[:, n, :]), B3 if n % 2 else A3, b3(hT[:, n, :]), ADD).then_inc(evac_done, 1)

            def add_square(n):
                dve.wait_ge(sq_ready, KD + n + 1)
                if n >= 2:
                    dve.wait_ge(sq_used, KD - 1 + n - 1)
                tt_(sq_sum[:, :], sq_sum[:, :], sq[:, n % 2, :], ADD).then_inc(sq_used, 1)

            base_step = steps[0]
            for r in range(2):
                hidden(r, T_FFN + 2 * r, T_FFN + 2 * r + 1, r, base_step + r + 1)
                hidden_lo(r, r)
            with dve.Fori(1, FCH) as c:
                t0 = 12 * c + (T_LOOP - 12)
                hidden(0, t0, t0 + 1, 2 * c, 2 * c + (base_step + 1))
                for n in range(KD):
                    add_down(t0 + 2, n)
                hidden_lo(0, 2 * c)
                hidden(1, t0 + 10, t0 + 11, 2 * c + 1, 2 * c + (base_step + 2))
                hidden_lo(1, 2 * c + 1)
            steps[0] = base_step + 2 * FCH
            for n in range(KD):
                add_down(T_LAST, n)
                if n >= 2:
                    add_square(n - 1)
            add_square(KD - 1)
            dve.wait_ge(ss_turned, 2)
            inverse_root(3, aux[:, 0, 0:TT], None)
            dve.wait_ge(diag_ready, 3)
            for tt in range(0, TT, 2):
                dve.wait_ge(tok_turned, tt + 1)
                if tt >= 4:
                    dve.wait_ge(y_stored[tt % 4], 16 * (tt // 4))
                dve.tensor_scalar(y_out[0:tok(tt), tt % 4, :], bank_a[0:tok(tt), 0:2, :].rearrange("p b c -> p (b c)"),
                                  ss[0:tok(tt), 2, tt:tt + 1], None, MUL).then_inc(tok_used[0], 1)


INPUTS = ["x_prompt", "x_sample", "state_ssm_re", "state_ssm_im", "state_pool", "g_mix", "w_in", "ssm_a_re", "ssm_a_im",
          "ssm_log_dt", "ssm_b_re", "ssm_b_im", "ssm_c_re", "ssm_c_im", "ssm_d", "w_glu_a", "w_glu_b", "pool_w",
          "pool_scale", "w_out", "g_ffn", "w_ffn_gate", "w_ffn_up", "w_ffn_down", "g_final"]
OUTPUTS = {"y_p": (1, SEQ, D), "y_s": (1, DEC, D), "re_p": (1, 1, G, NS), "im_p": (1, 1, G, NS),
           "pool_p": (1, 1, HIST, W_POOL), "re_s": (1, 1, G, NS), "im_s": (1, 1, G, NS), "pool_s": (1, 1, HIST, W_POOL)}


def kernel(**inputs):
    import concourse.bacc as bacc
    from concourse.bass_utils import run_bass_kernel_spmd

    arrays = {name: np.ascontiguousarray(inputs[name]) for name in INPUTS}
    arrays["c_ident"] = np.eye(P, dtype=np.float32)
    counts = [[1.0 / min(t + 1, w) for t in range(16)] for w in WINDOWS]
    arrays["c_inv_count"] = np.broadcast_to(np.array(counts, np.float32), (P, 4, 16)).copy()
    nc = bacc.Bacc("TRN2", target_bir_lowering=False, num_devices=1, dynamic_dma_scratch_size=1024)
    t_in = {n: nc.dram_tensor(f"in_{n}", a.shape, F32, kind="ExternalInput").ap() for n, a in arrays.items()}
    t_out = {n: nc.dram_tensor(f"out_{n}", s, F32, kind="ExternalOutput").ap() for n, s in OUTPUTS.items()}
    hybrid_layer(nc, t_in, t_out)
    r = run_bass_kernel_spmd(nc, [{f"in_{n}": a for n, a in arrays.items()}], core_ids=[0])
    return tuple(r.results[0][f"out_{n}"] for n in OUTPUTS)
```

```python
from contextlib import ExitStack

import numpy as np

import concourse.bass as bass
from concourse import mybir
from concourse.alu_op_type import AluOpType as ALU

F32 = mybir.dt.float32
F32R = mybir.dt.float32r
I32 = mybir.dt.int32
ACT = mybir.ActivationFunctionType
ds = bass.ds

P = 128
D = 1024
SEQ, DEC = 1024, 32
T = SEQ + DEC
KD = D // P
BLK = T // 3
TT = -(-T // P)
W_SSM = W_POOL = D // 2
KS = W_SSM // P
G, H, NS = 32, 16, 64
PAIRS = G // 2
L = 8
NC = T // L
NCP = SEQ // L
NCG = NC + 1
SLOTS = NCG + 1
SEG, STEPS = 8, NCP // 8
WINDOWS = (2, 4, 8, 16)
HIST = 15
FF = 2816
FCH = FF // P // 2
EPS = 1e-6
XG_SLOTS, XR_SLOTS = 4, 5
PRM_LOADS = 15
SLAB = 8 * P
GELU_C = 2.0 * 0.7978845608028654
TWO_PI = (6.28125, 0.0019350051879882812, 3.019916050561733e-07)
LN2 = (0.693359375, -2.12194440e-4)
EXP_POLY = [1.0 / 5040, 1.0 / 720, 1.0 / 120, 1.0 / 24, 1.0 / 6, 0.5, 1.0]
MAGIC = 12582912.0

S_POOL, T_POOL = 4, 4
S_GATE, T_GATE = 20, 24
S_GLU, T_GLU = 28, 32
S_OUT, T_OUT = 36, 48
S_FFN, T_FFN = 44, 56
S_LOOP, T_LOOP = 48, 60
S_TAIL, T_TAIL = 102, 168


def hybrid_layer(nc, t_in, t_out):
    ctx = ExitStack()
    with ctx:
        def sb(name, shape, dt=F32, stack=ctx):
            return stack.enter_context(nc.sbuf_tensor(name, shape, dt))

        def overlay(*tensors):
            with ExitStack() as stack:
                return [sb(n, s, d, stack) for n, s, d in tensors]

        def sem(name):
            return ctx.enter_context(nc.semaphore(name))

        ident = sb("ident", [P, P])
        ones = sb("ones", [P, P])
        inv_count = sb("inv_count", [P, 4, 16])
        gains = sb("gains", [P, 4, KD])
        stage = sb("stage", [P, 2, SLAB])
        w_hi = sb("w_hi", [P, 2, SLAB], F32R)
        w_lo = sb("w_lo", [P, 2, SLAB], F32R)
        rstd_row = sb("rstd_row", [P, T])
        ss = sb("ss", [P, 4, TT])
        a8pow = sb("a8pow", [P, 2, STEPS, PAIRS])
        neg_a = sb("neg_a", [P, 2, PAIRS])
        pool_hist = sb("pool_hist", [P, 4, HIST])
        new_pool = sb("new_pool", [HIST, 2, W_POOL])
        d_skip = sb("d_skip", [2 * H, PAIRS])
        eye2 = sb("eye2", [2 * H, H])
        out_state = sb("out_state", [PAIRS, 4, P])
        log_dt = sb("log_dt", [PAIRS, 2])
        zeros = sb("zeros", [P, 16])
        state0 = sb("state0", [P, 2, PAIRS])
        head = sb("head", [P, 16])
        base = ExitStack()
        x_hi = sb("x_hi", [P, KD, T], F32R, base)
        x_lo = sb("x_lo", [P, KD, T], F32R, base)
        U, S, TO, CA, W, UT, pl_hi, pl_lo, gate_t = overlay(
            ("U", [P, G, NCG], F32),
            ("S", [P, 2, PAIRS, SLOTS], F32),
            ("TO", [P, G, P], F32),
            ("CA", [P, 2, PAIRS, (L + 1) * H], F32),
            ("W", [P, 2, PAIRS, P], F32),
            ("UT", [P, KS, L, NCG], F32),
            ("pl_hi", [P, T], F32R), ("pl_lo", [P, T], F32R),
            ("gate_t", [P, 2, T], F32))
        (xg,) = overlay(("xg", [P, XG_SLOTS, D], F32))
        (K_sb,) = overlay(("K_sb", [2 * H, PAIRS, P], F32))
        _, x_raw = overlay(("pad0", [P, G * NCG], F32), ("x_raw", [P, XR_SLOTS, D], F32))
        _, WT = overlay(("pad1", [P, G * NCG], F32), ("WT", [P, 2, PAIRS, P], F32))
        q_space = G * NCG + 2 * PAIRS * SLOTS
        _, x_t = overlay(("pad17", [P, q_space], F32), ("x_t", [P, TT, D], F32))
        _, tmp_a, _, tmp_b = overlay(("pad2", [P, q_space], F32), ("tmp_a", [P, PAIRS * 9 * H], F32),
                                     ("pad3", [P, G * P - PAIRS * 9 * H + 2 * PAIRS * 9 * H], F32),
                                     ("tmp_b", [P, PAIRS * 9 * H], F32))
        ut_at = q_space + G * P + 2 * PAIRS * 9 * H + 2 * PAIRS * P
        _, diag = overlay(("pad4", [P, ut_at], F32), ("diag", [P, TT, P], F32))
        _, UP, sum_a, sum_b = overlay(("pad5", [P, ut_at], F32), ("UP", [P, T + 2 * HIST], F32),
                                      ("sum_a", [P, T + 2 * HIST], F32), ("sum_b", [P, T + 2 * HIST], F32))
        pl_at = ut_at + KS * L * NCG
        _, rows, c_raw, b_raw, prm, pt, BB, CT, PW = overlay(
            ("pad6", [P, pl_at], F32),
            ("rows", [32, 10, P], F32), ("c_raw", [P, 2, 4, 2, NS], F32), ("b_raw", [P, 2, PAIRS, H], F32),
            ("prm", [P, 5, PAIRS], F32), ("pt", [P, 30, PAIRS], F32), ("BB", [P, 2, PAIRS, H], F32),
            ("CT", [P, 2, PAIRS, H], F32), ("PW", [P, 2, L + 1, PAIRS], F32))
        _, BD = overlay(("pad18", [P, pl_at], F32), ("BD", [P, 2, PAIRS, 2 * H], F32))
        _, skip_k = overlay(("pad16", [P, pl_at], F32), ("skip_k", [2 * H, PAIRS * H], F32))
        w_at = q_space + G * P + 2 * PAIRS * 9 * H
        _, CA_st = overlay(("pad7", [P, w_at], F32), ("CA_st", [P, G, P], F32))
        _, S_st = overlay(("pad19", [P, w_at - 2 * PAIRS * 9 * H], F32), ("S_st", [P, G, NCG], F32))
        n_fill = PAIRS // 2 * (SEG - 1) * (STEPS - 1)
        _, sc_a, sc_b = overlay(("pad20", [P, w_at - 2 * PAIRS * 9 * H], F32), ("sc_a", [P, n_fill], F32),
                                ("sc_b", [P, n_fill], F32))
        _, end_a, end_b = overlay(("pad21", [P, pl_at], F32), ("end_a", [P, n_fill], F32), ("end_b", [P, n_fill], F32))
        _, x_sq = overlay(("pad8", [P, ut_at + TT * P], F32), ("x_sq", [P, D], F32))
        y_hi, y_lo = overlay(("y_hi", [P, KS, T], F32R), ("y_lo", [P, KS, T], F32R))
        _, YT = overlay(("pad9", [P, ut_at + 4 * T], F32), ("YT", [P, KS, L, NCG], F32))
        _, ge_a, ge_b, ge_c = overlay(("pad10", [P, w_at], F32), ("ge_a", [P, L * NCG], F32),
                                      ("ge_b", [P, L * NCG], F32), ("ge_c", [P, T], F32))
        _, merged = overlay(("pad11", [P, q_space], F32), ("merged", [P, KD, T], F32))
        _, glu_a, glu_b = overlay(("pad12", [P, w_at], F32), ("glu_a", [P, T], F32), ("glu_b", [P, T], F32))
        _, pool_t, sig_s = overlay(("pad13", [P, ut_at], F32), ("pool_t", [P, 2, T], F32),
                                   ("sig_s", [P, 2, T], F32))
        hT, _, hg_hi, hg_lo, sq, sq_sum = overlay(
            ("hT", [P, KD, T], F32), ("pad14", [P, q_space - KD * T], F32),
            ("hg_hi", [P, KD, T], F32R), ("hg_lo", [P, KD, T], F32R), ("sq", [P, 2, T], F32), ("sq_sum", [P, T], F32))
        _, hf = overlay(("pad22", [P, q_space], F32), ("hf", [P, KD, T], F32))
        base.close()
        f_hi, f_lo, f_g, f_s, f_u, f_h = overlay(
            ("f_hi", [P, 2, T], F32R), ("f_lo", [P, 2, T], F32R), ("f_g", [P, T], F32), ("f_s", [P, T], F32),
            ("f_u", [P, T], F32), ("f_h", [P, T], F32))
        _, f2_hi, f2_lo = overlay(("pad15", [P, 8 * T], F32), ("f2_hi", [P, 2, T], F32R), ("f2_lo", [P, 2, T], F32R))
        (y_out,) = overlay(("y_out", [P, TT, D], F32))
        (diag2,) = overlay(("diag2", [P, TT, P], F32))

        bank_a = ctx.enter_context(nc.psum_tensor("bank_a", [P, 3, 512], F32))
        bank_b = ctx.enter_context(nc.psum_tensor("bank_b", [P, 3, 512], F32))
        aux = ctx.enter_context(nc.psum_tensor("aux", [P, 2, 512], F32))
        out_banks = [bank_a, bank_b, aux]
        A3, B3 = bank_a[:, :, 0:BLK], bank_b[:, :, 0:BLK]

        def gate_at(n):
            return sig_s[:, n, :] if n < 2 else merged[:, n, :]

        def at_tile(buf, n):
            return buf[:, n, :] if isinstance(n, int) else buf[:, ds(n, 1), :].rearrange("p a t -> p (a t)")

        def b3(ap):
            return ap.rearrange("p (b t) -> p b t", b=3)

        consts_in, inv_in, prm_in, gains_in = sem("consts_in"), sem("inv_in"), sem("prm_in"), sem("gains_in")
        x_in = [sem(f"x_in{i}") for i in range(TT)]
        stage_in = [sem("stage_in0"), sem("stage_in1")]
        hi_ready, lo_ready = sem("hi_ready"), sem("lo_ready")
        tile_done, evac_done = sem("tile_done"), sem("evac_done")
        ones_ready, dve_step = sem("ones_ready"), sem("dve_step")
        x_turned, x_squared, xg_ready, xraw_ready = sem("x_turned"), sem("x_squared"), sem("xg_ready"), sem("xraw_ready")
        x_hi_ready, x_lo_ready, xraw_out = sem("x_hi_ready"), sem("x_lo_ready"), [sem(f"xraw_out{i}") for i in range(XR_SLOTS)]
        ms_ready, root_ready, diag_ready, row_ready, row_used = (
            sem("ms_ready"), sem("root_ready"), sem("diag_ready"), sem("row_ready"), sem("row_used"))
        rows_ready, prm_turned, prm_used = sem("rows_ready"), sem("prm_turned"), sem("prm_used")
        angle_ready, sine_ready = sem("angle_ready"), sem("sine_ready")
        ca_ready, wt_ready, k_turn, k_evac, w_turn, w_evac = (
            sem("ca_ready"), sem("wt_ready"), sem("k_turn"), sem("k_evac"), sem("w_turn"), sem("w_evac"))
        to_zero, k_ready, to_in = sem("to_zero"), sem("k_ready"), sem("to_in")
        ut_out, u_in = sem("ut_out"), sem("u_in")
        pooled_ready, pooled_hi, pooled_lo, np_turned, np_evac = (
            sem("pooled_ready"), sem("pooled_hi"), sem("pooled_lo"), sem("np_turned"), sem("np_evac"))
        gp_sig, mp_out = sem("gp_sig"), [sem("mp_out0"), sem("mp_out1")]
        s_stacked, ca_stacked = sem("s_stacked"), sem("ca_stacked")
        v_turn, v_evac, s_ready, y_turn, y_evac, st_turn, st_evac = (
            sem("v_turn"), sem("v_evac"), sem("s_ready"), sem("y_turn"), sem("y_evac"), sem("st_turn"), sem("st_evac"))
        y_out_dram, yt_in = sem("y_out_dram"), [sem(f"yt_in{n}") for n in range(KS)]
        y_sq, y_arg, y_sig, y_val, y_hi_ready, y_lo_ready = (
            sem("y_sq"), sem("y_arg"), sem("y_sig"), sem("y_val"), sem("y_hi_ready"), sem("y_lo_ready"))
        gs_sig, b_sig, mp_in, merged_ready, m_hi_ready, m_lo_ready = (
            sem("gs_sig"), sem("b_sig"), [sem("mp_in0"), sem("mp_in1")], sem("merged_ready"),
            sem("m_hi_ready"), sem("m_lo_ready"))
        ss_turned, hg_hi_ready, hg_lo_ready, sq_ready, sq_used = (
            sem("ss_turned"), sem("hg_hi_ready"), sem("hg_lo_ready"), sem("sq_ready"), sem("sq_used"))
        fs_ready, fh_ready, f_hi_ready, f_lo_ready = (
            sem("fs_ready"), sem("fh_ready"), sem("f_hi_ready"), sem("f_lo_ready"))
        hf_ready, tok_turned, tok_used, y_stored = (sem("hf_ready"), sem("tok_turned"), [sem("tok_used0"), sem("tok_used1")],
                                                    sem("y_stored"))
        small_out = sem("small_out")
        xt_in = [sem(f"xt_in{k}") for k in range(KD)]

        w_in = t_in["w_in"][0].rearrange("(k p) n -> p k n", p=P)
        w_a = t_in["w_glu_a"][0].rearrange("(k p) n -> p k n", p=P)
        w_b = t_in["w_glu_b"][0].rearrange("(k p) n -> p k n", p=P)
        w_o = t_in["w_out"][0].rearrange("(k p) n -> p k n", p=P)
        w_g = t_in["w_ffn_gate"][0].rearrange("(k p) n -> p k n", p=P)
        w_u = t_in["w_ffn_up"][0].rearrange("(k p) n -> p k n", p=P)
        w_d = t_in["w_ffn_down"][0].rearrange("(k p) n -> p k n", p=P)
        pool_w = t_in["pool_w"][0]
        xt_dram = nc.dram_tensor("xt_scratch", [D, T], F32).ap()
        u_dram = nc.dram_tensor("u_scratch", [W_SSM, L, NCG], F32).ap()
        y_dram = nc.dram_tensor("y_scratch", [W_SSM, L, NCG], F32).ap()
        mp_dram = nc.dram_tensor("mp_scratch", [D, T], F32).ap()
        x_p, x_s = t_in["x_prompt"][0], t_in["x_sample"][0]

        def tok(tt):
            return min(P, T - tt * P)

        def slab3(slot):
            return stage[:, slot, :].rearrange("p (k n) -> p k n", n=P)

        prm_loads = [
            (rows[0:16, 0, :], t_in["ssm_a_re"][0].rearrange("(pr g) p -> pr (g p)", g=2)),
            (rows[0:16, 1, :], t_in["ssm_a_im"][0].rearrange("(pr g) p -> pr (g p)", g=2)),
            (rows[0:16, 2, :], t_in["state_ssm_re"][0, 0].rearrange("(pr g) p -> pr (g p)", g=2)),
            (rows[0:16, 3, :], t_in["state_ssm_im"][0, 0].rearrange("(pr g) p -> pr (g p)", g=2)),
            (log_dt[:, :], t_in["ssm_log_dt"][0].rearrange("(pr g) -> pr g", g=2)),
            (rows[0:HIST, 6:10, :], t_in["state_pool"][0, 0].rearrange("i (g c) -> i g c", g=4)),
            (d_skip[:, :], t_in["ssm_d"][0].rearrange("(pr g) h -> (g h) pr", g=2)),
        ]
        for comp, name in enumerate(("ssm_c_re", "ssm_c_im")):
            src = t_in[name][0].rearrange("(t g) h p -> (g h) t p", t=4)
            for copy in range(2):
                prm_loads.append((c_raw[:, comp, :, copy, :], src))
        for comp, name in enumerate(("ssm_b_re", "ssm_b_im")):
            src = t_in[name][0].rearrange("(pr g) p h -> g p pr h", g=2)
            for g2 in range(2):
                prm_loads.append((b_raw[64 * g2:64 * g2 + 64, comp], src[g2]))
        assert len(prm_loads) == PRM_LOADS

        def spill_x(sp, tt):
            sp.wait_ge(xraw_ready, tt + 1)
            sp.dma_start(xt_dram[:, tt * P:tt * P + tok(tt)].rearrange("(k p) t -> p k t", p=P),
                         x_raw[:, tt % XR_SLOTS, :].rearrange("p (k t) -> p k t", k=KD)[:, :, 0:tok(tt)]
                         ).then_inc(xraw_out[tt % XR_SLOTS], 16)

        def spill_mp(sp, g):
            for r in range(2):
                n = 2 * g + r
                sp.wait_ge(evac_done, T_POOL + 5 * g + 4 + r)
                sp.dma_start(mp_dram[n * P:(n + 1) * P, :], gate_t[:, r, :]).then_inc(mp_out[r], 16)

        block = ctx.enter_context(nc.Block())

        @block.sync
        def _(sp):
            def slab(s, slot, pieces):
                if not (isinstance(s, int) and s < 2):
                    sp.wait_ge(lo_ready, s - 1)
                for i, (dst, src) in enumerate(pieces):
                    sp.dma_start(dst, src).then_inc(stage_in[slot], 16)

            sp.dma_start(ident[:], t_in["c_ident"]).then_inc(consts_in, 16)

            def load_x(tt):
                src = x_p[tt * P:(tt + 1) * P, :] if tt < SEQ // P else x_s
                sp.dma_start(x_t[0:tok(tt), tt, :], src).then_inc(x_in[tt], 16)

            for tt in range(6):
                load_x(tt)
            slab(0, 0, [(slab3(0), w_in[:, :, 0:P])])
            for tt in range(6, TT):
                load_x(tt)
            spill_x(sp, 0)
            slab(1, 1, [(slab3(1), w_in[:, :, P:2 * P])])
            spill_x(sp, 1)
            spill_x(sp, 2)
            spill_x(sp, 3)
            sp.dma_start(inv_count[:], t_in["c_inv_count"]).then_inc(inv_in, 16)
            with nc.allow_non_contiguous_dma(reason="512 skip weights, one per (channel, group)"):
                for dst, src in prm_loads:
                    sp.dma_start(dst, src).then_inc(prm_in, 16)
            for tt in range(4, TT):
                spill_x(sp, tt)
            for s in (2, 3):
                slab(s, s % 2, [(slab3(s % 2), w_in[:, :, s * P:(s + 1) * P])])
            slab(4, 0, [(slab3(0), w_in[:, :, W_SSM:W_SSM + P])])
            slab(5, 1, [(slab3(1), w_in[:, :, 2 * W_SSM + D:2 * W_SSM + D + P])])

            def third_pool_slab(g):
                c0 = 2 * W_SSM + D + (2 * g + 1) * P
                slab(S_POOL + 4 * g + 2, 0, [(slab3(0), w_in[:, :, c0:c0 + P])])

            def pool_w_slab(g):
                slab(S_POOL + 4 * g + 3, 1, [(stage[:, 1, 0:2 * P], pool_w[g])])

            third_pool_slab(0)
            sp.wait_ge(evac_done, KS)
            sp.dma_start(u_dram.rearrange("(n p) j c -> p n j c", p=P), UT[:, :, :, :]).then_inc(ut_out, 16)
            pool_w_slab(0)
            sp.wait_ge(k_ready, 1)
            sp.wait_ge(to_zero, 1)
            for i in range(L):
                j = L - 1 - i
                for g2 in range(2):
                    sp.dma_start(TO[16 * i:16 * i + 16, g2:G:2, 16 * j:P],
                                 K_sb[16 * g2:16 * g2 + 16, :, 0:P - 16 * j]).then_inc(to_in, 16)
            sp.wait_ge(ut_out, 16)
            sp.wait_ge(to_in, 32 * L)
            for i in range(L):
                sp.dma_start(U[16 * i:16 * i + 16, :, :],
                             u_dram[:, L - 1 - i, :].rearrange("(g h) c -> h g c", h=H)).then_inc(u_in, 16)
            for g in range(1, 4):
                s0 = S_POOL + 4 * g
                slab(s0, 0, [(slab3(0), w_in[:, :, W_SSM + g * P:W_SSM + (g + 1) * P])])
                c0 = 2 * W_SSM + D + 2 * g * P
                slab(s0 + 1, 1, [(slab3(1), w_in[:, :, c0:c0 + P])])
                if g == 1:
                    sp.wait_ge(v_turn, PAIRS)
                    for comp in range(2):
                        for g2 in range(2):
                            sp.dma_start(CA_st[64 * comp:64 * comp + 64, g2:G:2, :],
                                         CA[64 * g2:64 * g2 + 64, comp, :, H:9 * H]).then_inc(ca_stacked, 16)
                third_pool_slab(g)
                pool_w_slab(g)
                spill_mp(sp, g - 1)

            def gate_slab(n):
                c0 = 2 * W_SSM + n * P
                slab(S_GATE + n, n % 2, [(slab3(n % 2), w_in[:, :, c0:c0 + P])])

            for n in range(2):
                gate_slab(n)
            spill_mp(sp, 3)
            for n in range(2, 6):
                gate_slab(n)
            sp.wait_ge(np_evac, 4)
            sp.dma_start(t_out["pool_p"][0, 0], new_pool[:, 0, :]).then_inc(small_out, 16)
            sp.dma_start(t_out["pool_s"][0, 0], new_pool[:, 1, :]).then_inc(small_out, 16)
            sp.wait_ge(y_evac, 12)
            for j in range(L):
                sp.dma_start(y_dram[:, j, :].rearrange("(g h) c -> h g c", h=H),
                             U[16 * j:16 * j + 16, :, :]).then_inc(y_out_dram, 16)
            for q in mp_out:
                sp.wait_ge(q, 16 * 4)
            sp.wait_ge(y_out_dram, 16 * L)
            for n in range(KS):
                sp.dma_start(YT[:, n], y_dram[n * P:(n + 1) * P]).then_inc(yt_in[n], 16)
            sp.wait_ge(st_evac, 1)
            for i, name in enumerate(("re_p", "im_p", "re_s", "im_s")):
                sp.dma_start(t_out[name][0, 0].rearrange("(pr g) p -> pr (g p)", g=2),
                             out_state[:, i, :]).then_inc(small_out, 16)
            for n in range(6, KD):
                gate_slab(n)
            for n in range(KD):
                r = n % 2
                half = slab3(r)
                slab(S_GLU + n, r, [(half[:, 0:4], w_a[:, :, n * P:(n + 1) * P]),
                                    (half[:, 4:8], w_b[:, :, n * P:(n + 1) * P])])
                if n >= 2:
                    sp.wait_ge(merged_ready, n - 1)
                sp.dma_start(pool_t[:, r, :], mp_dram[n * P:(n + 1) * P, :]).then_inc(mp_in[r], 16)
            for n in range(KD):
                slab(S_OUT + n, n % 2, [(slab3(n % 2), w_o[:, :, n * P:(n + 1) * P])])
                if n == 1:
                    sp.wait_ge(tile_done, T_OUT)
                    for i, q in enumerate(xraw_out):
                        sp.wait_ge(q, 16 * len(range(i, TT, XR_SLOTS)))
                    for k in range(KD):
                        sp.dma_start(hT[:, k, :], xt_dram[k * P:(k + 1) * P, :]).then_inc(xt_in[k], 16)
            for f in range(2):
                slab(S_FFN + 2 * f, 0, [(slab3(0), w_g[:, :, f * P:(f + 1) * P])])
                slab(S_FFN + 2 * f + 1, 1, [(slab3(1), w_u[:, :, f * P:(f + 1) * P])])
            down = [stage[:, r, :].rearrange("p (k n) -> p k n", n=4 * P) for r in range(2)]
            with sp.Fori(1, FCH - 1) as c:
                s0 = 6 * c + (S_LOOP - 6)
                slab(s0, 0, [(slab3(0), w_g[:, :, ds(c * (2 * P), P)])])
                slab(s0 + 1, 1, [(slab3(1), w_u[:, :, ds(c * (2 * P), P)])])
                for r in range(2):
                    slab(s0 + 2 + r, r, [(down[r], w_d[:, ds(c * 2 - 2, 2), r * 4 * P:(r + 1) * 4 * P])])
                slab(s0 + 4, 0, [(slab3(0), w_g[:, :, ds(c * (2 * P) + P, P)])])
                slab(s0 + 5, 1, [(slab3(1), w_u[:, :, ds(c * (2 * P) + P, P)])])
            for f in (2 * FCH - 2, 2 * FCH - 1):
                s0 = S_TAIL + 2 * (f % 2)
                slab(s0, 0, [(slab3(0), w_g[:, :, f * P:(f + 1) * P])])
                slab(s0 + 1, 1, [(slab3(1), w_u[:, :, f * P:(f + 1) * P])])
            for i, f in enumerate((2 * FCH - 4, 2 * FCH - 2)):
                for r in range(2):
                    slab(S_TAIL + 4 + 2 * i + r, r, [(down[r], w_d[:, f:f + 2, r * 4 * P:(r + 1) * 4 * P])])
            for tt in range(TT):
                sp.wait_ge(tok_used[tt % 2], tt // 2 + 1)
                dst = t_out["y_p"][0, tt * P:(tt + 1) * P, :] if tt < SEQ // P else t_out["y_s"][0]
                sp.dma_start(dst, y_out[0:tok(tt), tt, :]).then_inc(y_stored, 16)
            sp.wait_ge(y_stored, 16 * TT)
            sp.wait_ge(small_out, 16 * 6)


        @block.tensor
        def _(pe):
            def tile(t, banks, slot, terms, hi, lo, ready=None, halfway=None):
                if not (isinstance(t, int) and t < 2):
                    pe.wait_ge(evac_done, t - 1)
                for i, (col, k) in enumerate(terms):
                    if halfway is not None and 2 * i == len(terms):
                        halfway()
                    if ready is not None:
                        pe.wait_ge(ready, k + 1)
                    for step, (w, x) in enumerate(((w_hi, hi), (w_hi, lo), (w_lo, hi))):
                        for b in range(3):
                            mm = pe.matmul(banks[:, b, 0:BLK], w[:, slot, col:col + P],
                                           x[:, k, b * BLK:(b + 1) * BLK],
                                           start=(i == 0 and step == 0), stop=(i == len(terms) - 1 and step == 2))
                mm.then_inc(tile_done, 1)

            ALL = [(k * P, k) for k in range(KD)]

            def rstd_rows(n, scaled):
                pe.wait_ge(diag_ready, n)
                for tt in range(TT):
                    out = aux[:, tt // 4, (tt % 4) * P:(tt % 4 + 1) * P] if tt < 8 else bank_a[:, 2, 384:384 + DEC]
                    mm = pe.matmul(out, ones[0:tok(tt), :], scaled[0:tok(tt), tt, 0:tok(tt)], start=True, stop=True)
                mm.then_inc(row_ready, 1)

            pe.wait_ge(consts_in, 16)
            for tt in range(TT):
                pe.wait_ge(x_in[tt], 16)
                if tt >= 2:
                    pe.wait_ge(xraw_ready, tt - 1)
                    pe.wait_ge(xg_ready, tt - 1)
                banks = bank_b if tt % 2 else bank_a
                for k in range(KD):
                    mm = pe.transpose(banks[:, k // 4, (k % 4) * P:(k % 4) * P + tok(tt)],
                                      x_t[0:tok(tt), tt, k * P:(k + 1) * P], ident[0:tok(tt), 0:tok(tt)])
                mm.then_inc(x_turned, 1)
                if tt == 0:
                    pe.wait_ge(gains_in, 64)
                    pe.transpose(aux[:, 0, 0:32], rows[0:32, 5, :], ident[0:32, 0:32]).then_inc(prm_turned, 1)
            def turn_parameters():
                pe.wait_ge(rows_ready, 1)
                for i in range(5):
                    pe.transpose(aux[:, 0, 16 * i:16 * i + 16], rows[0:16, i, :], ident[0:16, 0:16])
                for g in range(4):
                    pe.transpose(aux[:, 0, 192 + 16 * g:192 + 16 * g + HIST], rows[0:HIST, 6 + g, :], ident[0:HIST, 0:HIST])
                for comp in range(2):
                    for i in range(4):
                        mm = pe.transpose((bank_b[:, 2] if comp else aux[:, 1])[:, i * P:(i + 1) * P],
                                          c_raw[:, comp, i].rearrange("r a p -> r (a p)"), ident[:, :])
                mm.then_inc(prm_turned, 1)

            pe.wait_ge(xraw_ready, TT)
            for w, x, ready, count in ((w_hi, x_hi, x_hi_ready, TT), (w_lo, x_hi, lo_ready, 1), (w_hi, x_lo, x_lo_ready, TT)):
                pe.wait_ge(ready, count)
                if w is w_hi:
                    pe.wait_ge(hi_ready, 1)
                for k in range(KD):
                    for b in range(3):
                        mm = pe.matmul(bank_a[:, b, 0:BLK], w[:, 0, k * P:(k + 1) * P], x[:, k, b * BLK:(b + 1) * BLK],
                                       start=(w is w_hi and x is x_hi and k == 0), stop=(x is x_lo and k == KD - 1))
                if w is w_hi and x is x_hi:
                    turn_parameters()
            mm.then_inc(tile_done, 1)
            for s in range(4):
                if s:
                    pe.wait_ge(lo_ready, s + 1)
                    tile(s, bank_b if s % 2 else bank_a, s % 2, ALL, x_hi, x_lo)
                if s == 0:
                    pe.wait_ge(prm_used, 2)
                    rstd_rows(1, diag)
            pe.wait_ge(ca_ready, 1)
            pe.wait_ge(row_used, 1)
            for q in range(4):
                if q >= 2:
                    pe.wait_ge(k_evac, q - 1)
                for i in range(4):
                    for comp in range(2):
                        mm = pe.matmul(aux[0:2 * H, q % 2, i * P:(i + 1) * P], BD[:, comp, 4 * q + i, :],
                                       CA[:, comp, 4 * q + i, 0:P], start=(comp == 0), stop=(comp == 1))
                mm.then_inc(k_turn, 1)
            def turn_w():
                pe.wait_ge(wt_ready, 1)
                pe.wait_ge(k_evac, 4)
                for r in range(8):
                    if r >= 2:
                        pe.wait_ge(w_evac, r - 1)
                    for i in range(4):
                        mm = pe.transpose(aux[:, r % 2, i * P:(i + 1) * P], WT[:, r // 4, 4 * (r % 4) + i, :], ident[:, :])
                    mm.then_inc(w_turn, 1)
                pe.wait_ge(w_evac, 8)

            def pool_group(g, after_first=None):
                s0, t0 = 4 * g + S_POOL, 5 * g + T_POOL
                pe.wait_ge(lo_ready, s0 + 1)
                tile(t0, bank_a, 0, ALL, x_hi, x_lo)
                if after_first is not None:
                    after_first()
                pe.wait_ge(lo_ready, s0 + 2)
                tile(t0 + 1, bank_b, 1, ALL, x_hi, x_lo)
                pe.wait_ge(lo_ready, s0 + 3)
                tile(t0 + 2, bank_a, 0, ALL, x_hi, x_lo)
                pe.wait_ge(lo_ready, s0 + 4)
                pe.wait_ge(pooled_lo, g + 1)
                hi, lo = pl_hi[:, :].unsqueeze(1), pl_lo[:, :].unsqueeze(1)
                tile(t0 + 3, bank_b, 1, [(0, 0)], hi, lo)
                if not isinstance(g, int):
                    pe.wait_ge(np_evac, g)
                pe.transpose(aux[0:HIST, 0, 0:P], UP[:, SEQ:SEQ + HIST], ident[:, :])
                pe.transpose(aux[0:HIST, 0, P:2 * P], UP[:, T + HIST:T + 2 * HIST], ident[:, :]).then_inc(np_turned, 1)
                pe.wait_ge(evac_done, t0 + 4)
                tile(t0 + 4, bank_b, 1, [(P, 0)], hi, lo)

            pool_group(0, turn_w)
            pe.wait_ge(u_in, 16 * L)
            for pr in range(PAIRS):
                if pr == 1:
                    pe.wait_ge(np_evac, 1)
                if pr >= 2:
                    pe.wait_ge(v_evac, pr - 1)
                for comp in range(2):
                    for g2 in range(2):
                        mm = pe.matmul(aux[64 * g2:64 * g2 + 64, (pr + 1) % 2, comp * NCG:(comp + 1) * NCG],
                                       W[:, comp, pr, 64 * g2:64 * g2 + 64], U[:, 2 * pr + g2, :], start=True, stop=True)
                mm.then_inc(v_turn, 1)
            pe.wait_ge(v_evac, PAIRS)
            with pe.Fori(1, 4) as g:
                pool_group(g)
            for r, banks in enumerate((bank_a, bank_b)):
                pe.wait_ge(lo_ready, S_GATE + 1 + r)
                tile(T_GATE + r, banks, r, ALL, x_hi, x_lo)
            pe.wait_ge(s_stacked, 4)
            pe.wait_ge(ca_stacked, 64)
            pe.wait_ge(to_in, 32 * L)
            pe.wait_ge(np_evac, 4)
            for r in range(12):
                g2, prs = r % 2, range(3 * (r // 2), min(3 * (r // 2) + 3, PAIRS))
                if r >= 2:
                    pe.wait_ge(y_evac, r - 1)
                for i, pr in enumerate(prs):
                    out = aux[:, g2, i * NCG:(i + 1) * NCG]
                    pe.matmul(out, TO[:, 2 * pr + g2, :], U[:, 2 * pr + g2, :], start=True, stop=False)
                    mm = pe.matmul(out, CA_st[:, 2 * pr + g2, :], S_st[:, 2 * pr + g2, :], start=False, stop=True)
                mm.then_inc(y_turn, 1)
            pe.wait_ge(y_evac, 12)
            for i, (comp, slot) in enumerate(((0, NCP), (1, NCP), (0, NCG), (1, NCG))):
                mm = pe.transpose(aux[0:PAIRS, 0, i * P:(i + 1) * P], S[:, comp, :, slot], ident[:, :])
            mm.then_inc(st_turn, 1)
            with pe.Fori(1, 4) as m:
                for r, banks in enumerate((bank_a, bank_b)):
                    pe.wait_ge(lo_ready, 2 * m + (S_GATE + 1 + r))
                    tile(2 * m + (T_GATE + r), banks, r, ALL, x_hi, x_lo)
            pe.wait_ge(y_lo_ready, KS)
            with pe.Fori(0, 4) as m:
                for r in range(2):
                    pe.wait_ge(lo_ready, 2 * m + (S_GLU + 1 + r))
                    tile(4 * m + (T_GLU + 2 * r), bank_a, r, [(k * P, k) for k in range(KS)], y_hi, y_lo)
                    tile(4 * m + (T_GLU + 2 * r + 1), bank_b, r, [((KS + k) * P, k) for k in range(KS)], y_hi, y_lo)

            def sum_squares(n):
                pe.wait_ge(sq_used, (KD - 1) * n)
                pe.matmul(aux[:, 0, 0:TT], ones[:, :], zeros[:, 0:TT], start=True, stop=False, skip_group_check=True)
                for tt in range(TT):
                    mm = pe.matmul(aux[0:tok(tt), 0, tt:tt + 1], sq_sum[:, tt * P:tt * P + tok(tt)], ones[:, 0:1],
                                   start=False, stop=False, skip_group_check=True)
                mm.then_inc(ss_turned, 1)

            pe.wait_ge(st_evac, 1)
            pe.wait_ge(lo_ready, S_OUT + 1)
            tile(T_OUT, bank_a, 0, ALL, x_hi, x_lo, ready=m_lo_ready)
            with pe.Fori(0, 3) as i:
                for r, banks in ((1, bank_b), (0, bank_a)):
                    n = 2 * i + 2 - r
                    pe.wait_ge(lo_ready, n + (S_OUT + 1))
                    tile(n + T_OUT, banks, r, ALL, x_hi, x_lo)
            pe.wait_ge(lo_ready, S_OUT + 8)
            tile(T_OUT + 7, bank_b, 1, ALL, x_hi, x_lo)
            pe.wait_ge(lo_ready, S_FFN + 1)
            tile(T_FFN, bank_a, 0, ALL, hg_hi, hg_lo, ready=hg_lo_ready)
            pe.wait_ge(lo_ready, S_FFN + 2)
            sum_squares(1)
            tile(T_FFN + 1, bank_b, 1, ALL, hg_hi, hg_lo, halfway=lambda: rstd_rows(2, diag2))
            for r, banks in enumerate((bank_a, bank_b)):
                pe.wait_ge(lo_ready, S_FFN + 3 + r)
                tile(T_FFN + 2 + r, banks, r, ALL, hg_hi, hg_lo)

            def down(t0, s0, n, hi=f_hi, lo=f_lo):
                if n % 4 == 0:
                    pe.wait_ge(lo_ready, s0 + 1 + n // 4)
                col = (n % 4) * P
                tile(t0 + n, bank_b if n % 2 else bank_a, n // 4, [(col, 0), (4 * P + col, 1)], hi, lo)

            with pe.Fori(1, FCH - 1) as c:
                s0, t0 = 6 * c + (S_LOOP - 6), 12 * c + (T_LOOP - 12)
                for r, banks in enumerate((bank_a, bank_b)):
                    pe.wait_ge(lo_ready, s0 + 1 + r)
                    tile(t0 + r, banks, r, ALL, hg_hi, hg_lo)
                pe.wait_ge(f_lo_ready, 2 * c)
                for n in range(KD):
                    down(t0 + 2, s0 + 2, n)
                for r, banks in enumerate((bank_a, bank_b)):
                    pe.wait_ge(lo_ready, s0 + 5 + r)
                    tile(t0 + 10 + r, banks, r, ALL, hg_hi, hg_lo)
            for r in range(4):
                pe.wait_ge(lo_ready, S_TAIL + 1 + r)
                tile(T_TAIL + r, bank_b if r % 2 else bank_a, r % 2, ALL, hg_hi, hg_lo)
            for n in range(KD):
                down(T_TAIL + 4, S_TAIL + 4, n)
            pe.wait_ge(f_lo_ready, 2 * FCH)
            for n in range(KD):
                down(T_TAIL + 12, S_TAIL + 6, n, f2_hi, f2_lo)
            sum_squares(2)
            pe.wait_ge(hf_ready, KD)
            pe.wait_ge(evac_done, T_TAIL + 20)
            for tt in range(TT):
                if tt == 2:
                    pe.wait_ge(ms_ready, 3)
                if tt >= 3:
                    pe.wait_ge(tok_used[(tt - 3) % 2], (tt - 3) // 2 + 1)
                banks = out_banks[tt % 3]
                for k in range(KD):
                    mm = pe.transpose(banks[0:tok(tt), k // 4, (k % 4) * P:(k % 4 + 1) * P],
                                      hf[:, k, tt * P:tt * P + tok(tt)], ident[:, :])
                mm.then_inc(tok_turned, 1)

        @block.scalar
        def _(act):
            def split(s, slot, landed, done, cols=SLAB):
                act.wait_ge(stage_in[slot], landed)
                if done is not None:
                    act.wait_ge(tile_done, done)
                act.activation(w_hi[:, slot, 0:cols], stage[:, slot, 0:cols], ACT.Copy).then_inc(hi_ready, 1)

            def landed(s):
                return 16 * (s // 2 + 1) + (64 if s >= S_OUT else 16 * ((s - S_GLU) // 2 + 1) if s >= S_GLU else 0)

            for dst, src in ((rows[0:8, 5, :], t_in["g_mix"][0]), (rows[8:16, 5, :], t_in["g_ffn"][0]),
                             (rows[16:24, 5, :], t_in["g_final"]), (rows[24:32, 5, :], t_in["pool_scale"][0])):
                act.dma_start(dst, src.rearrange("(k p) -> k p", p=P)).then_inc(gains_in, 16)
            act.wait_ge(ones_ready, 1)
            for tt in range(TT + 1):
                if tt < TT:
                    act.wait_ge(x_in[tt], 16)
                    if tt:
                        act.wait_ge(x_squared, tt)
                    act.activation(x_sq[0:tok(tt), :], x_t[0:tok(tt), tt, :], ACT.Square,
                                   accum_out=ss[0:tok(tt), 0, tt:tt + 1]).then_inc(x_squared, 1)
                if tt:
                    u = tt - 1
                    act.wait_ge(xg_ready, tt)
                    act.activation(x_hi[:, :, u * P:u * P + tok(u)],
                                   xg[:, u % XG_SLOTS, :].rearrange("p (k t) -> p k t", k=KD)[:, :, 0:tok(u)],
                                   ACT.Copy).then_inc(x_hi_ready, 1)
                if tt == 5:
                    split(0, 0, landed(0), None)
            split(1, 1, landed(1), None)

            def root(n):
                act.wait_ge(ms_ready, n)
                act.activation(ss[:, 1, :], ss[:, 0, :], ACT.Sqrt).then_inc(root_ready, 1)

            root(1)
            act.wait_ge(angle_ready, 1)
            act.activation(pt[:, 8:10, :], pt[:, 6:8, :], ACT.Sin).then_inc(sine_ready, 1)
            for s in range(2, 6):
                split(s, s % 2, landed(s), s - 1)
            act.wait_ge(x_lo_ready, TT)
            for q in range(4):
                act.wait_ge(k_turn, q + 1)
                act.activation(K_sb[:, 4 * q:4 * q + 4, :], aux[0:2 * H, q % 2, :].rearrange("h (i c) -> h i c", i=4),
                               ACT.Copy).then_inc(k_evac, 1)
            for r in range(8):
                act.wait_ge(w_turn, r + 1)
                act.activation(W[:, r // 4, 4 * (r % 4):4 * (r % 4) + 4, :],
                               aux[:, r % 2, :].rearrange("p (i c) -> p i c", i=4), ACT.Copy).then_inc(w_evac, 1)
            for g in range(4):
                s0, t0 = 4 * g + S_POOL, 5 * g + T_POOL
                split(s0 + 2, 0, landed(s0 + 2), t0 + 1)
                act.wait_ge(pooled_ready, g + 1)
                act.activation(pl_hi[:, :], (sum_b if g % 2 == 0 else sum_a)[:, 0:T], ACT.Copy).then_inc(pooled_hi, 1)
                for r in range(2):
                    split(s0 + 3 + r, 1 - r, landed(s0 + 3 + r), t0 + 2 + r, cols=(2 * P, SLAB)[r])
                    act.wait_ge(evac_done, t0 + 2 + r)
                    act.activation(gate_t[:, r, :], gate_t[:, r, :], ACT.Sigmoid).then_inc(gp_sig, 1)
                split(s0 + 5, 1, landed(s0 + 5), t0 + 5)
                act.wait_ge(np_turned, g + 1)
                act.activation(new_pool[:, :, g * P:(g + 1) * P], aux[0:HIST, 0, 0:2 * P].rearrange("i (a c) -> i a c", a=2),
                               ACT.Copy).then_inc(np_evac, 1)
                if g == 0:
                    act.wait_ge(wt_ready, 1)
                    for pr in range(PAIRS):
                        act.wait_ge(v_turn, pr + 1)
                        act.activation(S[:, :, pr, 1:NCG + 1], aux[:, (pr + 1) % 2, 0:2 * NCG].rearrange("p (a c) -> p a c", a=2),
                                       ACT.Copy).then_inc(v_evac, 1)

            def gate(n):
                split(S_GATE + n + 2, n % 2, landed(S_GATE + n + 2), T_GATE + n + 1)
                act.wait_ge(evac_done, T_GATE + n + 1)
                g_at = gate_at(n)
                act.activation(g_at, g_at, ACT.Sigmoid).then_inc(gs_sig, 1)

            for comp in range(2):
                act.wait_ge(s_ready, comp + 1)
                for g2 in range(2):
                    act.activation(S_st[64 * comp:64 * comp + 64, g2:G:2, :], S[64 * g2:64 * g2 + 64, comp, :, 0:NCG],
                                   ACT.Copy).then_inc(s_stacked, 1)
            gate(0)
            gate(1)
            for r in range(12):
                g2, n = r % 2, min(3, PAIRS - 3 * (r // 2))
                act.wait_ge(y_turn, r + 1)
                act.activation(U[:, 6 * (r // 2) + g2:6 * (r // 2) + 2 * n:2, :],
                               aux[:, g2, 0:n * NCG].rearrange("p (i c) -> p i c", i=n), ACT.Copy).then_inc(y_evac, 1)
            act.wait_ge(st_turn, 1)
            act.activation(out_state[:, :, :], aux[0:PAIRS, 0, :].rearrange("q (i c) -> q i c", i=4), ACT.Copy).then_inc(st_evac, 1)

            def gelu(n):
                act.wait_ge(yt_in[n], 16)
                if n:
                    act.wait_ge(y_val, n)
                act.activation(ge_a[:, :], YT[:, n].rearrange("p j c -> p (j c)"), ACT.Square).then_inc(y_sq, 1)
                act.wait_ge(y_arg, n + 1)
                act.activation(ge_b[:, :], ge_a[:, :], ACT.Sigmoid, scale=GELU_C).then_inc(y_sig, 1)
                act.wait_ge(y_val, n + 1)
                act.activation(y_hi[:, n, :], ge_c[:, :], ACT.Copy).then_inc(y_hi_ready, 1)

            def glu(n, r, count):
                act.wait_ge(tile_done, n * 2 + (T_GLU + 2))
                act.activation(b3(glu_b[:, :]), B3, ACT.Sigmoid).then_inc(b_sig, 1)
                split(n + (S_GLU + 2), r, count, None)
                act.wait_ge(merged_ready, n + 1)
                act.activation(at_tile(x_hi, n), at_tile(merged, n), ACT.Copy).then_inc(m_hi_ready, 1)

            gate(2)
            gate(3)
            for n in range(KS):
                gelu(n)
                gate(n + 4)
            with act.Fori(0, 3) as m:
                for r in range(2):
                    glu(2 * m + r, r, 32 * m + (landed(S_GLU) + 32))
            for n in (6, 7):
                glu(n, n % 2, landed(S_OUT + n - 6))

            def squares(n, i0, src):
                if n >= 3:
                    act.wait_ge(sq_used, i0 + n - 2)
                act.activation(sq[:, n % 2, :] if n else sq_sum[:, :], src, ACT.Square).then_inc(sq_ready, 1)

            for n in range(KD):
                split(S_OUT + n + 2, n % 2, landed(S_OUT + n + 2), T_OUT + n + 1)
                act.wait_ge(evac_done, T_OUT + n + 1)
                act.activation(hg_hi[:, n, :], hT[:, n, :], ACT.Copy, scale=gains[:, 1, n:n + 1]).then_inc(hg_hi_ready, 1)
                squares(n, 0, hT[:, n, :])

            def sig_f(t_gate):
                act.wait_ge(evac_done, t_gate + 1)
                act.activation(f_s[:, :], f_g[:, :], ACT.Sigmoid).then_inc(fs_ready, 1)

            def hi_f(r, count, to=f_hi):
                act.wait_ge(fh_ready, count)
                act.activation(to[:, r, :], f_h[:, :], ACT.Copy).then_inc(f_hi_ready, 1)

            split(S_FFN + 2, 0, landed(S_FFN + 2), T_FFN + 1)
            root(2)
            split(S_FFN + 3, 1, landed(S_FFN + 3), T_FFN + 2)
            sig_f(T_FFN)
            split(S_FFN + 4, 0, landed(S_FFN + 4), T_FFN + 3)
            hi_f(0, 1)
            sig_f(T_FFN + 2)
            split(S_FFN + 5, 1, landed(S_FFN + 5), T_FFN + 4)
            hi_f(1, 2)
            with act.Fori(1, FCH - 1) as c:
                s0, t0 = 6 * c + (S_LOOP - 6), 12 * c + (T_LOOP - 12)
                l0 = 48 * c + (landed(S_LOOP) - 48)
                split(s0 + 2, 0, l0 + 16, t0 + 1)
                sig_f(t0)
                split(s0 + 3, 1, l0 + 16, t0 + 2)
                split(s0 + 4, 0, l0 + 32, t0 + 6)
                split(s0 + 5, 1, l0 + 32, t0 + 10)
                hi_f(0, 2 * c + 1)
                split(s0 + 6, 0, l0 + 48, t0 + 11)
                sig_f(t0 + 10)
                split(s0 + 7, 1, l0 + 48, t0 + 12)
                hi_f(1, 2 * c + 2)
            for s, done in ((2, 1), (3, 2), (4, 3), (5, 4), (6, 8), (7, 12)):
                split(S_TAIL + s, s % 2, landed(S_TAIL + s), T_TAIL + done)
                if s in (2, 4):
                    sig_f(T_TAIL + s - 2)
                if s in (3, 5):
                    hi_f((s - 3) // 2, 2 * FCH - 1 + (s - 3) // 2, f2_hi)
            for n in range(KD):
                act.wait_ge(evac_done, T_TAIL + 12 + n + 1)
                squares(n, KD - 1, hT[:, n, :])
                act.activation(hf[:, n, :], hT[:, n, :], ACT.Copy, scale=gains[:, 2, n:n + 1]).then_inc(hf_ready, 1)
            root(3)
            act.wait_ge(diag_ready, 3)
            for tt in range(1, TT, 2):
                act.wait_ge(tok_turned, tt + 1)
                act.activation(y_out[0:tok(tt), tt, :], out_banks[tt % 3][0:tok(tt), 0:2, :].rearrange("p b c -> p (b c)"), ACT.Copy,
                               scale=ss[0:tok(tt), 2, tt:tt + 1]).then_inc(tok_used[1], 1)

        @block.gpsimd
        def _(pool):
            def lo(s, slot, cols=SLAB):
                pool.wait_ge(hi_ready, s + 1)
                pool.tensor_tensor(w_lo[:, slot, 0:cols], stage[:, slot, 0:cols], w_hi[:, slot, 0:cols],
                                   ALU.subtract).then_inc(lo_ready, 1)

            for tt in range(TT):
                pool.wait_ge(x_hi_ready, tt + 1)
                cut = slice(tt * P, tt * P + tok(tt))
                pool.tensor_tensor(x_lo[:, :, cut], xg[:, tt % XG_SLOTS, :].rearrange("p (k t) -> p k t", k=KD)[:, :, 0:tok(tt)],
                                   x_hi[:, :, cut], ALU.subtract).then_inc(x_lo_ready, 1)
                if tt == 6:
                    lo(0, 0)
            for s in range(1, 5):
                lo(s, s % 2)
            pool.wait_ge(wt_ready, 1)
            pool.memset(TO[:, :, :], 0.0).then_inc(to_zero, 1)
            for s in range(5, S_GATE):
                lo(s, s % 2, 2 * P if s % 4 == 3 else SLAB)
            with pool.Fori(0, (S_OUT + 2 - S_GATE) // 2) as i:
                for r in range(2):
                    lo(2 * i + (S_GATE + r), r)
            for n in range(KD):
                lo(S_OUT + n + 2, n % 2)
                if n:
                    pool.wait_ge(sq_ready, n + 1)
                    if n >= 2:
                        pool.wait_ge(sq_used, n - 1)
                    pool.tensor_tensor(sq_sum[:, :], sq_sum[:, :], sq[:, n % 2, :], ALU.add).then_inc(sq_used, 1)
            with pool.Fori(0, (S_TAIL + 8 - (S_FFN + 2)) // 2) as i:
                for r in range(2):
                    lo(2 * i + (S_FFN + 2 + r), r)

        @block.vector
        def _(dve):
            steps = [0]

            def then(ins):
                steps[0] += 1
                ins.then_inc(dve_step, 1)
                dve.wait_ge(dve_step, steps[0])

            def tt_(out, a, b, op):
                return dve.tensor_tensor(out, a, b, op)

            MUL, ADD, SUB = ALU.mult, ALU.add, ALU.subtract
            dve.memset(zeros[:, :], 0.0)
            dve.memset(ss[:, :, :], 1.0)
            dve.memset(ones[:, :], 1.0).then_inc(ones_ready, 1)

            def take_gains():
                dve.wait_ge(prm_turned, 1)
                dve.tensor_copy(gains[:, :, :], aux[:, 0, 0:32].rearrange("p (v k) -> p v k", v=4)).then_inc(prm_used, 1)
                dve.wait_ge(prm_used, 1)

            for tt in range(TT):
                dve.wait_ge(x_turned, tt + 1)
                if tt >= XG_SLOTS:
                    dve.wait_ge(x_lo_ready, tt - XG_SLOTS + 1)
                    dve.wait_ge(x_squared, 1)
                turned = (bank_b if tt % 2 else bank_a)[:, 0:2, :].rearrange("p b (k t) -> p (b k) t", t=P)[:, :, 0:tok(tt)]

                def cut(buf, slots):
                    return buf[:, tt % slots, :].rearrange("p (k t) -> p k t", k=KD)[:, :, 0:tok(tt)]
                if tt == 0:
                    dve.tensor_copy(cut(x_raw, XR_SLOTS), turned).then_inc(xraw_ready, 1)
                    take_gains()
                tt_(cut(xg, XG_SLOTS), turned, gains[:, 0, :].unsqueeze(2).to_broadcast([P, KD, tok(tt)]), MUL).then_inc(xg_ready, 1)
                if tt >= XR_SLOTS:
                    dve.wait_ge(xraw_out[tt % XR_SLOTS], 16 * (tt // XR_SLOTS))
                if tt:
                    dve.tensor_copy(cut(x_raw, XR_SLOTS), turned).then_inc(xraw_ready, 1)

            def inverse_root(n, mean_in, scaled):
                dve.tensor_scalar(ss[:, 0, :], mean_in, 1.0 / D, EPS, MUL, ADD).then_inc(ms_ready, 1)
                dve.wait_ge(root_ready, n)
                then(dve.reciprocal(ss[:, 2, :], ss[:, 1, :]))
                then(tt_(ss[:, 3, :], ss[:, 2, :], ss[:, 2, :], MUL))
                then(tt_(ss[:, 3, :], ss[:, 3, :], ss[:, 0, :], MUL))
                then(dve.tensor_scalar(ss[:, 3, :], ss[:, 3, :], -0.5, 1.5, MUL, ADD))
                if scaled is None:
                    tt_(ss[:, 2, :], ss[:, 2, :], ss[:, 3, :], MUL).then_inc(diag_ready, 1)
                    return
                then(tt_(ss[:, 2, :], ss[:, 2, :], ss[:, 3, :], MUL))
                tt_(scaled[:, :, :], ident[:, :].unsqueeze(1).to_broadcast([P, TT, P]),
                    ss[:, 2, :].unsqueeze(2).to_broadcast([P, TT, P]), MUL).then_inc(diag_ready, 1)

            def take_rows(n):
                dve.wait_ge(row_ready, n)
                dve.tensor_copy(rstd_row[:, 0:SEQ], aux[:, :, :].rearrange("p b c -> p (b c)"))
                dve.tensor_copy(rstd_row[:, SEQ:T], bank_a[:, 2, 384:384 + DEC]).then_inc(row_used, 1)
                dve.wait_ge(row_used, n)

            dve.wait_ge(prm_in, 16 * PRM_LOADS)
            dve.tensor_copy(rows[0:16, 4, :].rearrange("q (g p) -> q g p", g=2),
                            log_dt[:, :].unsqueeze(2).to_broadcast([16, 2, NS])).then_inc(rows_ready, 1)
            dve.wait_ge(x_squared, TT)
            inverse_root(1, ss[:, 0, :], diag)
            dve.wait_ge(prm_turned, 2)
            dve.tensor_copy(prm[:, :, :], aux[:, 0, 0:80].rearrange("p (i q) -> p i q", i=5))
            dve.tensor_copy(state0[:, :, :], aux[:, 0, 32:64].rearrange("p (a q) -> p a q", a=2))
            dve.tensor_copy(pool_hist[:, :, :], aux[:, 0, 192:256].rearrange("p (g i) -> p g i", g=4)[:, :, 0:HIST])
            for comp, turned in enumerate((aux[:, 1], bank_b[:, 2])):
                by_group = turned.rearrange("p (q g h) -> p g q h", g=2, h=H)
                for g2 in range(2):
                    half = slice(64 * g2, 64 * g2 + 64)
                    ins = dve.tensor_copy(CT[half, comp], by_group[half, g2])
            ins.then_inc(prm_used, 1)
            dve.wait_ge(prm_used, 2)

            q = [pt[:, i, :] for i in range(30)]

            def exp_of(out, x, k, r, p):
                then(dve.tensor_scalar(x, x, -87.0, 88.0, ALU.max, ALU.min))
                then(dve.tensor_scalar(k, x, 1.4426950408889634, None, MUL))
                then(dve.tensor_scalar(k, k, MAGIC, None, ADD))
                then(dve.tensor_scalar(k, k, MAGIC, None, SUB))
                then(dve.scalar_tensor_tensor(r, k, -LN2[0], x, MUL, ADD))
                then(dve.scalar_tensor_tensor(r, k, -LN2[1], r, MUL, ADD))
                then(dve.tensor_scalar(p, r, EXP_POLY[0], None, MUL))
                for coef in EXP_POLY[1:]:
                    then(dve.scalar_tensor_tensor(p, p, coef, r, ADD, MUL))
                then(dve.tensor_scalar(r.bitcast(I32), k, 127.0, 8388608.0, ADD, MUL))
                then(dve.scalar_tensor_tensor(out, p, 1.0, r, ADD, MUL))

            def cmul(re, im, ar, ai, br, bi, t1, t2):
                tt_(t1, ar, br, MUL)
                then(tt_(t2, ai, bi, MUL))
                then(tt_(re, t1, t2, SUB))
                tt_(t1, ar, bi, MUL)
                then(tt_(t2, ai, br, MUL))
                then(tt_(im, t1, t2, ADD))

            def take_u(n):
                dve.wait_ge(tile_done, n + 1)
                banks = bank_b if n % 2 else bank_a
                for b0, nb, c0, nch, to in ((0, 2, 0, 44, 0), (2, 1, 88, 40, 88), (2, 1, 128, 4, NCP + 1)):
                    o = UT[:, n, :, to:to + nb * nch].rearrange("p j (b c) -> p b c j", b=nb)
                    off = 0 if c0 != 128 else 40 * L
                    i0 = banks[:, b0:b0 + nb, off:off + nch * L].rearrange("p b (c j) -> p b c j", j=L)
                    i1 = rstd_row[:, c0 * L:(c0 + nb * nch) * L].rearrange("p (b c j) -> p b c j", b=nb, j=L)
                    ins = tt_(o, i0, i1, MUL)
                ins.then_inc(evac_done, 1)

            lam, om, dt, e = q[0], prm[:, 1, :], q[1], q[2]
            then(dve.tensor_copy(q[3], prm[:, 4, :]))
            exp_of(dt, q[3], q[4], q[5], q[10])
            then(dve.tensor_scalar(lam, prm[:, 0, :], -1e-4, None, ALU.min))
            then(tt_(q[3], lam, dt, MUL))
            exp_of(e, q[3], q[4], q[5], q[10])
            then(tt_(q[3], om, dt, MUL))
            then(dve.tensor_scalar(q[4], q[3], 0.15915494309189535, None, MUL))
            then(dve.tensor_scalar(q[4], q[4], MAGIC, None, ADD))
            then(dve.tensor_scalar(q[4], q[4], MAGIC, None, SUB))
            for part in TWO_PI:
                then(dve.scalar_tensor_tensor(q[3], q[4], -part, q[3], MUL, ADD))
            then(dve.tensor_scalar(q[6], q[3], 3.1415925, -3.1415925, ALU.min, ALU.max))
            then(dve.tensor_scalar(q[7], q[6], -1.0, None, MUL))
            then(tt_(q[7], q[6], q[7], ALU.max))
            dve.tensor_scalar(q[7], q[7], -1.0, 1.5707963267948966, MUL, ADD).then_inc(angle_ready, 1)
            take_rows(1)
            take_u(0)
            dve.wait_ge(sine_ready, 1)
            dve.memset(BD[:, :, :, :], 0.0)
            tt_(eye2[:, :], ident[0:2 * H, 0:H], ident[0:2 * H, H:2 * H], ADD)
            then(dve.memset(PW[:, 1, 0, :], 0.0))
            then(dve.memset(PW[:, 0, 0, :], 1.0))
            ar, ai = PW[:, 0, 1, :], PW[:, 1, 1, :]
            then(tt_(ar, e, q[9], MUL))
            then(tt_(ai, e, q[8], MUL))
            then(tt_(q[10], lam, lam, MUL))
            then(tt_(q[11], om, om, MUL))
            then(tt_(q[10], q[10], q[11], ADD))
            then(dve.reciprocal(q[11], q[10]))
            then(dve.tensor_scalar(q[12], ar, -1.0, None, ADD))
            then(tt_(q[13], q[12], lam, MUL))
            then(tt_(q[14], ai, om, MUL))
            then(tt_(q[13], q[13], q[14], ADD))
            then(tt_(q[13], q[13], q[11], MUL))
            then(tt_(q[14], ai, lam, MUL))
            then(tt_(q[15], q[12], om, MUL))
            then(tt_(q[14], q[14], q[15], SUB))
            then(tt_(q[14], q[14], q[11], MUL))

            def bc_h(ap):
                return ap.unsqueeze(2).to_broadcast([P, PAIRS, H])
            for i, out in enumerate(xraw_out):
                dve.wait_ge(out, 16 * len(range(i, TT, XR_SLOTS)))
            t1, t2 = [t[:, 0:PAIRS * H].rearrange("p (q h) -> p q h", h=H) for t in (tmp_a, tmp_b)]
            cmul(BB[:, 0], BB[:, 1], bc_h(q[13]), bc_h(q[14]), b_raw[:, 0], b_raw[:, 1], t1, t2)
            for comp in range(2):
                for g2 in range(2):
                    half = slice(64 * g2, 64 * g2 + 64)
                    dve.tensor_copy(BD[half, comp, :, 16 * g2:16 * g2 + 16], BB[half, comp])

            def powers(tab, n, t1, t2):
                k = 1
                while k < n:
                    last = [tab[:, c, k - 1, :].unsqueeze(1).to_broadcast([P, k, PAIRS]) for c in range(2)]
                    cmul(tab[:, 0, k:2 * k, :], tab[:, 1, k:2 * k, :], tab[:, 0, 0:k, :], tab[:, 1, 0:k, :],
                         last[0], last[1], t1[:, 0:k, :], t2[:, 0:k, :])
                    k *= 2
            tp1, tp2 = pt[:, 14:22, :], pt[:, 22:30, :]
            powers(PW[:, :, 1:L + 1, :], L, tp1, tp2)

            take_u(1)
            big = [P, PAIRS, L + 1, H]

            def big_of(t):
                return t[:, 0:PAIRS * 9 * H].rearrange("p (q k h) -> p q k h", q=PAIRS, h=H)
            pw = [PW[:, c].rearrange("p k q -> p q k").unsqueeze(3).to_broadcast(big) for c in range(2)]
            ct = [CT[:, c].unsqueeze(2).to_broadcast(big) for c in range(2)]
            ca = [CA[:, c].rearrange("p q (k h) -> p q k h", h=H) for c in range(2)]
            tt_(big_of(tmp_a), ct[0], pw[0], MUL)
            then(tt_(big_of(tmp_b), ct[1], pw[1], MUL))
            then(tt_(ca[0], big_of(tmp_a), big_of(tmp_b), SUB))
            tt_(big_of(tmp_a), ct[0], pw[1], MUL)
            then(tt_(big_of(tmp_b), ct[1], pw[0], MUL))
            dve.scalar_tensor_tensor(CA[:, 1].rearrange("p q c -> p (q c)"), tmp_a[:, :], -1.0, tmp_b[:, :], MUL,
                                     SUB).then_inc(ca_ready, 1)
            mid = [P, PAIRS, L, H]

            def mid_of(t):
                return t[:, 0:PAIRS * L * H].rearrange("p (q k h) -> p q k h", q=PAIRS, h=H)
            pw = [PW[:, c, 0:L, :].rearrange("p k q -> p q k").unsqueeze(3).to_broadcast(mid) for c in range(2)]
            bb = [BB[:, c].unsqueeze(2).to_broadcast(mid) for c in range(2)]
            wt = [WT[:, c].rearrange("p q (k h) -> p q k h", h=H) for c in range(2)]
            take_u(2)
            dve.wait_ge(ca_ready, 1)
            tt_(mid_of(tmp_a), bb[0], pw[0], MUL)
            then(tt_(mid_of(tmp_b), bb[1], pw[1], MUL))
            then(tt_(wt[0], mid_of(tmp_a), mid_of(tmp_b), SUB))
            tt_(mid_of(tmp_a), bb[0], pw[1], MUL)
            then(tt_(mid_of(tmp_b), bb[1], pw[0], MUL))
            tt_(wt[1], mid_of(tmp_a), mid_of(tmp_b), ADD).then_inc(wt_ready, 1)
            then(dve.memset(UT[:, :, :, NCP:NCP + 1], 0.0))
            take_u(3)
            dve.wait_ge(k_evac, 4)
            lag0 = K_sb[:, :, 0:H]
            skip = skip_k[:, :].rearrange("h (q c) -> h q c", q=PAIRS)
            then(tt_(skip, eye2[:, :].unsqueeze(1).to_broadcast([2 * H, PAIRS, H]),
                     d_skip[:, :].unsqueeze(2).to_broadcast([2 * H, PAIRS, H]), MUL))
            tt_(lag0, lag0, skip, ADD).then_inc(k_ready, 1)

            then(dve.tensor_copy(a8pow[:, :, 0, :], PW[:, :, L, :]))
            powers(a8pow, STEPS, tp1, tp2)
            then(dve.tensor_scalar(neg_a[:, 0, :], a8pow[:, 1, 0, :], -1.0, None, MUL))
            then(dve.tensor_scalar(neg_a[:, 1, :], a8pow[:, 1, STEPS - 1, :], -1.0, None, MUL))

            def mark(ins):
                steps[0] += 1
                ins.then_inc(dve_step, 1)
                return steps[0]

            def advance(cur, prev, k, scratch=(sc_a, sc_b)):
                shape = list(prev.shape)
                n = int(np.prod(shape[1:]))

                def f(ap):
                    return ap.rearrange("p (c q s) -> p c q s", c=2, q=PAIRS) if len(shape) == 4 else \
                        ap.rearrange("p (c q) -> p c q", c=2)

                def bc(ap, like):
                    return ap.unsqueeze(2).to_broadcast(like) if len(shape) == 4 else ap
                a_re = a8pow[:, 0, k, :].unsqueeze(1)
                a_re = a_re.unsqueeze(3).to_broadcast(shape) if len(shape) == 4 else a_re.to_broadcast(shape)
                one = [P] + shape[2:]
                u1, u2 = [f(t[:, 0:n]) for t in scratch]
                first = mark(tt_(u1, prev, a_re, MUL))
                tt_(u2[:, 0], prev[:, 1], bc(neg_a[:, 1 if k else 0, :], one), MUL)
                mark(tt_(u2[:, 1], prev[:, 0], bc(a8pow[:, 1, k, :], one), MUL))
                dve.wait_ge(dve_step, first)
                then(tt_(cur, cur, u1, ADD))
                then(tt_(cur, cur, u2, ADD))

            both = S[:, :, :, 1:NCP + 1].rearrange("p c q (s i) -> p c q s i", i=STEPS)
            seg = [both[:, 0], both[:, 1]]

            def scan_steps(i0, i1, scratch=(sc_a, sc_b)):
                for i in range(i0, i1):
                    advance(both[:, :, :, :, i], both[:, :, :, :, i - 1], 0, scratch)

            def scan_ends(s0, s1):
                for s in range(s0, s1):
                    advance(both[:, :, :, s, STEPS - 1], both[:, :, :, s - 1, STEPS - 1], STEPS - 1)

            def scan_sample():
                for k in range(NCP + 2, SLOTS):
                    advance(S[:, :, :, k], S[:, :, :, k - 1], 0)

            def scan_fill(c, pairs, scratch):
                for q0 in pairs:
                    shape = [P, 8, SEG - 1, STEPS - 1]
                    n = 8 * (SEG - 1) * (STEPS - 1)
                    end = [x[:, q0:q0 + 8, 0:SEG - 1, STEPS - 1].unsqueeze(3).to_broadcast(shape) for x in seg]
                    apw = [a8pow[:, k, 0:STEPS - 1, q0:q0 + 8].rearrange("p i q -> p q i").unsqueeze(2).to_broadcast(shape)
                           for k in range(2)]
                    u1 = scratch[0][:, 0:n].rearrange("p (q s i) -> p q s i", q=8, s=SEG - 1)
                    u2 = scratch[1][:, 0:n].rearrange("p (q s i) -> p q s i", q=8, s=SEG - 1)
                    dst = seg[c][:, q0:q0 + 8, 1:SEG, 0:STEPS - 1]
                    tt_(u1, end[0], apw[c], MUL)
                    then(tt_(u2, end[1], apw[1 - c], MUL))
                    then(tt_(scratch[0][:, 0:n], scratch[0][:, 0:n], scratch[1][:, 0:n], SUB if c == 0 else ADD))
                    if q0:
                        tt_(dst, dst, u1, ADD).then_inc(s_ready, 1)
                        dve.wait_ge(s_ready, c + 1)
                    else:
                        then(tt_(dst, dst, u1, ADD))

            def scan_start():
                dve.wait_ge(v_evac, PAIRS)
                then(dve.memset(S[:, :, :, 0:1], 0.0))
                then(dve.tensor_copy(S[:, :, :, NCP + 1], state0[:, :, :]))

            dve.wait_ge(ut_out, 16)
            then(dve.memset(UP[:, 0:HIST], 0.0))
            for g in range(4):
                t0 = 5 * g + T_POOL
                if g == 1:
                    scan_start()
                    scan_steps(1, 5, (end_a, end_b))
                if g:
                    dve.wait_ge(np_turned, g)
                then(dve.tensor_copy(UP[:, HIST + SEQ:2 * HIST + SEQ], pool_hist[:, g, :]))
                dve.wait_ge(tile_done, t0 + 1)
                tt_(UP[:, HIST:HIST + 2 * BLK].rearrange("p (b t) -> p b t", b=2), A3[:, 0:2],
                    rstd_row[:, 0:2 * BLK].rearrange("p (b t) -> p b t", b=2), MUL)
                tt_(UP[:, HIST + 2 * BLK:HIST + SEQ], bank_a[:, 2, 0:BLK - DEC], rstd_row[:, 2 * BLK:SEQ], MUL)
                tt_(UP[:, 2 * HIST + SEQ:], bank_a[:, 2, BLK - DEC:BLK], rstd_row[:, SEQ:], MUL).then_inc(evac_done, 1)
                dve.wait_ge(evac_done, t0 + 1)
                src, dst = UP, sum_a
                for k in range(g + 1):
                    sh = 1 << k
                    lo_i = 2 * sh - 1
                    then(tt_(dst[:, lo_i:], src[:, lo_i:], src[:, lo_i - sh:T + 2 * HIST - sh], ADD))
                    src, dst = dst, (sum_b if dst is sum_a else sum_a)
                w = WINDOWS[g]
                dve.scalar_tensor_tensor(dst[:, 0:SEQ], src[:, HIST:HIST + SEQ], 1.0 / w, UP[:, HIST:HIST + SEQ], MUL, SUB)
                dve.scalar_tensor_tensor(dst[:, SEQ:T], src[:, 2 * HIST + SEQ:], 1.0 / w, UP[:, 2 * HIST + SEQ:], MUL, SUB)
                if g == 0:
                    dve.wait_ge(inv_in, 16)
                then(tt_(head[:, :], src[:, HIST:HIST + 16], inv_count[:, g, :], MUL))
                tt_(dst[:, 0:16], head[:, :], UP[:, HIST:HIST + 16], SUB).then_inc(pooled_ready, 1)
                dve.wait_ge(pooled_hi, g + 1)
                tt_(pl_lo[:, :], dst[:, 0:T], pl_hi[:, :], SUB).then_inc(pooled_lo, 1)
                if g == 3:
                    scan_fill(0, (0,), (sc_a, sc_b))
                for r, banks in enumerate((B3, A3)):
                    dve.wait_ge(tile_done, t0 + 2 + r)
                    if g:
                        dve.wait_ge(mp_out[r], 16 * g)
                    tt_(b3(gate_t[:, r, :]), banks, b3(rstd_row[:, :]), MUL).then_inc(evac_done, 1)
                    if r == 0 and g == 1:
                        dve.wait_ge(ca_stacked, 64)
                        scan_steps(5, 10)
                    if r == 0 and g == 2:
                        scan_steps(15, STEPS)
                        scan_ends(1, 5)
                    if r == 0 and g == 3:
                        scan_fill(0, (8,), (sc_a, sc_b))
                for r in range(2):
                    dve.wait_ge(gp_sig, 2 * g + r + 1)
                    dve.wait_ge(tile_done, t0 + 4 + r)
                    dve.scalar_tensor_tensor(b3(gate_t[:, r, :]), B3, gains[:, 3, 2 * g + r:2 * g + r + 1],
                                             b3(gate_t[:, r, :]), MUL, MUL).then_inc(evac_done, 1)
                if g == 1:
                    scan_steps(10, 15)
                if g == 2:
                    scan_ends(5, SEG)
                    scan_sample()
            scan_fill(1, (0, 8), (end_a, end_b))

            def gelu(n):
                y = YT[:, n].rearrange("p j c -> p (j c)")
                dve.wait_ge(y_sq, n + 1)
                then(dve.tensor_scalar(ge_a[:, :], ge_a[:, :], 0.044715, 1.0, MUL, ADD))
                tt_(ge_a[:, :], ge_a[:, :], y, MUL).then_inc(y_arg, 1)
                dve.wait_ge(y_sig, n + 1)
                if n:
                    dve.wait_ge(y_hi_ready, n)
                s = ge_b[:, :].rearrange("p (j c) -> p j c", c=NCG)
                tt_(ge_c[:, 0:SEQ].rearrange("p (c j) -> p j c", j=L), YT[:, n, :, 0:NCP], s[:, :, 0:NCP], MUL)
                tt_(ge_c[:, SEQ:T].rearrange("p (c j) -> p j c", j=L), YT[:, n, :, NCP + 1:], s[:, :, NCP + 1:],
                    MUL).then_inc(y_val, 1)
                dve.wait_ge(y_hi_ready, n + 1)
                tt_(y_lo[:, n, :], ge_c[:, :], y_hi[:, n, :], SUB).then_inc(y_lo_ready, 1)

            def gate(n):
                dve.wait_ge(tile_done, T_GATE + n + 1)
                tt_(b3(gate_at(n)), B3 if n % 2 else A3, b3(rstd_row[:, :]), MUL).then_inc(evac_done, 1)

            def merge(n, m, r):
                dve.wait_ge(tile_done, n * 2 + (T_GLU + 1))
                if not (isinstance(n, int) and n == 0):
                    dve.wait_ge(merged_ready, n)
                tt_(b3(glu_a[:, :]), A3, b3(gate_at(n) if isinstance(n, int) else at_tile(merged, n)),
                    MUL).then_inc(evac_done, 1)
                dve.wait_ge(evac_done, n * 2 + (T_GLU + 1))
                dve.wait_ge(b_sig, n + 1)
                tt_(glu_a[:, :], glu_a[:, :], glu_b[:, :], MUL).then_inc(evac_done, 1)
                dve.wait_ge(evac_done, n * 2 + (T_GLU + 2))
                dve.wait_ge(mp_in[r], m * 16 + 16)
                tt_(at_tile(merged, n), glu_a[:, :], pool_t[:, r, :], ADD).then_inc(merged_ready, 1)
                dve.wait_ge(m_hi_ready, n + 1)
                tt_(at_tile(x_lo, n), at_tile(merged, n), at_tile(x_hi, n), SUB).then_inc(m_lo_ready, 1)

            for n in range(4):
                gate(n)
            for n in range(KS):
                gelu(n)
                gate(n + 4)
            dve.wait_ge(gs_sig, KD)
            for r in range(2):
                merge(r, 0, r)
            with dve.Fori(1, 4) as m:
                for r in range(2):
                    merge(2 * m + r, m, r)

            for n in range(KD):
                dve.wait_ge(tile_done, T_OUT + n + 1)
                dve.wait_ge(xt_in[n], 16)
                tt_(b3(hT[:, n, :]), B3 if n % 2 else A3, b3(hT[:, n, :]), ADD).then_inc(evac_done, 1)
                dve.wait_ge(hg_hi_ready, n + 1)
                dve.scalar_tensor_tensor(hg_lo[:, n, :], hT[:, n, :], gains[:, 1, n:n + 1], hg_hi[:, n, :], MUL,
                                         SUB).then_inc(hg_lo_ready, 1)
            dve.wait_ge(ss_turned, 1)
            inverse_root(2, aux[:, 0, 0:TT], diag2)
            take_rows(2)

            def hidden(r, t_gate, t_up, n, step):
                dve.wait_ge(tile_done, t_gate + 1)
                tt_(b3(f_g[:, :]), A3, b3(rstd_row[:, :]), MUL).then_inc(evac_done, 1)
                dve.wait_ge(evac_done, t_gate + 1)
                dve.wait_ge(fs_ready, n + 1)
                tt_(f_g[:, :], f_g[:, :], f_s[:, :], MUL).then_inc(dve_step, 1)
                dve.wait_ge(tile_done, t_up + 1)
                tt_(b3(f_u[:, :]), B3, b3(rstd_row[:, :]), MUL).then_inc(evac_done, 1)
                dve.wait_ge(dve_step, step)
                dve.wait_ge(evac_done, t_up + 1)
                tt_(f_h[:, :], f_g[:, :], f_u[:, :], MUL).then_inc(fh_ready, 1)

            def hidden_lo(r, n, hi=f_hi, lo=f_lo):
                dve.wait_ge(f_hi_ready, n + 1)
                tt_(lo[:, r, :], f_h[:, :], hi[:, r, :], SUB).then_inc(f_lo_ready, 1)

            def add_down(t0, n):
                dve.wait_ge(tile_done, t0 + n + 1)
                tt_(b3(hT[:, n, :]), B3 if n % 2 else A3, b3(hT[:, n, :]), ADD).then_inc(evac_done, 1)

            def add_square(n):
                dve.wait_ge(sq_ready, KD + n + 1)
                if n >= 2:
                    dve.wait_ge(sq_used, KD - 1 + n - 1)
                tt_(sq_sum[:, :], sq_sum[:, :], sq[:, n % 2, :], ADD).then_inc(sq_used, 1)

            base_step = steps[0]
            for r in range(2):
                hidden(r, T_FFN + 2 * r, T_FFN + 2 * r + 1, r, base_step + r + 1)
                hidden_lo(r, r)
            with dve.Fori(1, FCH - 1) as c:
                t0 = 12 * c + (T_LOOP - 12)
                hidden(0, t0, t0 + 1, 2 * c, 2 * c + (base_step + 1))
                for n in range(KD):
                    add_down(t0 + 2, n)
                hidden_lo(0, 2 * c)
                hidden(1, t0 + 10, t0 + 11, 2 * c + 1, 2 * c + (base_step + 2))
                hidden_lo(1, 2 * c + 1)
            last = 2 * FCH - 2
            hidden(0, T_TAIL, T_TAIL + 1, last, base_step + last + 1)
            hidden_lo(0, last, f2_hi, f2_lo)
            hidden(1, T_TAIL + 2, T_TAIL + 3, last + 1, base_step + last + 2)
            steps[0] = base_step + 2 * FCH
            for n in range(KD):
                add_down(T_TAIL + 4, n)
                if n == 0:
                    hidden_lo(1, last + 1, f2_hi, f2_lo)
            for n in range(KD):
                add_down(T_TAIL + 12, n)
                if n >= 2:
                    add_square(n - 1)
            add_square(KD - 1)
            dve.wait_ge(ss_turned, 2)
            inverse_root(3, aux[:, 0, 0:TT], None)
            dve.wait_ge(diag_ready, 3)
            for tt in range(0, TT, 2):
                dve.wait_ge(tok_turned, tt + 1)
                dve.tensor_scalar(y_out[0:tok(tt), tt, :], out_banks[tt % 3][0:tok(tt), 0:2, :].rearrange("p b c -> p (b c)"),
                                  ss[0:tok(tt), 2, tt:tt + 1], None, MUL).then_inc(tok_used[0], 1)


INPUTS = ["x_prompt", "x_sample", "state_ssm_re", "state_ssm_im", "state_pool", "g_mix", "w_in", "ssm_a_re", "ssm_a_im",
          "ssm_log_dt", "ssm_b_re", "ssm_b_im", "ssm_c_re", "ssm_c_im", "ssm_d", "w_glu_a", "w_glu_b", "pool_w",
          "pool_scale", "w_out", "g_ffn", "w_ffn_gate", "w_ffn_up", "w_ffn_down", "g_final"]
OUTPUTS = {"y_p": (1, SEQ, D), "y_s": (1, DEC, D), "re_p": (1, 1, G, NS), "im_p": (1, 1, G, NS),
           "pool_p": (1, 1, HIST, W_POOL), "re_s": (1, 1, G, NS), "im_s": (1, 1, G, NS), "pool_s": (1, 1, HIST, W_POOL)}


def kernel(**inputs):
    import concourse.bacc as bacc
    from concourse.bass_utils import run_bass_kernel_spmd

    arrays = {name: np.ascontiguousarray(inputs[name]) for name in INPUTS}
    arrays["c_ident"] = np.eye(P, dtype=np.float32)
    counts = [[1.0 / min(t + 1, w) for t in range(16)] for w in WINDOWS]
    arrays["c_inv_count"] = np.broadcast_to(np.array(counts, np.float32), (P, 4, 16)).copy()
    nc = bacc.Bacc("TRN2", target_bir_lowering=False, num_devices=1, dynamic_dma_scratch_size=1024)
    t_in = {n: nc.dram_tensor(f"in_{n}", a.shape, F32, kind="ExternalInput").ap() for n, a in arrays.items()}
    t_out = {n: nc.dram_tensor(f"out_{n}", s, F32, kind="ExternalOutput").ap() for n, s in OUTPUTS.items()}
    hybrid_layer(nc, t_in, t_out)
    r = run_bass_kernel_spmd(nc, [{f"in_{n}": a for n, a in arrays.items()}], core_ids=[0])
    return tuple(r.results[0][f"out_{n}"] for n in OUTPUTS)
```
